# Optimizing a Trainium2 kernel written in Bass

```python
import jax, jax.numpy as jnp
from jax import lax
import numpy as np

D_MODEL = 1024
BATCH = 1
SEQ = 512
DEPTH = 2

CHUNK = 64
HEAD_DIM = 64
ATT_HEADS = 6
ATT_WIDTH = ATT_HEADS * HEAD_DIM
ATT_LEFT_CHUNKS = 8
ATT_BAND = (ATT_LEFT_CHUNKS + 1) * CHUNK
REL_CLIP = 128
CONV_WIDTH = D_MODEL // 4
CONV_KERNEL = 31
RET_HEADS = 6
RET_WIDTH = RET_HEADS * HEAD_DIM
D_MIX = ATT_WIDTH + CONV_WIDTH + RET_WIDTH
D_IN = 3 * ATT_WIDTH + 2 * CONV_WIDTH + 4 * RET_WIDTH
SPLITS = (ATT_WIDTH, 2 * ATT_WIDTH, 3 * ATT_WIDTH,
          3 * ATT_WIDTH + 2 * CONV_WIDTH,
          3 * ATT_WIDTH + 2 * CONV_WIDTH + RET_WIDTH,
          3 * ATT_WIDTH + 2 * CONV_WIDTH + 2 * RET_WIDTH,
          3 * ATT_WIDTH + 2 * CONV_WIDTH + 3 * RET_WIDTH)
D_FF = 4 * D_MODEL
ROPE_BASE = 10000.0
EPS = 1e-6
NEG_INF = -1e30


def rms_norm(x, g):
    xf = x.astype(jnp.float32)
    y = xf * lax.rsqrt(jnp.mean(xf * xf, axis=-1, keepdims=True) + EPS)
    return (y * g.astype(jnp.float32)).astype(x.dtype)

def layer_norm(x):
    xf = x.astype(jnp.float32)
    mu = jnp.mean(xf, axis=-1, keepdims=True)
    var = jnp.mean(jnp.square(xf - mu), axis=-1, keepdims=True)
    return (xf - mu) * lax.rsqrt(var + EPS)

def chunk_attention(q, k, v, rel_bias):
    b, s, _ = q.shape
    nc = s // CHUNK
    shp = (b, nc, CHUNK, ATT_HEADS, HEAD_DIM)
    q = q.reshape(shp) * (HEAD_DIM ** -0.5)
    k = k.reshape(shp)
    v = v.reshape(shp)
    pad = ((0, 0), (ATT_LEFT_CHUNKS, 0), (0, 0), (0, 0), (0, 0))
    kp, vp = jnp.pad(k, pad), jnp.pad(v, pad)
    band_idx = jnp.arange(nc)[:, None] + jnp.arange(ATT_LEFT_CHUNKS + 1)[None, :]
    kb = kp[:, band_idx].reshape(b, nc, ATT_BAND, ATT_HEADS, HEAD_DIM)
    vb = vp[:, band_idx].reshape(b, nc, ATT_BAND, ATT_HEADS, HEAD_DIM)
    scores = jnp.einsum('bnqhd,bnkhd->bnhqk', q, kb).astype(jnp.float32)
    qpos = jnp.arange(CHUNK)
    kpos = jnp.arange(ATT_BAND)
    rel = qpos[:, None] + ATT_LEFT_CHUNKS * CHUNK - kpos[None, :]
    rel_idx = jnp.clip(rel, -REL_CLIP, REL_CLIP) + REL_CLIP
    bias = rel_bias[:, rel_idx].astype(jnp.float32)
    key_chunk = jnp.arange(nc)[:, None] + (kpos // CHUNK)[None, :] - ATT_LEFT_CHUNKS
    valid = key_chunk >= 0
    scores = jnp.where(valid[None, :, None, None, :], scores + bias[None, None], NEG_INF)
    p = jax.nn.softmax(scores, axis=-1).astype(v.dtype)
    o = jnp.einsum('bnhqk,bnkhd->bnqhd', p, vb)
    return o.reshape(b, s, ATT_WIDTH)

def conv_module(u, conv_w, conv_b, ln_g, ln_b):
    a, gate = jnp.split(u, 2, axis=-1)
    y = a * jax.nn.sigmoid(gate)
    y = jnp.pad(y, ((0, 0), (CONV_KERNEL - 1, 0), (0, 0)))
    y = lax.conv_general_dilated(y, conv_w[:, None, :], (1,), 'VALID',
                                 dimension_numbers=('NWC', 'WIO', 'NWC'),
                                 feature_group_count=CONV_WIDTH) + conv_b
    y = layer_norm(y) * ln_g.astype(jnp.float32) + ln_b.astype(jnp.float32)
    return jax.nn.silu(y).astype(u.dtype)

def rotary(x, pos):
    half = HEAD_DIM // 2
    inv = 1.0 / (ROPE_BASE ** jnp.linspace(0.0, 1.0, half, dtype=jnp.float32))
    ang = pos[:, None] * inv[None, :]
    cos = jnp.cos(ang)[None, :, None, :]
    sin = jnp.sin(ang)[None, :, None, :]
    x1 = x[..., :half].astype(jnp.float32)
    x2 = x[..., half:].astype(jnp.float32)
    out = jnp.concatenate([x1 * cos - x2 * sin, x2 * cos + x1 * sin], axis=-1)
    return out.astype(x.dtype)

def retention(q, k, v, g):
    b, s, _ = q.shape
    nc = s // CHUNK
    dt = q.dtype
    pos = jnp.arange(s, dtype=jnp.float32)
    q = rotary(q.reshape(b, s, RET_HEADS, HEAD_DIM), pos)
    k = rotary(k.reshape(b, s, RET_HEADS, HEAD_DIM), pos) * (HEAD_DIM ** -0.5)
    shp = (b, nc, CHUNK, RET_HEADS, HEAD_DIM)
    qc, kc, vc = q.reshape(shp), k.reshape(shp), v.reshape(shp)
    log_g = jnp.log1p(-(2.0 ** (-5.0 - jnp.arange(RET_HEADS, dtype=jnp.float32))))
    idx = jnp.arange(CHUNK, dtype=jnp.float32)
    diff = idx[:, None] - idx[None, :]
    intra = jnp.where(diff >= 0, jnp.exp(jnp.maximum(diff, 0.0) * log_g[:, None, None]), 0.0)
    xi = jnp.exp((idx + 1.0)[None, :] * log_g[:, None]).astype(dt)
    zeta = jnp.exp((CHUNK - 1.0 - idx)[None, :] * log_g[:, None]).astype(dt)
    gamma_c = jnp.exp(CHUNK * log_g).astype(dt)
    sc = jnp.einsum('bnihd,bnjhd->bnhij', qc, kc) * intra.astype(dt)
    y_intra = jnp.einsum('bnhij,bnjhe->bnihe', sc, vc)
    kv = jnp.einsum('bnjhd,hj,bnjhe->nbhde', kc, zeta, vc)

    def step(state, kv_n):
        return state * gamma_c[None, :, None, None] + kv_n, state

    _, state_prev = lax.scan(step, jnp.zeros_like(kv[0]), kv)
    y_cross = jnp.einsum('bnihd,hi,nbhde->bnihe', qc, xi, state_prev)
    y = (y_intra + y_cross).reshape(b, s, RET_HEADS, HEAD_DIM)
    y = layer_norm(y).reshape(b, s, RET_WIDTH)
    return (jax.nn.silu(g.astype(jnp.float32)) * y).astype(dt)

def hybrid_layer(x, g_mix_pre, g_mix_post, g_mlp_pre, g_mlp_post, w_in, rel_bias,
                 conv_w, conv_b, conv_ln_g, conv_ln_b, w_out, w_up, w_down):
    h = rms_norm(x, g_mix_pre)
    u = h @ w_in
    aq, ak, av, cu, rq, rk, rv, rg = jnp.split(u, SPLITS, axis=-1)
    y_att = chunk_attention(aq, ak, av, rel_bias)
    y_conv = conv_module(cu, conv_w, conv_b, conv_ln_g, conv_ln_b)
    y_ret = retention(rq, rk, rv, rg)
    mix = jnp.concatenate([y_att, y_conv, y_ret], axis=-1) @ w_out
    x = x + rms_norm(mix, g_mix_post)
    h = rms_norm(x, g_mlp_pre)
    f = jnp.square(jax.nn.relu(h @ w_up)) @ w_down
    return x + rms_norm(f, g_mlp_post)

def first_inputs(seed: int = 0) -> dict:
    key = jax.random.key(seed)
    ks = jax.random.split(key, 16)
    f32 = jnp.float32

    def nrm(k, shape, scale):
        return jax.random.normal(k, shape, f32) * scale

    def gain(k, shape):
        return 1.0 + nrm(k, shape, 0.02)

    return {
        "x": nrm(ks[0], (BATCH, SEQ, D_MODEL), 1.0),
        "norm_mix_pre": gain(ks[1], (DEPTH, D_MODEL)),
        "norm_mix_post": gain(ks[2], (DEPTH, D_MODEL)),
        "norm_mlp_pre": gain(ks[3], (DEPTH, D_MODEL)),
        "norm_mlp_post": gain(ks[4], (DEPTH, D_MODEL)),
        "w_in": nrm(ks[5], (DEPTH, D_MODEL, D_IN), D_MODEL ** -0.5),
        "attn_rel_bias": nrm(ks[6], (DEPTH, ATT_HEADS, 2 * REL_CLIP + 1), 0.5),
        "conv_w": nrm(ks[7], (DEPTH, CONV_KERNEL, CONV_WIDTH), CONV_KERNEL ** -0.5),
        "conv_b": nrm(ks[8], (DEPTH, CONV_WIDTH), 0.02),
        "conv_ln_g": gain(ks[9], (DEPTH, CONV_WIDTH)),
        "conv_ln_b": nrm(ks[10], (DEPTH, CONV_WIDTH), 0.02),
        "w_out": nrm(ks[11], (DEPTH, D_MIX, D_MODEL), D_MIX ** -0.5),
        "w_up": nrm(ks[12], (DEPTH, D_MODEL, D_FF), D_MODEL ** -0.5),
        "w_down": nrm(ks[13], (DEPTH, D_FF, D_MODEL), D_FF ** -0.5),
    }

def first_block(x, norm_mix_pre, norm_mix_post, norm_mlp_pre, norm_mlp_post, w_in,
              attn_rel_bias, conv_w, conv_b, conv_ln_g, conv_ln_b, w_out, w_up, w_down):
    for l in range(DEPTH):
        x = hybrid_layer(x, norm_mix_pre[l], norm_mix_post[l], norm_mlp_pre[l], norm_mlp_post[l],
                         w_in[l], attn_rel_bias[l], conv_w[l], conv_b[l], conv_ln_g[l],
                         conv_ln_b[l], w_out[l], w_up[l], w_down[l])
    return x


MLA_HEADS = 6
MLA_NOPE = 64
MLA_ROPE = 32
MLA_V = 64
MLA_Q_LORA = 256
MLA_KV_LORA = 128
NSA_HEADS = 6
NSA_KV_HEADS = 2
NSA_GROUP = NSA_HEADS // NSA_KV_HEADS
NSA_BRANCHES = 3
CMP_LEN = 32
CMP_STRIDE = 16
CMP_HIDDEN = 128
SEL_LEN = 64
SEL_TOPK = 16
WINDOW = 512
SB_HEADS = 4
D_MIX_2 = MLA_HEADS * MLA_V + NSA_HEADS * HEAD_DIM + SB_HEADS * HEAD_DIM
D_FF_2 = 2816
ROPE_THETA = 500000.0
PARTIAL_ROT = HEAD_DIM // 4
Q_BLOCK = 128
NEG_INF_2 = -1e30
FORCE_SCORE = 1e4
NSA_KV_W = NSA_KV_HEADS * HEAD_DIM
IN_WIDTHS = (MLA_Q_LORA, MLA_KV_LORA, MLA_ROPE,
             NSA_HEADS * HEAD_DIM,
             NSA_KV_W, NSA_KV_W, NSA_KV_W, NSA_KV_W, NSA_KV_W, NSA_KV_W,
             NSA_HEADS * NSA_BRANCHES,
             SB_HEADS * HEAD_DIM, SB_HEADS * HEAD_DIM, SB_HEADS * HEAD_DIM)
D_IN_2 = sum(IN_WIDTHS)


def rmsnorm(x, g):
    xf = x.astype(jnp.float32)
    y = xf * lax.rsqrt(jnp.mean(xf * xf, axis=-1, keepdims=True) + EPS)
    return (y * g.astype(jnp.float32)).astype(x.dtype)

def rope(x, pos, rot_dim):
    half = rot_dim // 2
    inv_freq = ROPE_THETA ** (-jnp.arange(half, dtype=jnp.float32) / half)
    ang = pos.astype(jnp.float32)[:, None] * inv_freq[None, :]
    cos = jnp.cos(ang)[:, None, :]
    sin = jnp.sin(ang)[:, None, :]
    xr = x[..., :rot_dim].astype(jnp.float32)
    x1, x2 = xr[..., :half], xr[..., half:]
    rot = jnp.concatenate([x1 * cos - x2 * sin, x2 * cos + x1 * sin], axis=-1)
    return jnp.concatenate([rot.astype(x.dtype), x[..., rot_dim:]], axis=-1)

def masked_softmax(s, mask):
    return jax.nn.softmax(jnp.where(mask, s.astype(jnp.float32), NEG_INF_2), axis=-1)

def swiglu(h, w_gate, w_up, w_down):
    return (jax.nn.silu(h @ w_gate) * (h @ w_up)) @ w_down

def split_heads(t, n_heads):
    b, s, _ = t.shape
    return t.reshape(b, s, n_heads, -1)

def sweep_query_blocks(block_fn, n_blocks):
    out = lax.map(block_fn, jnp.arange(n_blocks, dtype=jnp.int32))
    nb, b, q, h, d = out.shape
    return out.transpose(1, 0, 2, 3, 4).reshape(b, nb * q, h, d)

def mla_attention(c_q, c_kv, k_rope, q_norm, w_uq, kv_norm, w_ukv, pos):
    b, s, _ = c_q.shape
    q = (rmsnorm(c_q, q_norm) @ w_uq).reshape(b, s, MLA_HEADS, MLA_NOPE + MLA_ROPE)
    q_nope = q[..., :MLA_NOPE]
    q_pe = rope(q[..., MLA_NOPE:], pos, MLA_ROPE)
    kv = (rmsnorm(c_kv, kv_norm) @ w_ukv).reshape(b, s, MLA_HEADS, MLA_NOPE + MLA_V)
    k_nope, v = kv[..., :MLA_NOPE], kv[..., MLA_NOPE:]
    k_pe = rope(k_rope[:, :, None, :], pos, MLA_ROPE)[:, :, 0]
    scale = (MLA_NOPE + MLA_ROPE) ** -0.5

    def block(i):
        q0 = i * Q_BLOCK
        qn = lax.dynamic_slice_in_dim(q_nope, q0, Q_BLOCK, axis=1)
        qp = lax.dynamic_slice_in_dim(q_pe, q0, Q_BLOCK, axis=1)
        sc = (jnp.einsum('bqhd,bkhd->bhqk', qn, k_nope)
              + jnp.einsum('bqhr,bkr->bhqk', qp, k_pe)).astype(jnp.float32) * scale
        qpos = q0 + jnp.arange(Q_BLOCK)
        p = masked_softmax(sc, pos[None, :] <= qpos[:, None]).astype(v.dtype)
        return jnp.einsum('bhqk,bkhd->bqhd', p, v)

    return sweep_query_blocks(block, s // Q_BLOCK)

def compress_blocks(x, pos_emb, w1, w2):
    b, s, g, d = x.shape
    chunks = x.reshape(b, s // CMP_STRIDE, CMP_STRIDE, g, d)
    blocks = jnp.concatenate([chunks[:, :-1], chunks[:, 1:]], axis=2)
    blocks = blocks + pos_emb[None, None, :, None, :]
    flat = blocks.transpose(0, 1, 3, 2, 4).reshape(b, s // CMP_STRIDE - 1, g, CMP_LEN * d)
    return jax.nn.gelu(flat @ w1) @ w2

def nsa_attention(q, k_cmp, v_cmp, k_sel, v_sel, k_win, v_win, gates,
                  cmp_pos_k, cmp_w1_k, cmp_w2_k, cmp_pos_v, cmp_w1_v, cmp_w2_v, pos):
    b, s, h, d = q.shape
    q = rope(q, pos, PARTIAL_ROT)
    k_cmp = rope(k_cmp, pos, PARTIAL_ROT)
    k_sel = rope(k_sel, pos, PARTIAL_ROT)
    k_win = rope(k_win, pos, PARTIAL_ROT)
    scale = d ** -0.5
    kc = compress_blocks(k_cmp, cmp_pos_k, cmp_w1_k, cmp_w2_k)
    vc = compress_blocks(v_cmp, cmp_pos_v, cmp_w1_v, cmp_w2_v)
    n_cmp = s // CMP_STRIDE - 1
    cmp_start = jnp.arange(n_cmp) * CMP_STRIDE
    cmp_end = cmp_start + CMP_LEN - 1
    n_slc = s // SEL_LEN
    n_top = min(SEL_TOPK, n_slc)
    slc_start = jnp.arange(n_slc) * SEL_LEN
    overlap = ((cmp_start[:, None] < slc_start[None, :] + SEL_LEN)
               & (cmp_start[:, None] + CMP_LEN > slc_start[None, :])).astype(jnp.float32)
    ksb = k_sel.reshape(b, n_slc, SEL_LEN, NSA_KV_HEADS, d).transpose(0, 3, 1, 2, 4)
    vsb = v_sel.reshape(b, n_slc, SEL_LEN, NSA_KV_HEADS, d).transpose(0, 3, 1, 2, 4)
    b_ix = jnp.arange(b)[:, None, None, None]
    g_ix = jnp.arange(NSA_KV_HEADS)[None, :, None, None]
    blk = jnp.arange(n_slc)
    kw = jnp.pad(k_win, ((0, 0), (WINDOW, 0), (0, 0), (0, 0)))
    vw = jnp.pad(v_win, ((0, 0), (WINDOW, 0), (0, 0), (0, 0)))

    def block(i):
        q0 = i * Q_BLOCK
        qpos = q0 + jnp.arange(Q_BLOCK)
        qb = lax.dynamic_slice_in_dim(q, q0, Q_BLOCK, axis=1).reshape(b, Q_BLOCK, NSA_KV_HEADS, NSA_GROUP, d)
        sc = jnp.einsum('bqgrd,bcgd->bgrqc', qb, kc).astype(jnp.float32) * scale
        cmask = cmp_end[None, :] <= qpos[:, None]
        p_cmp = masked_softmax(sc, cmask)
        p_cmp = jnp.where(cmask.any(axis=-1)[:, None], p_cmp, 0.0)
        o_cmp = jnp.einsum('bgrqc,bcgd->bqgrd', p_cmp.astype(vc.dtype), vc)
        score = jnp.einsum('bgrqc,cn->bgqn', p_cmp, overlap)
        cur = qpos // SEL_LEN
        forced = (blk[None, :] == 0) | (blk[None, :] == cur[:, None]) | (blk[None, :] == cur[:, None] - 1)
        future = blk[None, :] > cur[:, None]
        score = jnp.where(forced, FORCE_SCORE, jnp.where(future, -1.0, score))
        _, idx = lax.top_k(score, n_top)
        kg = ksb[b_ix, g_ix, idx]
        vg = vsb[b_ix, g_ix, idx]
        tok = idx[..., None] * SEL_LEN + jnp.arange(SEL_LEN)
        smask = (tok <= qpos[None, None, :, None, None])[:, :, None]
        ss = jnp.einsum('bqgrd,bgqnld->bgrqnl', qb, kg).astype(jnp.float32) * scale
        ss = jnp.where(smask, ss, NEG_INF_2).reshape(b, NSA_KV_HEADS, NSA_GROUP, Q_BLOCK, n_top * SEL_LEN)
        p_sel = jax.nn.softmax(ss, axis=-1).astype(vg.dtype).reshape(b, NSA_KV_HEADS, NSA_GROUP, Q_BLOCK, n_top, SEL_LEN)
        o_sel = jnp.einsum('bgrqnl,bgqnld->bqgrd', p_sel, vg)
        kwb = lax.dynamic_slice_in_dim(kw, q0, WINDOW + Q_BLOCK, axis=1)
        vwb = lax.dynamic_slice_in_dim(vw, q0, WINDOW + Q_BLOCK, axis=1)
        wpos = q0 - WINDOW + jnp.arange(WINDOW + Q_BLOCK)
        wmask = ((wpos[None, :] <= qpos[:, None]) & (wpos[None, :] > qpos[:, None] - WINDOW)
                 & (wpos[None, :] >= 0))
        sw = jnp.einsum('bqgrd,bkgd->bgrqk', qb, kwb).astype(jnp.float32) * scale
        p_win = masked_softmax(sw, wmask).astype(vwb.dtype)
        o_win = jnp.einsum('bgrqk,bkgd->bqgrd', p_win, vwb)
        g = lax.dynamic_slice_in_dim(gates, q0, Q_BLOCK, axis=1).reshape(b, Q_BLOCK, NSA_KV_HEADS, NSA_GROUP, NSA_BRANCHES)
        o = g[..., 0:1] * o_cmp + g[..., 1:2] * o_sel + g[..., 2:3] * o_win
        return o.reshape(b, Q_BLOCK, h, d)

    return sweep_query_blocks(block, s // Q_BLOCK)

def stick_breaking_attention(q, k, v):
    b, s, h, d = q.shape
    scale = d ** -0.5
    kpos = jnp.arange(s)

    def block(i):
        q0 = i * Q_BLOCK
        qpos = q0 + jnp.arange(Q_BLOCK)
        qb = lax.dynamic_slice_in_dim(q, q0, Q_BLOCK, axis=1)
        z = jnp.einsum('bqhd,bkhd->bhqk', qb, k).astype(jnp.float32) * scale
        strict = kpos[None, :] < qpos[:, None]
        log_beta = jax.nn.log_sigmoid(z)
        log_rem = jnp.where(strict, jax.nn.log_sigmoid(-z), 0.0)
        suffix = lax.cumsum(log_rem, axis=3, reverse=True) - log_rem
        a = jnp.where(strict, jnp.exp(log_beta + suffix), 0.0).astype(v.dtype)
        return jnp.einsum('bhqk,bkhd->bqhd', a, v)

    return sweep_query_blocks(block, s // Q_BLOCK)

def second_inputs(seed: int = 0) -> dict:
    key = jax.random.key(seed)
    ks = iter(jax.random.split(key, 32))
    f32 = jnp.float32
    L = DEPTH

    def nrm(shape, fan_in):
        return jax.random.normal(next(ks), shape, f32) * (fan_in ** -0.5)

    def gain(shape):
        return 1.0 + 0.02 * jax.random.normal(next(ks), shape, f32)

    return {
        'x': jax.random.normal(next(ks), (BATCH, SEQ, D_MODEL), f32),
        'ffn1_norm': gain((L, D_MODEL)),
        'ffn1_w_gate': nrm((L, D_MODEL, D_FF_2), D_MODEL),
        'ffn1_w_up': nrm((L, D_MODEL, D_FF_2), D_MODEL),
        'ffn1_w_down': nrm((L, D_FF_2, D_MODEL), D_FF_2),
        'mix_norm': gain((L, D_MODEL)),
        'w_in': nrm((L, D_MODEL, D_IN_2), D_MODEL),
        'mla_q_norm': gain((L, MLA_Q_LORA)),
        'mla_w_uq': nrm((L, MLA_Q_LORA, MLA_HEADS * (MLA_NOPE + MLA_ROPE)), MLA_Q_LORA),
        'mla_kv_norm': gain((L, MLA_KV_LORA)),
        'mla_w_ukv': nrm((L, MLA_KV_LORA, MLA_HEADS * (MLA_NOPE + MLA_V)), MLA_KV_LORA),
        'nsa_gate_bias': 0.1 * jax.random.normal(next(ks), (L, NSA_HEADS * NSA_BRANCHES), f32),
        'nsa_cmp_pos_k': 0.1 * jax.random.normal(next(ks), (L, CMP_LEN, HEAD_DIM), f32),
        'nsa_cmp_w1_k': nrm((L, CMP_LEN * HEAD_DIM, CMP_HIDDEN), CMP_LEN * HEAD_DIM),
        'nsa_cmp_w2_k': nrm((L, CMP_HIDDEN, HEAD_DIM), CMP_HIDDEN),
        'nsa_cmp_pos_v': 0.1 * jax.random.normal(next(ks), (L, CMP_LEN, HEAD_DIM), f32),
        'nsa_cmp_w1_v': nrm((L, CMP_LEN * HEAD_DIM, CMP_HIDDEN), CMP_LEN * HEAD_DIM),
        'nsa_cmp_w2_v': nrm((L, CMP_HIDDEN, HEAD_DIM), CMP_HIDDEN),
        'w_out': nrm((L, D_MIX_2, D_MODEL), D_MIX_2),
        'ffn2_norm': gain((L, D_MODEL)),
        'ffn2_w_gate': nrm((L, D_MODEL, D_FF_2), D_MODEL),
        'ffn2_w_up': nrm((L, D_MODEL, D_FF_2), D_MODEL),
        'ffn2_w_down': nrm((L, D_FF_2, D_MODEL), D_FF_2),
        'final_norm': gain((D_MODEL,)),
    }

def second_block(x, ffn1_norm, ffn1_w_gate, ffn1_w_up, ffn1_w_down, mix_norm, w_in,
              mla_q_norm, mla_w_uq, mla_kv_norm, mla_w_ukv,
              nsa_gate_bias, nsa_cmp_pos_k, nsa_cmp_w1_k, nsa_cmp_w2_k,
              nsa_cmp_pos_v, nsa_cmp_w1_v, nsa_cmp_w2_v, w_out,
              ffn2_norm, ffn2_w_gate, ffn2_w_up, ffn2_w_down, final_norm):
    b, s, _ = x.shape
    pos = jnp.arange(s, dtype=jnp.int32)
    split_at = [int(c) for c in np.cumsum(IN_WIDTHS)[:-1]]
    for l in range(DEPTH):
        x = x + 0.5 * swiglu(rmsnorm(x, ffn1_norm[l]), ffn1_w_gate[l], ffn1_w_up[l], ffn1_w_down[l])
        h = rmsnorm(x, mix_norm[l])
        (c_q, c_kv, k_rope, n_q, n_kc, n_vc, n_ks, n_vs, n_kw, n_vw, n_gate,
         sb_q, sb_k, sb_v) = jnp.split(h @ w_in[l], split_at, axis=-1)
        o_mla = mla_attention(c_q, c_kv, k_rope, mla_q_norm[l], mla_w_uq[l],
                              mla_kv_norm[l], mla_w_ukv[l], pos)
        gates = jax.nn.sigmoid(n_gate + nsa_gate_bias[l]).reshape(b, s, NSA_HEADS, NSA_BRANCHES)
        o_nsa = nsa_attention(split_heads(n_q, NSA_HEADS),
                              split_heads(n_kc, NSA_KV_HEADS), split_heads(n_vc, NSA_KV_HEADS),
                              split_heads(n_ks, NSA_KV_HEADS), split_heads(n_vs, NSA_KV_HEADS),
                              split_heads(n_kw, NSA_KV_HEADS), split_heads(n_vw, NSA_KV_HEADS),
                              gates, nsa_cmp_pos_k[l], nsa_cmp_w1_k[l], nsa_cmp_w2_k[l],
                              nsa_cmp_pos_v[l], nsa_cmp_w1_v[l], nsa_cmp_w2_v[l], pos)
        o_sb = stick_breaking_attention(split_heads(sb_q, SB_HEADS), split_heads(sb_k, SB_HEADS),
                                        split_heads(sb_v, SB_HEADS))
        o = jnp.concatenate([o_mla.reshape(b, s, -1), o_nsa.reshape(b, s, -1),
                             o_sb.reshape(b, s, -1)], axis=-1)
        x = x + o @ w_out[l]
        x = x + 0.5 * swiglu(rmsnorm(x, ffn2_norm[l]), ffn2_w_gate[l], ffn2_w_up[l], ffn2_w_down[l])
    return rmsnorm(x, final_norm)


def setup_inputs(seed=0):
    out = dict(first_inputs(seed))
    for name, value in second_inputs(seed + 1).items():
        if name != "x":
            out[name + "_2"] = value
    return out


def reference(
    x, norm_mix_pre, norm_mix_post, norm_mlp_pre, norm_mlp_post, w_in, attn_rel_bias, conv_w,
    conv_b, conv_ln_g, conv_ln_b, w_out, w_up, w_down, ffn1_norm_2, ffn1_w_gate_2, ffn1_w_up_2,
    ffn1_w_down_2, mix_norm_2, w_in_2, mla_q_norm_2, mla_w_uq_2, mla_kv_norm_2, mla_w_ukv_2,
    nsa_gate_bias_2, nsa_cmp_pos_k_2, nsa_cmp_w1_k_2, nsa_cmp_w2_k_2, nsa_cmp_pos_v_2,
    nsa_cmp_w1_v_2, nsa_cmp_w2_v_2, w_out_2, ffn2_norm_2, ffn2_w_gate_2, ffn2_w_up_2,
    ffn2_w_down_2, final_norm_2,
):
    x = first_block(
        x, norm_mix_pre, norm_mix_post, norm_mlp_pre, norm_mlp_post, w_in, attn_rel_bias,
        conv_w, conv_b, conv_ln_g, conv_ln_b, w_out, w_up, w_down,
    )
    return second_block(
        x, ffn1_norm_2, ffn1_w_gate_2, ffn1_w_up_2, ffn1_w_down_2, mix_norm_2, w_in_2,
        mla_q_norm_2, mla_w_uq_2, mla_kv_norm_2, mla_w_ukv_2, nsa_gate_bias_2, nsa_cmp_pos_k_2,
        nsa_cmp_w1_k_2, nsa_cmp_w2_k_2, nsa_cmp_pos_v_2, nsa_cmp_w1_v_2, nsa_cmp_w2_v_2,
        w_out_2, ffn2_norm_2, ffn2_w_gate_2, ffn2_w_up_2, ffn2_w_down_2, final_norm_2,
    )


_drawn_inputs = setup_inputs


def setup_inputs(seed=0):
    import zlib

    import numpy as np

    out = dict(_drawn_inputs(seed))
    spreads = {}
    factors = {'norm_mlp_pre': 2.995,
     'norm_mlp_post': 3.146,
     'conv_ln_g': 3.345,
     'conv_ln_b': 3.552,
     'ffn1_norm_2': 8.0,
     'mix_norm_2': 8.0,
     'mla_q_norm_2': 8.0,
     'mla_kv_norm_2': 8.0,
     'nsa_gate_bias_2': 8.0,
     'nsa_cmp_pos_k_2': 8.0,
     'nsa_cmp_w1_k_2': 3.269,
     'nsa_cmp_w2_k_2': 3.128,
     'nsa_cmp_pos_v_2': 14.96,
     'ffn2_norm_2': 8.0,
     'final_norm_2': 8.167}
    for name, (base, spread) in spreads.items():
        noise = np.random.default_rng([zlib.crc32(name.encode()), seed]).standard_normal(out[name].shape)
        drawn = base * np.exp(spread * noise) if base else spread * noise
        out[name] = __import__('jax').numpy.asarray(drawn.astype(out[name].dtype))
    for name, factor in factors.items():
        out[name] = (out[name] * factor).astype(out[name].dtype)
    return out
```

```python
from contextlib import ExitStack

import numpy as np

import concourse.bass as bass
from concourse import mybir

F32 = mybir.dt.float32
F32R = mybir.dt.float32r
BF16 = mybir.dt.bfloat16
ALU = mybir.AluOpType
ACT = mybir.ActivationFunctionType
AXX = mybir.AxisListType.X

P = 128
D = 1024
S = 512
KT = D // P
QT = S // P
LAYERS = 2
UNIT = 1024
RING = 4
LOOK = 2
EPS = 1e-6
NEG = -1e30
LN_SET = "natural_log_exp_and_others"
HD = 64

D_IN, FF1, HEADS1 = 3200, 4096, 6
T1 = FF1 // P
TAPS, CONV = 31, 256
BIAS_ROW = 640
D_IN2, FF2 = 2354, 2816
T2 = FF2 // P
MLA_H, MLA_D, SB_H, NSA_H = 6, 96, 4, 6
CMP_N = 31
MLA_SCALE, HEAD_SCALE = float(96) ** -0.5, 0.125

C_IDENT, C_ONES, C_BLK, C_TRI, C_STRICT, C_PERM_R, C_PERM_N, C_PERM_M, C_VALID = [128 * i for i in range(9)]
C_WORDS = 8 * 128 + 4
SCR_SQ, SCR_RSTD, SCR_TMP = 0, 1024, 1536
A_P, A_PT, A_SB, A_H = 0, 1024, 2048, 3072
A_Q, A_K, A_V, A_SG, A_Y, A_RQ, A_RK, A_RV, MIX = 4096, 5632, 7168, 8704, 9728, 10816, 12352, 13888, 15424
F_AT = 3072
YW = 544
M_GATE, M_POSX, M_KC, M_VC, M_HID = 2048, 2128, 2640, 2704, 2832
M_Q, M_K, M_V, M_PE = 3072, 6144, 9216, 10752
B_Q, B_K, B_V = 11264, 12288, 13312
N_Q, N_KC, N_VC, N_KS, N_KW, N_VS, N_VW = 3072, 4608, 5120, 5632, 6144, 6656, 7168
B_LR, B_LB = 7680, 8960
G_WORDS = 19520
OUT_AT = 4096
MASK_AT = 6144
SB_AT = [0, 512, 896, 1152]
ACT_STEPS, DVE_STEPS = (6, 37), (119, 318)
P1_MIX, P1_POST, P1_MLP, P1_MPOST, P1_CW, P1_CB, P1_LG, P1_LB = 0, 8, 16, 24, 32, 94, 96, 98
P2_F1, P2_MIX, P2_F2, P2_QN, P2_KVN, P2_GB, P2_PK, P2_PV, P2_WK, P2_WV = 0, 8, 16, 24, 26, 27, 45, 77, 109, 173
PRM_WORDS = 240


def constants():
    f = np.float32
    p = np.arange(P)
    c = np.zeros((P, C_WORDS), f)
    c[:, C_IDENT:C_IDENT + P] = np.eye(P)
    c[:, C_ONES:C_ONES + P] = 1.0
    c[:, C_BLK:C_BLK + P] = (p[:, None] // HD == p[None, :] // HD) / HD
    c[:, C_TRI:C_TRI + P] = p[:, None] > p[None, :]
    c[:, C_STRICT:C_STRICT + P] = p[:, None] < p[None, :]
    in_head = p % HD
    partner_r = p - in_head + (in_head + 32) % HD
    partner_n = np.where(in_head < 8, p + 8, np.where(in_head < 16, p - 8, p))
    partner_m = np.where((p >= 64) & (p < 80), p + 16, np.where((p >= 80) & (p < 96), p - 16, p))
    for at, partner in ((C_PERM_R, partner_r), (C_PERM_N, partner_n), (C_PERM_M, partner_m)):
        c[partner, at + p] = 1.0
    c[:, C_VALID:C_VALID + QT] = (p[:, None] + P * np.arange(QT)[None, :]) >= 31
    q, k = p[:, None], p[None, :]
    masks = np.zeros((P, 4 * P), f)
    masks[:, 0:P] = np.eye(P)
    masks[:, P:2 * P] = np.where(k > q, NEG, 0)
    masks[:, 2 * P:3 * P] = np.where(k // 64 > q // 64, NEG, 0)
    blk = np.arange(32)[None, None, :]
    tok = (p[:, None] + P * np.arange(QT)[None, :])[:, :, None]
    masks[:, 3 * P:] = np.where(16 * blk + 31 > tok, NEG, 0).reshape(P, P)

    pos = np.arange(S, dtype=f)
    t1 = np.zeros((P, 4096), f)
    log_g = np.log1p(-(2.0 ** (-5.0 - np.arange(HEADS1))))
    diff = (np.arange(S)[None, :] - p[:, None]).astype(np.float64)
    for h in range(HEADS1):
        t1[:, h * S:(h + 1) * S] = np.where(diff >= 0, np.exp(np.maximum(diff, 0) * log_g[h]) * HEAD_SCALE, 0)
    inv = (f(1.0) / (f(10000.0) ** np.linspace(0, 1, 32, dtype=f))).astype(f)
    ang = (inv[in_head % 32][:, None] * pos[None, :]).astype(f)
    t1[:, 3072:3584] = np.cos(ang)
    t1[:, 3584:4096] = np.where(in_head < 32, -1, 1)[:, None] * np.sin(ang)

    t2 = np.zeros((P, 2048), f)

    def partial(at, first, half, rows):
        theta = (f(500000.0) ** (-np.arange(half, dtype=f) / f(half))).astype(f)
        a = (theta[np.where(first >= 0, first, 0) % half][:, None] * pos[None, :]).astype(f)
        on = (first >= 0)[:, None]
        t2[:, at:at + S] = np.where(on, np.cos(a), 1)
        t2[:, at + S:at + 2 * S] = np.where(on, np.where(first < half, -1, 1)[:, None] * np.sin(a), 0)
    partial(0, np.where(in_head < 16, in_head, -1), 8, P)
    partial(1024, np.where((p >= 64) & (p < 96), p - 64, -1), 16, P)
    return c, masks, t1, t2


class Count:

    def __init__(self, sem, per, base=0, step=1):
        self.sem, self.per, self.base, self.step, self.k = sem, per, base, step, 0

    def at(self, layer, k):
        return layer * (self.per * self.step) + (self.base + k) * self.step

    def next(self):
        self.k += 1
        return self.sem

    def now(self, layer):
        return self.at(layer, self.k)

    def check(self):
        if self.k != self.per:
            raise ValueError(f"{self.k} steps, {self.per} stated")


class Counts:

    def evac(self, gr):
        return self.evacs[gr["bank"]]

    def emptied(self, layer, gr):
        return self.evac(gr).at(layer, gr["e"] // 2 + 1)


def softmax_items_block1():
    return [dict(h=h, i=i, n=P * (i + 1), branch=None, first=True, last=True) for h in range(HEADS1) for i in range(QT)]


def softmax_items_block2():
    mla = [dict(h=h, i=i, n=P * (i + 1), branch="mla", first=True, last=True) for h in range(MLA_H) for i in range(QT)]
    nsa = [dict(h=h, i=i, n=32 if b == "cmp" else P * (i + 1), branch=b, first=b == "sel", last=b == "cmp")
           for h in range(NSA_H) for i in range(QT) for b in ("sel", "win", "cmp")]
    return mla, nsa




def copies(groups):
    e = 0
    for gr in groups:
        gr["bank"], gr["e"] = e % 2, e
        if gr.get("evac", True):
            e += 1
    return groups, e


def plan_block1():
    units, groups = [], {}
    turn = ["act", "dve"]

    def proj(name, kind, col, **more):
        units.append(("w_in", col))
        groups[name] = dict(name=name, kind=kind, unit=len(units) - 1, **more)

    names = []
    def add(name, kind, col, **more):
        proj(name, kind, col, **more)
        names.append(name)
    def copy_to(n, at, scale=None):
        return dict(frees=turn[n % 2], dst=at)
    add("q0", "fm", 0, **copy_to(0, A_Q))
    add("k0", "fm", 384, **copy_to(1, A_K))
    add("v0", "tm", 768, frees="act", dst=A_V, off=0, pitch=384)
    for t in range(2):
        add(f"cg{t}", "fm", 1408 + 128 * t, frees="act", dst=A_SG + S * t, func="Sigmoid")
    for t in range(2):
        add(f"ca{t}", "fm", 1152 + 128 * t, frees="dve", glu=t)
    for t in (1, 2):
        add(f"q{t}", "fm", 128 * t, **copy_to(0, A_Q + S * t))
        add(f"k{t}", "fm", 384 + 128 * t, **copy_to(1, A_K + S * t))
        add(f"v{t}", "tm", 768 + 128 * t, frees="act", dst=A_V, off=128 * t, pitch=384)
    for m, (at, col) in enumerate(((A_RQ, 1664), (A_RK, 2048))):
        for t in range(3):
            add(f"r{'qk'[m]}{t}", "fm", col + 128 * t, frees="act", dst=at + S * t)
            if t:
                names.append(f"s{'qk'[m]}{t - 1}")
        names.append(f"s{'qk'[m]}2")
        for t in range(3):
            groups[f"s{'qk'[m]}{t}"] = dict(name=f"s{'qk'[m]}{t}", kind="swap", of=f"r{'qk'[m]}{t}", tile=at + S * t,
                                          rows=(0, P), perm="r", tab=3072, frees="dve")
    for t in range(3):
        add(f"rv{t}", "tm", 2432 + 128 * t, frees="dve", dst=A_RV, off=128 * t, pitch=384)
    for t in range(3):
        add(f"rg{t}", "fm", 2816 + 128 * t, frees="act", dst=MIX + S * (5 + t), func="Silu")
    steps = [("g", n) for n in names[:3]]
    items = softmax_items_block1()
    i = taps = 0
    for n in names[3:]:
        steps.append(("g", n))
        if not n.startswith(("cg", "rg")) and i < len(items) + 2:
            steps.append(("i", i))
            i += 1
        if ("g", "ca1") in steps and n != "ca1" and taps < TAPS:
            steps.append(("taps", taps, min(taps + 2, TAPS)))
            taps += 2
    while i < len(items) + 2:
        steps.append(("i", i))
        i += 1
        if taps < TAPS:
            steps.append(("taps", taps, min(taps + 2, TAPS)))
            taps += 2
    if taps < TAPS:
        steps.append(("taps", taps, TAPS))
    groups["cm"] = dict(name="cm", kind="cmean", frees="dve")
    groups["cv"] = dict(name="cv", kind="cvar", frees="act")
    steps += [("r", j) for j in range(4)] + [("g", "cm")] + [("r", j) for j in range(4, 8)] + [("g", "cv")]
    for t in range(3):
        if t:
            steps += [("r", j) for j in range(8 * t, 8 * t + 8)]
        steps.append(("r_out", t))
        groups[f"lm{t}"] = dict(name=f"lm{t}", kind="rmean", t=t, frees="dve")
        groups[f"lv{t}"] = dict(name=f"lv{t}", kind="rvar", t=t, frees="act")
        steps += [("g", f"lm{t}"), ("g", f"lv{t}")]
    order = [groups[s[1]] for s in steps if s[0] == "g"]
    n_in = len(units)
    units += [("w_out", 128 * m) for m in range(KT)] + [("w_up", t) for t in range(T1)] + [("w_down", t) for t in range(T1)]
    return units, order, groups, steps, n_in


def plan_block2():
    units = []
    for t in range(T2):
        units += [("g1", t), ("u1", t)]
    units += [("d1", t) for t in range(T2)]
    first = len(units)
    groups, steps, units_at = {}, [], {}

    def add(name, kind, src, **more):
        if src is not None:
            units.append(src)
            more["unit"] = len(units) - 1
        groups[name] = dict(name=name, kind=kind, **more)
        return ("g", name)

    for t in range(2):
        steps.append(add(f"cq{t}", "fm", ("w_in", 128 * t), frees="act", dst=M_V + S * t))
    steps.append(add("ckv", "fm", ("w_in", 256), frees="act", dst=M_V + 2 * S))
    steps.append(("rn", "cq"))
    steps.append(("rn", "ckv"))
    steps.append(add("pe", "fm", ("w_in", 320), frees="act", dst=M_PE, rows=(64, 96)))
    steps.append(add("spe", "swap", None, of="pe", tile=M_PE, rows=(64, 96), perm="m", tab=1024, frees="dve"))
    for j in range(2):
        for i in range(3):
            h = 3 * j + i
            if i == 0:
                units.append(("w_uq", 288 * j))
            groups[f"mq{h}"] = dict(name=f"mq{h}", kind="uq", unit=len(units) - 1, j=i, frees="act", dst=M_Q + S * h, rows=(0, MLA_D))
            steps.append(("g", f"mq{h}"))
            if h:
                steps.append(("g", f"sm{h - 1}"))
            groups[f"sm{h}"] = dict(name=f"sm{h}", kind="swap", of=f"mq{h}", tile=M_Q + S * h, rows=(0, MLA_D), perm="m", tab=1024, frees="dve")
    steps.append(("g", "sm5"))
    units.append(("w_ukv", 0))
    for h in range(MLA_H):
        groups[f"mk{h}"] = dict(name=f"mk{h}", kind="ukv_k", unit=len(units) - 1, j=h, frees=("act", "dve")[h % 2], dst=M_K + S * h, rows=(0, HD))
        steps.append(("g", f"mk{h}"))
    for t in range(QT):
        groups[f"mv{t}"] = dict(name=f"mv{t}", kind="ukv_v", unit=len(units) - 1, j=t, frees=("act", "dve")[t % 2], dst=M_V + 384 * t)
        steps.append(("g", f"mv{t}"))
    fill = []
    for t in range(2):
        fill.append(add(f"bq{t}", "fm", ("w_in", 1586 + 128 * t), frees="act", dst=B_Q + S * t))
    for t in range(2):
        fill.append(add(f"bk{t}", "fm", ("w_in", 1842 + 128 * t), frees="dve", dst=B_K + S * t))
    for t in range(2):
        fill.append(add(f"bv{t}", "tm", ("w_in", 2098 + 128 * t), frees="act", dst=B_V, off=128 * t, pitch=256))
    for j in range(26):
        steps.append(("i", j, 0, 24))
        if j % 4 == 3 and fill:
            steps.append(fill.pop(0))
    fill = []
    for t in range(3):
        fill.append(add(f"nq{t}", "fm", ("w_in2", t), frees="act", dst=N_Q + S * t, overlay=True))
        if t:
            fill.append(("g", f"snq{t - 1}"))
    fill.append(("g", "snq2"))
    for name, col, at in (("kc", 800, N_KC), ("vc", 928, N_VC), ("ks", 1056, N_KS), ("kw", 1312, N_KW)):
        fill.append(add(f"n{name}", "fm", ("w_in", col), frees="act", dst=at, overlay=True))
        if name != "vc":
            fill.append(("g", f"sn{name}"))
    tiles = {"q0": N_Q, "q1": N_Q + S, "q2": N_Q + 2 * S, "kc": N_KC, "ks": N_KS, "kw": N_KW}
    for name, at in tiles.items():
        groups[f"sn{name}"] = dict(name=f"sn{name}", kind="swap", of=f"n{name}", tile=at, rows=(0, P), perm="n", tab=0, frees="dve")
    fill.append(add("nvs", "tm", ("w_in", 1184), frees="dve", dst=N_VS, off=0, pitch=128))
    fill.append(add("nvw", "tm", ("w_in", 1440), frees="dve", dst=N_VW, off=0, pitch=128))
    fill.append(add("gates", "gates", ("w_in", 1568), frees="dve"))
    for kv in range(2):
        for u in range(4):
            fill.append(add(f"c{kv}{u}", "cmp", ("w1", kv, u), kv=kv, u=u, evac=u == 3, frees="act"))
        groups[f"w2{kv}"] = dict(name=f"w2{kv}", kind="w2", kv=kv, frees="act")
        fill.append(("g", f"w2{kv}"))
    for h in range(SB_H):
        for s in (("z", h, 3), ("z", h, 2), ("suf", h, 3), ("z", h, 1), ("suf", h, 2), ("z", h, 0), ("suf", h, 1), ("suf", h, 0), ("sbo", h)):
            steps.append(s)
            if s[0] == "z" and fill:
                steps += [fill.pop(0) for _ in range(min(2, len(fill)))]
    steps += fill
    steps += [("i", j, 24, 96) for j in range(24, 98)]
    order = [groups[s[1]] for s in steps if s[0] == "g"]
    wo = len(units)
    units += [("w_out", 128 * m) for m in range(KT)]
    for t in range(T2):
        units += [("g2", t), ("u2", t)]
    units += [("d2", t) for t in range(T2)]
    return units, order, groups, steps, first, wo


def build(nc, x_in, cst, msk, tab1, tab2, scratch, out, w):
    with ExitStack() as ctx:
        def sb(name, shape, dt=F32):
            return ctx.enter_context(nc.sbuf_tensor(name, shape, dt))

        x = sb("x", [P, KT, S])
        hh, hl = sb("hh", [P, KT, S], F32R), sb("hl", [P, KT, S], F32R)
        raw = sb("raw", [P, RING, UNIT])
        whi, wlo = sb("whi", [P, RING, UNIT], F32R), sb("wlo", [P, RING, UNIT], F32R)
        fshi, fslo = sb("fshi", [P, 3, S], F32R), sb("fslo", [P, 3, S], F32R)
        G = sb("G", [P, G_WORDS])
        tab = sb("tab", [P, 4096])
        c_sb = sb("c_sb", [P, C_WORDS])
        m_sb = sb("m_sb", [P, 4 * P], BF16)
        prm = sb("prm", [P, PRM_WORDS])
        fin_g = sb("fin_g", [P, KT])
        stat = sb("stat", [P, 4, 4])
        eps = sb("eps", [P, 1])
        bank = [ctx.enter_context(nc.psum_tensor(f"bank{i}", [P, S], F32)) for i in range(8)]

        def g(at, n=S, rows=(0, P)):
            return G[rows[0]:rows[1], at:at + n]

        def cs(at, rows=(0, P), n=P):
            return c_sb[rows[0]:rows[1], at:at + n]

        def half(k):
            return (HD * k, HD * k + HD)

        ident, ones, blk, tri, strict = cs(C_IDENT), cs(C_ONES), cs(C_BLK), cs(C_TRI), cs(C_STRICT)
        identb, causal, chunked, cmpmask = (m_sb[:, P * i:P * i + P] for i in range(4))
        sq, rstd, tmp = [g(SCR_SQ), g(SCR_SQ + S)], g(SCR_RSTD), [g(SCR_TMP), g(SCR_TMP + S)]
        rt = [g(SCR_SQ), g(SCR_SQ + S)]
        S_B, T_B, O_B = (2, 3), (4, 5), (6, 7)

        units1, order1, groups1, steps1, wo1 = plan_block1()
        units2, order2, groups2, steps2, in2, wo2 = plan_block2()
        items = (softmax_items_block1(), sum(softmax_items_block2(), []))
        blocks = []
        for units, order, groups, steps, wo in ((units1, order1, groups1, steps1, wo1), (units2, order2, groups2, steps2, wo2)):
            first = 0 if units is units1 else in2
            _, n_evac = copies(order)
            done, last_of = 0, {}
            for i in range(first):
                last_of[i] = i + 1
            done = first
            for gr in order:
                done += 1
                gr["done"] = done
                if gr.get("unit") is not None:
                    gr["starts"] = gr["unit"] not in last_of
                    last_of[gr["unit"]] = done
            for i in range(wo, len(units)):
                done += 1
                last_of[i] = done
            loads = [2 if u[0] in ("w1", "w_in2") else 1 for u in units]
            size = [576 if u[0] == "w_uq" else 768 if u[0] == "w_ukv" else UNIT for u in units]
            blocks.append(dict(units=units, order=order, groups=groups, steps=steps, wo=wo, first=first, n=len(units),
                               last_of=last_of, groups_n=done, loads=loads, size=size, evacs=[(n_evac + 1) // 2, n_evac // 2]))
        b1, b2 = blocks

        def sem(name):
            return ctx.enter_context(nc.semaphore(name))

        n1, n2 = len(items[0]), len(items[1])
        made = {}

        def counts_of(b):
            c = Counts()

            def signal(name, per1, per2, start=0, step=1):
                if name not in made:
                    made[name] = sem(name)
                if b == 0:
                    return Count(made[name], per1, start, step)
                return Count(made[name], per2, start + LAYERS * per1, step)

            c.landed = [signal(f"landed{s}", sum(b1["loads"][s::RING]), sum(b2["loads"][s::RING]), 0, 16)
                        for s in range(RING)]
            c.hi_done = signal("hi_done", b1["n"], b2["n"])
            c.lo_done = signal("lo_done", b1["n"], b2["n"], RING)
            c.group_done = signal("group_done", b1["groups_n"], b2["groups_n"])
            c.evacs = [signal(f"evac{p}", b1["evacs"][p], b2["evacs"][p]) for p in range(2)]
            c.x_ready = signal("x_ready", 16, 24, KT)
            c.rn_sq = signal("rn_sq", 32, 27)
            c.rn_used = signal("rn_used", 32, 27)
            c.rn_rstd = signal("rn_rstd", 4, 5)
            c.rn_tmp = signal("rn_tmp", 16, 27)
            c.rn_hi = signal("rn_hi", 16, 27)
            c.rn_lo = signal("rn_lo", 16, 27)
            c.mix_hi = signal("mix_hi", KT, KT)
            c.mix_lo = signal("mix_lo", KT, KT)
            c.y0 = signal("y0", 2, 0)
            c.qk = signal("qk", n1, n2)
            c.biased = signal("biased", n1, 0)
            c.maxed = signal("maxed", n1, n2)
            c.exped = signal("exped", n1, n2)
            c.scaled = signal("scaled", n1, n2)
            c.turned = signal("turned", n1, n2)
            c.pt = signal("pt", n1, n2)
            c.pv = signal("pv", n1, n2)
            c.o_done = signal("o_done", 12, 16)
            c.h_in = [signal(f"h_in{s}", 3, 0, 0, 16) for s in range(2)]
            c.r_s = signal("r_s", 24, 0)
            c.r_dec = signal("r_dec", 24, 0)
            c.r_pv = signal("r_pv", 24, 0)
            c.ln_sq = signal("ln_sq", 5, 0)
            c.ln_rstd = signal("ln_rstd", 4, 0)
            c.cv_out = signal("cv_out", 2, 0)
            c.ret_out = signal("ret_out", 3, 0)
            c.taps = signal("taps", 1, 0)
            c.z = signal("z", 0, 16)
            c.z_ln = signal("z_ln", 0, 16)
            c.z_lr = signal("z_lr", 0, 16)
            c.suf = signal("suf", 0, 16)
            c.suf_t = signal("suf_t", 0, 16)
            c.suf_a = signal("suf_a", 0, 16)
            c.suf_m = signal("suf_m", 0, 16)
            c.sb_pv = signal("sb_pv", 0, SB_H)
            c.kpe = signal("kpe", 0, MLA_H)
            c.px = signal("px", 0, 8)
            c.px_hi = signal("px_hi", 0, 8)
            c.px_lo = signal("px_lo", 0, 8)
            c.gate = signal("gate", 0, 1)
            c.relu = signal("relu", T1, 0, 4)
            c.f_done = signal("f_done", T1, 0, 2)
            c.silu = signal("silu", 0, 2 * T2, 2)
            c.f2_done = signal("f2_done", 0, 2 * T2, 2)
            c.f_hi = signal("f_hi", T1, 2 * T2)
            c.f_lo = signal("f_lo", T1, 2 * T2)
            c.act_step = signal("act_step", ACT_STEPS[0], ACT_STEPS[1])
            c.dve_step = signal("dve_step", DVE_STEPS[0], DVE_STEPS[1])
            c.prm_in = signal("prm_in", 9, 12, 0, 16)
            return c

        const_in, x_dma, tin, out_dma, scr_dma, bias_sem, fin, fin_ev, tout, tab_in = (
            sem(n) for n in ("const_in", "x_dma", "tin", "out_dma", "scr_dma", "bias_sem", "fin", "fin_ev", "tout", "tab_in"))
        rows_zero, gain_in, masks_ready = sem("rows_zero"), sem("gain_in"), sem("masks_ready")

        def slot3(t, s, n=UNIT):
            return t[:, s, 0:n]

        def f_tile(t):
            return G[:, bass.ds(F_AT + t * S, S)]

        block = ctx.enter_context(nc.Block())

        @block.sync
        def _(sp):
            sp.dma_start(g(0, QT * D).rearrange("p (t d) -> p t d", t=QT), x_in.rearrange("a (t p) d -> p (a t) d", p=P)).then_inc(x_dma, 16)
            sp.dma_start(c_sb[:, :], cst).then_inc(const_in, 16)
            sp.dma_start(g(MASK_AT), msk).then_inc(const_in, 16)
            sp.dma_start(tab[:, :], tab1).then_inc(const_in, 16)

            def load(c, b, l, n, at=None, k=0):
                kind, arg = b["units"][n][:2]
                s = n % RING
                more = 0 if at is None else at
                sp.wait_ge(c.lo_done.sem, c.lo_done.at(l, (n - RING + 1 if at is not None else max(n - RING + 1, 0)) + more))
                la = bass.ds(l, 1)
                cols8 = slot3(raw, s).rearrange("p (k n) -> p k n", k=KT)
                done = c.landed[s].sem
                sfx = "" if b is b1 else "_2"
                if kind in ("w_in", "w_out"):
                    src = w[kind + sfx][la, :, arg:arg + P].rearrange("a (k p) n -> p (a k) n", p=P)
                    sp.dma_start(cols8, src).then_inc(done, 16)
                elif kind == "w_in2":
                    for j in range(2):
                        c0 = 416 + 64 * arg + 192 * j
                        src = w["w_in_2"][la, :, c0:c0 + HD].rearrange("a (k p) n -> p (a k) n", p=P)
                        sp.dma_start(cols8[:, :, HD * j:HD * j + HD], src).then_inc(done, 16)
                elif kind == "w_uq":
                    src = w["mla_w_uq_2"][la, :, arg:arg + 288].rearrange("a (k p) n -> p (a k) n", p=P)
                    sp.dma_start(slot3(raw, s, 576).rearrange("p (k n) -> p k n", k=2), src).then_inc(done, 16)
                elif kind == "w_ukv":
                    sp.dma_start(slot3(raw, s, 768), w["mla_w_ukv_2"][la, :, :].rearrange("a p n -> (a p) n")).then_inc(done, 16)
                elif kind == "w1":
                    name = ("nsa_cmp_w1_k_2", "nsa_cmp_w1_v_2")[arg]
                    u = b["units"][n][2]
                    src = w[name][la, 512 * u:512 * u + 512, :].rearrange("a (t d) n -> d (a t) n", d=HD)
                    for j in range(2):
                        sp.dma_start(raw[HD * j:HD * j + HD, s, :].rearrange("p (t n) -> p t n", t=8), src).then_inc(done, 16)
                else:
                    name = {"w_up": "w_up", "w_down": "w_down", "g1": "ffn1_w_gate_2", "u1": "ffn1_w_up_2", "d1": "ffn1_w_down_2",
                            "g2": "ffn2_w_gate_2", "u2": "ffn2_w_up_2", "d2": "ffn2_w_down_2"}[kind]
                    step = 2 if kind[0] in "gu" else 1
                    tile = arg * P + more * (P // step)
                    if kind in ("w_down", "d1", "d2"):
                        src = w[name][la, bass.ds(tile, P), :].rearrange("a p n -> (a p) n")
                        sp.dma_start(slot3(raw, s), src).then_inc(done, 16)
                    else:
                        src = w[name][la, :, bass.ds(tile, P)].rearrange("a (k p) n -> p (a k) n", p=P)
                        sp.dma_start(cols8, src).then_inc(done, 16)

            def mlp_units(c, b, l, n0, n):
                if n0 == 0:
                    for j in range(RING):
                        load(c, b, l, j)
                with sp.Fori(1 if n0 == 0 else 0, n // 4) as i:
                    for j in range(4):
                        load(c, b, l, n0 + j, i * 4)
                for j in range(n // 4 * 4, n):
                    load(c, b, l, n0 + j)

            c = counts_of(0)
            with sp.Fori(0, LAYERS) as l:
                for n in range(b1["wo"] + KT):
                    load(c, b1, l, n)
                mlp_units(c, b1, l, b1["wo"] + KT, T1)
                mlp_units(c, b1, l, b1["wo"] + KT + T1, T1)
            c = counts_of(1)
            with sp.Fori(0, LAYERS) as l:
                mlp_units(c, b2, l, 0, 2 * T2)
                mlp_units(c, b2, l, 2 * T2, T2)
                for n in range(b2["first"], b2["wo"] + KT):
                    load(c, b2, l, n)
                mlp_units(c, b2, l, b2["wo"] + KT, 2 * T2)
                mlp_units(c, b2, l, b2["wo"] + KT + 2 * T2, T2)
            for t in range(QT):
                sp.wait_ge(fin_ev, 2 * t + 2)
                sp.dma_start(out[0, P * t:P * t + P, :], g(OUT_AT + D * t, D)).then_inc(out_dma, 16)
            sp.wait_ge(out_dma, 16 * QT)

        @block.gpsimd
        def _(pool):
            pool.dma_start(fin_g[:, :], w["final_norm_2"].rearrange("(k p) -> p k", p=P), allow_slow_non_contiguous=True).then_inc(gain_in, 16)
            rows = LAYERS * HEADS1
            pool.dma_start(G[0:rows, 4096:4096 + 257], w["attn_rel_bias"].rearrange("l h n -> (l h) n")).then_inc(scr_dma, 16)
            pool.wait_ge(bias_sem, 3)
            pool.dma_start(scratch, G[0:rows, 4608:4608 + BIAS_ROW]).then_inc(scr_dma, 16)
            pool.wait_ge(scr_dma, 32)

            def columns(name, l, k):
                return w[name][bass.ds(l, 1), :].rearrange("a (k p) -> p (a k)", p=P)

            c = counts_of(0)
            with pool.Fori(0, LAYERS) as l:
                pool.wait_ge(c.x_ready.sem, c.x_ready.at(l, 0))
                done = c.prm_in.sem
                for name, at in (("norm_mix_pre", P1_MIX), ("norm_mix_post", P1_POST), ("norm_mlp_pre", P1_MLP), ("norm_mlp_post", P1_MPOST)):
                    pool.dma_start(prm[:, at:at + KT], columns(name, l, KT), allow_slow_non_contiguous=True).then_inc(done, 16)
                for name, at in (("conv_b", P1_CB), ("conv_ln_g", P1_LG), ("conv_ln_b", P1_LB)):
                    pool.dma_start(prm[:, at:at + 2], columns(name, l, 2), allow_slow_non_contiguous=True).then_inc(done, 16)
                for t in range(2):
                    src = w["conv_w"][bass.ds(l, 1), :, P * t:P * t + P].rearrange("a k p -> p (a k)")
                    pool.dma_start(prm[:, P1_CW + TAPS * t:P1_CW + TAPS * t + TAPS], src, allow_slow_non_contiguous=True).then_inc(done, 16)
                for h in range(HEADS1):
                    if h >= 2:
                        pool.wait_ge(c.biased.sem, c.biased.at(l, 4 * h - 4))
                    src = bass.AP(tensor=scratch.tensor, offset=l * (HEADS1 * BIAS_ROW) + h * BIAS_ROW, ap=[[1, P], [1, S]])
                    pool.dma_start(g(A_H + S * (h % 2)), src).then_inc(c.h_in[h % 2].sem, 16)
            c = counts_of(1)
            pool.wait_ge(c.x_ready.sem, c.x_ready.at(0, 0))
            pool.dma_start(tab[:, 0:2048], tab2).then_inc(tab_in, 16)
            with pool.Fori(0, LAYERS) as l:
                pool.wait_ge(c.x_ready.sem, c.x_ready.at(l, 0))
                done = c.prm_in.sem
                la = bass.ds(l, 1)
                for name, at, k in (("ffn1_norm_2", P2_F1, KT), ("mix_norm_2", P2_MIX, KT), ("ffn2_norm_2", P2_F2, KT),
                                    ("mla_q_norm_2", P2_QN, 2), ("mla_kv_norm_2", P2_KVN, 1)):
                    pool.dma_start(prm[:, at:at + k], columns(name, l, k), allow_slow_non_contiguous=True).then_inc(done, 16)
                pool.dma_start(prm[:, P2_GB:P2_GB + 18], w["nsa_gate_bias_2"][la, :].to_broadcast([P, 18])).then_inc(done, 16)
                for name, at in (("nsa_cmp_pos_k_2", P2_PK), ("nsa_cmp_pos_v_2", P2_PV)):
                    src = w[name][la, :, :].rearrange("a t d -> d (a t)")
                    for j in range(2):
                        pool.dma_start(prm[HD * j:HD * j + HD, at:at + 32], src, allow_slow_non_contiguous=True).then_inc(done, 16)
                for name, at in (("nsa_cmp_w2_k_2", P2_WK), ("nsa_cmp_w2_v_2", P2_WV)):
                    pool.dma_start(prm[:, at:at + HD], w[name][la, :, :].rearrange("a p n -> (a p) n")).then_inc(done, 16)

        def landed(c, b, eng, l, n, more=0):
            s = n % RING
            eng.wait_ge(c.landed[s].sem, c.landed[s].at(l, sum(b["loads"][s:n + 1:RING]) + more))

        @block.scalar
        def _(act):
            def hi(c, b, l, n, i=None):
                s, m = n % RING, b["size"][n]
                more = 0 if i is None else i * 4
                landed(c, b, act, l, n, 0 if i is None else i)
                if n >= RING or i is not None:
                    act.wait_ge(c.group_done.sem, c.group_done.at(l, b["last_of"][n - RING] + more if n >= RING else n - RING + 1 + more))
                elif b is b2:
                    act.wait_ge(c.group_done.sem, c.group_done.at(l, 0))
                act.activation(slot3(whi, s, m), slot3(raw, s, m), ACT.Copy).then_inc(c.hi_done.sem, 1)

            def norm(c, l, r, a, b0, src, ready, rbank, dim, dst=None):
                n = len(src)
                for t in range(n):
                    ready(t)
                    if t >= 2:
                        act.wait_ge(c.rn_used.sem, c.rn_used.at(l, a + t - 1))
                    act.activation(sq[t % 2], src[t], ACT.Square).then_inc(c.rn_sq.sem, 1)
                act.wait_ge(c.rn_used.sem, c.rn_used.at(l, a + n))
                act.activation(rstd, rbank, ACT.Ln, scale=1.0 / dim, bias=eps[:, 0:1]).then_inc(c.act_step.next(), 1)
                act.wait_ge(c.act_step.sem, c.act_step.now(l))
                act.activation(rstd, rstd, ACT.Exp, scale=-0.5).then_inc(c.rn_rstd.sem, 1)
                if dst is not None:
                    for t in range(n):
                        act.wait_ge(c.rn_tmp.sem, c.rn_tmp.at(l, b0 + t + 1))
                        act.activation(dst[t], tmp[t % 2], ACT.Copy).then_inc(c.rn_hi.sem, 1)

            def post_norm(c, l, r, a, y_k):
                act.activation(g(F_AT), bank[0][:, :], ACT.Copy).then_inc(c.y0.sem, 1)
                act.wait_ge(c.y0.sem, c.y0.at(l, y_k))
                norm(c, l, r, a, None, [g(F_AT)] + [bank[t][:, :] for t in range(1, KT)], lambda t: None, bank[0][:, :], D)

            def item(c, l, j, lo, n, block1):
                its = items[0 if block1 else 1]
                if lo <= j < n:
                    it = its[j]
                    st = stat[:, j % 4, :]
                    act.wait_ge(c.maxed.sem, c.maxed.at(l, j + 1))
                    if j - lo >= 2:
                        act.wait_ge(c.turned.sem, c.turned.at(l, j - 1))
                    m = it["n"]
                    src = g(A_SB + S * (j % 2), m) if block1 else bank[S_B[j % 2]][:, 0:m]
                    scale = 1.0 if block1 else MLA_SCALE if it["branch"] == "mla" else HEAD_SCALE
                    act.activation(g(A_P + S * (j % 2), m), src, ACT.Exp, bias=st[:, 0:1], scale=scale, accum_out=st[:, 1:2]).then_inc(c.exped.sem, 1)
                if lo <= j - 1 < n:
                    k, it = j - 1, its[j - 1]
                    act.wait_ge(c.turned.sem, c.turned.at(l, k + 1))
                    if k - lo >= 2:
                        act.wait_ge(c.pv.sem, c.pv.at(l, k - 1))
                    if it["n"] == 32:
                        act.activation(g(A_PT + S * (k % 2), P, (0, 32)), bank[T_B[k % 2]][0:32, 0:P], ACT.Copy).then_inc(c.pt.sem, 1)
                    else:
                        act.activation(g(A_PT + S * (k % 2), it["n"]), bank[T_B[k % 2]][:, 0:it["n"]], ACT.Copy).then_inc(c.pt.sem, 1)
                if lo <= j - 2 < n:
                    it = its[j - 2]
                    if it["i"] == QT - 1 and it["last"]:
                        act.wait_ge(c.pv.sem, c.pv.at(l, j - 1))
                        head_out(c, l, it["h"], it["h"] // 2 + (3 if it["branch"] == "cmp" else 0))

            def head_out(c, l, h, tile):
                act.activation(g(MIX + S * tile, S, half(h % 2)), bank[O_B[h % 2]][HD * (h % 2):HD * (h % 2) + HD, :],
                               ACT.Copy).then_inc(c.o_done.sem, 1)

            def group(c, b, l, gr):
                if gr.get("starts") and gr["unit"] + LOOK < b["n"]:
                    hi(c, b, l, gr["unit"] + LOOK)
                kind, bk = gr["kind"], bank[gr["bank"]]
                evac = c.evac(gr).sem
                if kind == "cmp":
                    k = 4 * gr["kv"] + gr["u"]
                    act.wait_ge(c.px.sem, c.px.at(l, k + 1))
                    if k >= 2:
                        act.wait_ge(c.group_done.sem, c.group_done.at(l, b["groups"][f"c{(k - 2) // 4}{(k - 2) % 4}"]["done"]))
                    else:
                        act.wait_ge(c.group_done.sem, c.group_done.at(l, b["groups"]["mv3"]["done"]))
                    act.activation(fshi[:, k % 2, :], g(M_POSX), ACT.Copy).then_inc(c.px_hi.sem, 1)
                if kind == "cvar" or kind == "rvar":
                    tiles = [A_SG, A_SG + S] if kind == "cvar" else [A_RQ + S * gr["t"]]
                    to = [A_Y, A_Y + S] if kind == "cvar" else [A_RK + S * gr["t"]]
                    act.wait_ge(c.evac(b["groups"]["cm" if kind == "cvar" else f"lm{gr['t']}"]).sem, c.emptied(l, b["groups"]["cm" if kind == "cvar" else f"lm{gr['t']}"]))
                    for s_, d_ in zip(tiles, to):
                        act.activation(g(d_), g(s_), ACT.Square).then_inc(c.ln_sq.sem, 1)
                    act.wait_ge(c.group_done.sem, c.group_done.at(l, gr["done"]))
                    act.activation(g(to[0]), bk[:, :], ACT.Ln, scale=1.0 / CONV if kind == "cvar" else 1.0, bias=eps[:, 0:1]).then_inc(evac, 1)
                    act.wait_ge(c.evac(gr).sem, c.emptied(l, gr))
                    act.activation(g(to[0]), g(to[0]), ACT.Exp, scale=-0.5).then_inc(c.ln_rstd.sem, 1)
                    if kind == "cvar":
                        for t in range(2):
                            act.wait_ge(c.cv_out.sem, c.cv_out.at(l, t + 1))
                            act.activation(g(MIX + S * (3 + t)), g(A_SG + S * t), ACT.Silu, scale=prm[:, P1_LG + t:P1_LG + t + 1],
                                                  bias=prm[:, P1_LB + t:P1_LB + t + 1]).then_inc(c.act_step.next(), 1)
                        act.preload_act_table_set(LN_SET)
                    return
                if gr["frees"] != "act" or not gr.get("evac", True):
                    if kind == "gates":
                        act.wait_ge(c.evac(gr).sem, c.emptied(l, gr))
                        act.activation(g(M_GATE, 72), g(M_GATE, 72), ACT.Sigmoid).then_inc(c.gate.sem, 1)
                        act.preload_act_table_set(LN_SET)
                    return
                act.wait_ge(c.group_done.sem, c.group_done.at(l, gr["done"]))
                if kind in ("fm", "uq", "ukv_k"):
                    r = gr.get("rows", (0, P))
                    if gr.get("overlay"):
                        act.wait_ge(c.pv.sem, c.pv.at(l, 24))
                    act.activation(g(gr["dst"], S, r), bk[r[0]:r[1], :], act_func(gr.get("func"))).then_inc(evac, 1)
                    if gr.get("func"):
                        act.preload_act_table_set(LN_SET)
                elif kind == "tm":
                    act.activation(tokens(gr), bk[:, :].rearrange("p (t n) -> p t n", t=QT), ACT.Copy).then_inc(evac, 1)
                elif kind == "ukv_v":
                    act.activation(g(gr["dst"], 384), bk[:, 0:384], ACT.Copy).then_inc(evac, 1)
                elif kind == "cmp":
                    act.activation(g(M_HID + 64 * gr["kv"], 64), bk[:, 0:64], ACT.Gelu_apprx_tanh).then_inc(evac, 1)
                    act.preload_act_table_set(LN_SET)
                elif kind == "w2":
                    if gr["kv"] == 0:
                        act.activation(g(M_KC, 32), bk[:, 0:32], ACT.Copy).then_inc(evac, 1)
                    else:
                        act.activation(g(M_VC, P, (0, 32)), bk[0:32, 0:P], ACT.Copy).then_inc(evac, 1)

            def act_func(name):
                return {None: ACT.Copy, "Sigmoid": ACT.Sigmoid, "Silu": ACT.Silu}[name]

            def tokens(gr):
                return g(gr["dst"], QT * gr["pitch"]).rearrange("p (t n) -> p t n", t=QT)[:, :, gr["off"]:gr["off"] + P]

            def down(c, b, l, n0, f0, nt, fsem):
                def one(j, i=None):
                    t, more = j, 0 if i is None else i * 4
                    f_hi(t + 1, more, i)
                    if n0 + t + LOOK < b["n"]:
                        hi(c, b, l, n0 + t + LOOK, i)

                def f_hi(t, more, i):
                    if t >= nt and i is None:
                        return
                    act.wait_ge(fsem.sem, fsem.at(l, f0 + t + 1 + more))
                    if t >= 2 or i is not None:
                        act.wait_ge(c.group_done.sem, c.group_done.at(l, b["last_of"][n0] + t - 2 + more))
                    else:
                        act.wait_ge(c.group_done.sem, c.group_done.at(l, b["last_of"][n0 - 1]))
                    act.activation(fshi[:, t % 2, :], f_tile(t + more), ACT.Copy).then_inc(c.f_hi.sem, 1)
                f_hi(0, 0, None)
                for j in range(4):
                    one(j)
                with act.Fori(1, (nt - 4) // 4 if nt % 4 == 0 else nt // 4) as i:
                    for j in range(4):
                        one(j, i)
                for j in range((nt - 4) if nt % 4 == 0 else nt // 4 * 4, nt):
                    one(j)

            act.preload_act_table_set(LN_SET)
            for k in range(KT):
                act.wait_ge(tin, k + 1)
                act.activation(x[:, k, :], bank[k % 2][:, :], ACT.Copy).then_inc(counts_of(0).x_ready.sem, 1)
            act.sem_inc(counts_of(0).relu.sem, 4)
            act.sem_inc(counts_of(1).silu.sem, 2)

            c, b = counts_of(0), b1
            x_tiles = [x[:, t, :] for t in range(KT)]
            h_tiles = [hh[:, t, :] for t in range(KT)]
            with act.Fori(0, LAYERS) as l:
                act.preload_act_table_set(LN_SET)
                for n in range(LOOK):
                    hi(c, b, l, n)
                norm(c, l, 0, 0, 0, x_tiles, lambda t: act.wait_ge(c.x_ready.sem, c.x_ready.at(l, 0)) if t == 0 else None, bank[0][:, :], D, h_tiles)
                act.wait_ge(c.prm_in.sem, c.prm_in.at(l, 9))
                for s in b["steps"]:
                    if s[0] == "g":
                        group(c, b, l, b["groups"][s[1]])
                    elif s[0] == "i":
                        item(c, l, s[1], 0, n1, True)
                    elif s[0] == "r_out":
                        for h in (2 * s[1], 2 * s[1] + 1):
                            act.wait_ge(c.r_pv.sem, c.r_pv.at(l, 4 * h + 4))
                            act.activation(g(A_RQ + S * s[1], S, half(h % 2)), bank[O_B[h % 2]][HD * (h % 2):HD * (h % 2) + HD, :],
                                           ACT.Copy).then_inc(c.o_done.sem, 1)
                act.wait_ge(c.o_done.sem, c.o_done.at(l, 6))
                act.wait_ge(c.act_step.sem, c.act_step.now(l))
                for k in range(KT):
                    if k >= 5:
                        act.wait_ge(c.ret_out.sem, c.ret_out.at(l, k - 4))
                    act.activation(hh[:, k, :], g(MIX + S * k), ACT.Copy).then_inc(c.mix_hi.sem, 1)
                for m in range(KT):
                    hi(c, b, l, b["wo"] + m + LOOK)
                act.wait_ge(c.group_done.sem, c.group_done.at(l, b["last_of"][b["wo"] + KT - 1]))
                post_norm(c, l, 1, 8, 1)
                norm(c, l, 2, 16, 8, x_tiles, lambda t: act.wait_ge(c.x_ready.sem, c.x_ready.at(l, t + 1)), bank[0][:, :], D, h_tiles)
                n0 = b["wo"] + KT
                with act.Fori(0, T1 // 4) as i:
                    for j in range(4):
                        hi(c, b, l, n0 + j + LOOK, i)
                        act.wait_ge(c.group_done.sem, c.group_done.at(l, b["last_of"][n0] + j + i * 4))
                        act.wait_ge(c.f_done.sem, c.f_done.at(l, j - 1 + i * 4))
                        act.activation(rt[j % 2], bank[j][:, :], ACT.Relu).then_inc(c.relu.sem, 1)
                n0 += T1
                down(c, b, l, n0, 0, T1, c.f_done)
                act.wait_ge(c.group_done.sem, c.group_done.at(l, b["last_of"][b["n"] - 1]))
                post_norm(c, l, 3, 24, 2)
            c.act_step.check()

            c, b = counts_of(1), b2

            def mlp(l, n0, f0, h0):
                with act.Fori(0, T2 // 2) as i:
                    for j in range(4):
                        hi(c, b, l, n0 + j + LOOK, i)
                        if j % 2 == 0:
                            t = j // 2
                            act.wait_ge(c.group_done.sem, c.group_done.at(l, b["last_of"][n0] + j + i * 4))
                            act.wait_ge(c.f2_done.sem, c.f2_done.at(l, f0 + t - 1 + i * 2))
                            act.activation(rt[t], bank[j][:, :], ACT.Silu).then_inc(c.silu.sem, 1)
                act.preload_act_table_set(LN_SET)
                down(c, b, l, n0 + 2 * T2, f0, T2, c.f2_done)

            with act.Fori(0, LAYERS) as l:
                act.preload_act_table_set(LN_SET)
                for n in range(LOOK):
                    hi(c, b, l, n)
                norm(c, l, 0, 0, 0, x_tiles, lambda t: act.wait_ge(c.x_ready.sem, c.x_ready.at(l, 0)) if t == 0 else None, bank[0][:, :], D, h_tiles)
                mlp(l, 0, 0, 0)
                norm(c, l, 1, 8, 8, x_tiles, lambda t: act.wait_ge(c.x_ready.sem, c.x_ready.at(l, t + 1)), bank[0][:, :], D, h_tiles)
                for s in b["steps"]:
                    if s[0] == "g":
                        group(c, b, l, b["groups"][s[1]])
                    elif s[0] == "rn" and s[1] == "cq":
                        norm(c, l, 2, 16, 16, [g(M_V), g(M_V + S)], lambda t: act.wait_ge(c.evac(b["groups"][f"cq{t}"]).sem, c.emptied(l, b["groups"][f"cq{t}"])),
                             bank[2][:, :], 256, [fshi[:, 0, :], fshi[:, 1, :]])
                    elif s[0] == "rn":
                        norm(c, l, 3, 18, 18, [g(M_V + 2 * S)], lambda t: act.wait_ge(c.evac(b["groups"]["ckv"]).sem, c.emptied(l, b["groups"]["ckv"])),
                             bank[2][:, :], 128, [fshi[:, 2, :]])
                    elif s[0] == "i":
                        item(c, l, s[1], s[2], s[3], False)
                    elif s[0] == "z":
                        h, jt = s[1:]
                        zi, n = 4 * h + 3 - jt, S - P * jt
                        t_ = g(A_P + S * (zi % 2), n)
                        act.wait_ge(c.z.sem, c.z.at(l, zi + 1))
                        act.activation(t_, bank[S_B[zi % 2]][:, 0:n], ACT.Abs, scale=HEAD_SCALE).then_inc(c.act_step.next(), 1)
                        act.wait_ge(c.act_step.sem, c.act_step.now(l))
                        act.activation(t_, t_, ACT.Exp, scale=-1.0).then_inc(c.act_step.next(), 1)
                        act.wait_ge(c.act_step.sem, c.act_step.now(l))
                        act.activation(t_, t_, ACT.Ln, bias=1.0).then_inc(c.z_ln.sem, 1)
                    elif s[0] == "suf":
                        h, jt = s[1:]
                        zi, n, at = 4 * h + 3 - jt, S - P * jt, SB_AT[jt]
                        act.wait_ge(c.suf_t.sem, c.suf_t.at(l, zi + 1))
                        act.activation(g(B_LB + at, n), g(B_LB + at, n), ACT.Exp).then_inc(c.suf_a.sem, 1)
                    elif s[0] == "sbo":
                        act.wait_ge(c.sb_pv.sem, c.sb_pv.at(l, s[1] + 1))
                        head_out(c, l, s[1], 6 + s[1] // 2)
                act.wait_ge(c.o_done.sem, c.o_done.at(l, 16))
                for k in range(KT):
                    act.activation(hh[:, k, :], g(MIX + S * k), ACT.Copy).then_inc(c.mix_hi.sem, 1)
                for m in range(KT):
                    hi(c, b, l, b["wo"] + m + LOOK)
                norm(c, l, 4, 19, 19, x_tiles, lambda t: act.wait_ge(c.x_ready.sem, c.x_ready.at(l, 9 + t)), bank[0][:, :], D, h_tiles)
                mlp(l, b["wo"] + KT, T2, 0)
            c.act_step.check()

            last = counts_of(1)
            for t in range(KT):
                act.wait_ge(last.x_ready.sem, last.x_ready.at(2, 0))
                if t >= 2:
                    act.wait_ge(last.rn_used.sem, last.rn_used.at(2, t - 1))
                act.activation(sq[t % 2], x_tiles[t], ACT.Square).then_inc(last.rn_sq.sem, 1)
            act.wait_ge(last.rn_used.sem, last.rn_used.at(2, KT))
            act.activation(rstd, bank[0][:, :], ACT.Ln, scale=1.0 / D, bias=eps[:, 0:1]).then_inc(fin, 1)
            act.wait_ge(fin, 1)
            act.activation(rstd, rstd, ACT.Exp, scale=-0.5).then_inc(last.rn_rstd.sem, 1)
            for n in range(2 * QT):
                act.wait_ge(tout, n + 1)
                if n == 0:
                    act.wait_ge(fin, 1 + KT)
                act.activation(g(OUT_AT + S * n), bank[2 + n % 4][:, :], ACT.Copy).then_inc(fin_ev, 1)

        @block.vector
        def _(dve):
            def lo(c, b, l, n, i=None):
                s, m = n % RING, b["size"][n]
                dve.wait_ge(c.hi_done.sem, c.hi_done.at(l, n + 1 + (0 if i is None else i * 4)))
                dve.tensor_tensor(slot3(wlo, s, m), slot3(raw, s, m), slot3(whi, s, m).bitcast(F32), ALU.subtract).then_inc(c.lo_done.sem, 1)

            def norm(c, l, r, b0, src, gains, hi_tiles, lo_tiles):
                dve.wait_ge(c.rn_rstd.sem, c.rn_rstd.at(l, r))
                if b0:
                    dve.wait_ge(c.rn_lo.sem, c.rn_lo.at(l, b0))
                n = len(src)
                for t in range(n + 1):
                    if t < n:
                        if t >= 2:
                            dve.wait_ge(c.rn_lo.sem, c.rn_lo.at(l, b0 + t - 1))
                        dve.scalar_tensor_tensor(out=tmp[t % 2], in0=src[t], scalar=gains[:, t:t + 1], in1=rstd, op0=ALU.mult,
                                                 op1=ALU.mult).then_inc(c.rn_tmp.sem, 1)
                    if t >= 1:
                        dve.wait_ge(c.rn_hi.sem, c.rn_hi.at(l, b0 + t))
                        dve.tensor_tensor(lo_tiles[t - 1], tmp[(t - 1) % 2], hi_tiles[t - 1].bitcast(F32), ALU.subtract).then_inc(c.rn_lo.sem, 1)

            def post_norm(c, l, r, gains):
                dve.wait_ge(c.rn_rstd.sem, c.rn_rstd.at(l, r))
                for t in range(KT):
                    y = g(F_AT) if t == 0 else bank[t][:, :]
                    dve.scalar_tensor_tensor(out=tmp[t % 2], in0=y, scalar=gains[:, t:t + 1], in1=rstd, op0=ALU.mult, op1=ALU.mult).then_inc(c.dve_step.next(), 1)
                    dve.wait_ge(c.dve_step.sem, c.dve_step.now(l))
                    dve.tensor_tensor(x[:, t, :], x[:, t, :], tmp[t % 2], ALU.add).then_inc(c.x_ready.sem, 1)

            def item(c, l, j, lo_, n, block1):
                its = items[0 if block1 else 1]
                if lo_ <= j < n:
                    it, m, st = its[j], its[j]["n"], stat[:, j % 4, :]
                    bk = bank[S_B[j % 2]]
                    dve.wait_ge(c.qk.sem, c.qk.at(l, j + 1))
                    if block1:
                        if it["i"] == 0:
                            dve.wait_ge(c.h_in[it["h"] % 2].sem, c.h_in[it["h"] % 2].at(l, it["h"] // 2 + 1))
                        if j >= 2:
                            dve.wait_ge(c.exped.sem, c.exped.at(l, j - 1))
                        s_ = g(A_SB + S * (j % 2), m)
                        h_ = A_H + S * (it["h"] % 2)
                        table = G[:, h_ + m - 1:(h_ - 1 if h_ else None):-1]
                        dve.scalar_tensor_tensor(out=s_, in0=bk[:, 0:m], scalar=HEAD_SCALE, in1=table, op0=ALU.mult, op1=ALU.add).then_inc(c.biased.sem, 1)
                        dve.wait_ge(c.biased.sem, c.biased.at(l, j + 1))
                        dve.tensor_reduce(st[:, 0:1], s_, AXX, ALU.max, negate=True).then_inc(c.maxed.sem, 1)
                    else:
                        dve.tensor_reduce(st[:, 3:4], bk[:, 0:m], AXX, ALU.max, negate=True).then_inc(c.dve_step.next(), 1)
                        dve.wait_ge(c.dve_step.sem, c.dve_step.now(l))
                        scale = MLA_SCALE if it["branch"] == "mla" else HEAD_SCALE
                        dve.tensor_scalar(st[:, 0:1], st[:, 3:4], scale, None, ALU.mult).then_inc(c.maxed.sem, 1)
                if lo_ <= j - 1 < n:
                    k = j - 1
                    it, st, p_ = its[k], stat[:, k % 4, :], g(A_P + S * (k % 2), its[k]["n"])
                    dve.wait_ge(c.exped.sem, c.exped.at(l, k + 1))
                    dve.reciprocal(st[:, 2:3], st[:, 1:2]).then_inc(c.dve_step.next(), 1)
                    dve.wait_ge(c.dve_step.sem, c.dve_step.now(l))
                    if it["branch"] in ("cmp", "sel", "win"):
                        gate = ("cmp", "sel", "win").index(it["branch"]) + 3 * it["h"] + 18 * it["i"]
                        if k == 24:
                            dve.wait_ge(c.gate.sem, c.gate.at(l, 1))
                        if it["branch"] == "cmp":
                            dve.tensor_tensor(st[:, 2:3], st[:, 2:3], cs(C_VALID + it["i"], n=1), ALU.mult).then_inc(c.dve_step.next(), 1)
                            dve.wait_ge(c.dve_step.sem, c.dve_step.now(l))
                        dve.tensor_scalar(p_, p_, st[:, 2:3], g(M_GATE + gate, 1), ALU.mult, ALU.mult).then_inc(c.scaled.sem, 1)
                    else:
                        dve.tensor_scalar(p_, p_, st[:, 2:3], None, ALU.mult).then_inc(c.scaled.sem, 1)

            def taps(c, l, a, z):
                for k in range(a, z):
                    for t in range(2):
                        y_, acc, wk = g(A_Y + YW * t + k), g(A_SG + S * t), prm[:, P1_CW + TAPS * t + k:P1_CW + TAPS * t + k + 1]
                        if k == 0:
                            if t == 0:
                                dve.wait_ge(c.dve_step.sem, c.dve_step.now(l))
                                for u in range(2):
                                    dve.wait_ge(c.evac(b1["groups"][f"ca{u}"]).sem, c.emptied(l, b1["groups"][f"ca{u}"]))
                            dve.tensor_scalar(acc, y_, wk, prm[:, P1_CB + t:P1_CB + t + 1], ALU.mult, ALU.add).then_inc(c.dve_step.next(), 1)
                            continue
                        dve.wait_ge(c.dve_step.sem, c.dve_step.at(l, tap_at[t]))
                        ins = dve.scalar_tensor_tensor(out=acc, in0=y_, scalar=wk, in1=acc, op0=ALU.mult, op1=ALU.add)
                        if k == TAPS - 1 and t == 1:
                            ins.then_inc(c.taps.sem, 1)
                        else:
                            ins.then_inc(c.dve_step.next(), 1)
                            tap_at[t] = c.dve_step.k
                    if k == 0:
                        tap_at[0], tap_at[1] = c.dve_step.k - 1, c.dve_step.k
            tap_at = [0, 0]

            def swap(c, l, gr, bk, evac):
                r = gr["rows"]
                tile, t0 = g(gr["tile"], S, r), gr["tab"]
                swapped = bk[r[0]:r[1], :]
                dve.tensor_tensor(swapped, swapped, tab[r[0]:r[1], (t0 + S):(t0 + 2 * S)], ALU.mult).then_inc(c.dve_step.next(), 1)
                dve.tensor_tensor(tile, tile, tab[r[0]:r[1], t0:t0 + S], ALU.mult).then_inc(c.dve_step.next(), 1)
                dve.wait_ge(c.dve_step.sem, c.dve_step.now(l))
                dve.tensor_tensor(tile, swapped, tile, ALU.add).then_inc(evac, 1)

            def group(c, b, l, gr):
                if gr.get("starts") and gr["unit"] + LOOK < b["n"]:
                    lo(c, b, l, gr["unit"] + LOOK)
                kind, bk = gr["kind"], bank[gr["bank"]]
                evac = c.evac(gr).sem
                if kind == "cmp":
                    k, u = 4 * gr["kv"] + gr["u"], gr["u"]
                    if k == 0:
                        dve.wait_ge(c.prm_in.sem, c.prm_in.at(l, 12))
                        dve.memset(g(M_POSX), 0.0).then_inc(c.dve_step.next(), 1)
                        dve.wait_ge(c.dve_step.sem, c.dve_step.now(l))
                    dve.wait_ge(c.evac(b["groups"]["nvc" if gr["kv"] else "snkc"]).sem, c.emptied(l, b["groups"]["nvc" if gr["kv"] else "snkc"]))
                    if k:
                        dve.wait_ge(c.px_lo.sem, c.px_lo.at(l, k))
                    src, pos = (N_VC, P2_PV) if gr["kv"] else (N_KC, P2_PK)
                    for j in range(2):
                        r = half(j)
                        dst = g(M_POSX, S, r).rearrange("p (t n) -> p t n", t=8)[:, :, 32 * j:32 * j + CMP_N]
                        tok = G[r[0]:r[1], src + 8 * u:src + 8 * u + 16 * CMP_N].rearrange("p (n t) -> p t n", t=16)[:, 0:8, :]
                        pe_ = prm[r[0]:r[1], pos + 8 * u:pos + 8 * u + 8].unsqueeze(2).to_broadcast([HD, 8, CMP_N])
                        ins = dve.tensor_tensor(dst, tok, pe_, ALU.add)
                        if j == 0:
                            ins.then_inc(c.dve_step.next(), 1)
                            dve.wait_ge(c.dve_step.sem, c.dve_step.now(l))
                        else:
                            ins.then_inc(c.px.sem, 1)
                    dve.wait_ge(c.px_hi.sem, c.px_hi.at(l, k + 1))
                    dve.tensor_tensor(fslo[:, k % 2, :], g(M_POSX), fshi[:, k % 2, :].bitcast(F32), ALU.subtract).then_inc(c.px_lo.sem, 1)
                    return
                if kind == "ukv_k":
                    if gr["name"] == "mk0":
                        dve.wait_ge(c.evac(b["groups"]["spe"]).sem, c.emptied(l, b["groups"]["spe"]))
                    dve.tensor_copy(g(M_K + S * gr["j"], S, (64, 96)), g(M_PE, S, (64, 96))).then_inc(c.kpe.sem, 1)
                if kind == "cvar":
                    dve.wait_ge(c.ln_rstd.sem, c.ln_rstd.at(l, 1))
                    for t in range(2):
                        dve.tensor_tensor(g(A_SG + S * t), g(A_SG + S * t), g(A_Y), ALU.mult).then_inc(c.cv_out.sem, 1)
                if kind == "rvar":
                    t = gr["t"]
                    dve.wait_ge(c.ln_rstd.sem, c.ln_rstd.at(l, 2 + t))
                    dve.tensor_tensor(g(A_RQ + S * t), g(A_RQ + S * t), g(A_RK + S * t), ALU.mult).then_inc(c.dve_step.next(), 1)
                    dve.wait_ge(c.dve_step.sem, c.dve_step.now(l))
                    dve.wait_ge(c.evac(b["groups"][f"rg{t}"]).sem, c.emptied(l, b["groups"][f"rg{t}"]))
                    dve.tensor_tensor(g(MIX + S * (5 + t)), g(MIX + S * (5 + t)), g(A_RQ + S * t), ALU.mult).then_inc(c.ret_out.sem, 1)
                if gr["frees"] != "dve" or not gr.get("evac", True):
                    return
                dve.wait_ge(c.group_done.sem, c.group_done.at(l, gr["done"]))
                if kind == "swap":
                    swap(c, l, gr, bk, evac)
                elif kind == "gates":
                    for t in range(QT):
                        ins = dve.tensor_tensor(g(M_GATE + 18 * t, 18), bk[:, P * t:P * t + 18], prm[:, P2_GB:P2_GB + 18], ALU.add)
                        if t < QT - 1:
                            ins.then_inc(c.dve_step.next(), 1)
                    ins.then_inc(evac, 1)
                elif kind == "cmean":
                    for t in range(2):
                        ins = dve.scalar_tensor_tensor(out=g(A_SG + S * t), in0=bk[:, :], scalar=-1.0 / CONV, in1=g(A_SG + S * t), op0=ALU.mult, op1=ALU.add)
                        if t == 0:
                            ins.then_inc(c.dve_step.next(), 1)
                    ins.then_inc(evac, 1)
                elif kind == "rmean":
                    tile = g(A_RQ + S * gr["t"])
                    dve.tensor_tensor(tile, tile, bk[:, :], ALU.subtract).then_inc(evac, 1)
                elif "glu" in gr:
                    t = gr["glu"]
                    dve.wait_ge(c.evac(b["groups"][f"cg{t}"]).sem, c.emptied(l, b["groups"][f"cg{t}"]))
                    dve.memset(g(A_Y + YW * t, TAPS - 1), 0.0).then_inc(c.dve_step.next(), 1)
                    dve.tensor_tensor(g(A_Y + YW * t + TAPS - 1), bk[:, :], g(A_SG + S * t), ALU.mult).then_inc(evac, 1)
                elif kind == "tm":
                    dve.tensor_copy(tokens(gr), bk[:, :].rearrange("p (t n) -> p t n", t=QT)).then_inc(evac, 1)
                elif kind == "ukv_v":
                    dve.tensor_copy(g(gr["dst"], 384), bk[:, 0:384]).then_inc(evac, 1)
                else:
                    r = gr.get("rows", (0, P))
                    dve.tensor_copy(g(gr["dst"], S, r), bk[r[0]:r[1], :]).then_inc(evac, 1)

            def tokens(gr):
                return g(gr["dst"], QT * gr["pitch"]).rearrange("p (t n) -> p t n", t=QT)[:, :, gr["off"]:gr["off"] + P]

            def down(c, b, l, n0, h0, nt):
                def f_lo(t, more, i):
                    if t >= nt and i is None:
                        return
                    dve.wait_ge(c.f_hi.sem, c.f_hi.at(l, h0 + t + 1 + more))
                    dve.tensor_tensor(fslo[:, t % 2, :], f_tile(t + more), fshi[:, t % 2, :].bitcast(F32), ALU.subtract).then_inc(c.f_lo.sem, 1)

                def one(t, i=None):
                    f_lo(t + 1, 0 if i is None else i * 4, i)
                    if n0 + t + LOOK < b["n"]:
                        lo(c, b, l, n0 + t + LOOK, i)
                f_lo(0, 0, None)
                for j in range(4):
                    one(j)
                whole = nt // 4 * 4 if nt % 4 else nt - 4
                with dve.Fori(1, whole // 4) as i:
                    for j in range(4):
                        one(j, i)
                for j in range(whole, nt):
                    one(j)

            dve.memset(eps[:, :], EPS).then_inc(bias_sem, 1)
            rows, ext = LAYERS * HEADS1, 4608
            dve.memset(G[0:rows, ext:ext + BIAS_ROW], 0.0).then_inc(rows_zero, 1)
            dve.wait_ge(rows_zero, 1)
            dve.wait_ge(scr_dma, 16)
            dve.tensor_copy(G[0:rows, ext:ext + 256], G[0:rows, 4097:4097 + 256]).then_inc(bias_sem, 1)
            dve.tensor_scalar(G[0:rows, ext + 256:ext + BIAS_ROW], G[0:rows, ext + 256:ext + BIAS_ROW], G[0:rows, 4096 + 256:4096 + 257], None,
                              ALU.add).then_inc(bias_sem, 1)
            dve.wait_ge(const_in, 48)
            dve.tensor_copy(m_sb[:, :], g(MASK_AT)).then_inc(masks_ready, 1)
            dve.sem_inc(counts_of(0).lo_done.sem, RING)
            dve.sem_inc(counts_of(0).f_done.sem, 2)
            dve.sem_inc(counts_of(1).f2_done.sem, 2)

            x_tiles = [x[:, t, :] for t in range(KT)]
            hi_tiles, lo_tiles = [hh[:, t, :] for t in range(KT)], [hl[:, t, :] for t in range(KT)]
            c, b = counts_of(0), b1
            with dve.Fori(0, LAYERS) as l:
                for n in range(LOOK):
                    lo(c, b, l, n)
                dve.wait_ge(c.prm_in.sem, c.prm_in.at(l, 9))
                norm(c, l, 1, 0, x_tiles, prm[:, P1_MIX:P1_MIX + KT], hi_tiles, lo_tiles)
                for s in b["steps"]:
                    if s[0] == "g":
                        group(c, b, l, b["groups"][s[1]])
                    elif s[0] == "i":
                        item(c, l, s[1], 0, n1, True)
                    elif s[0] == "taps":
                        taps(c, l, s[1], s[2])
                    elif s[0] == "r":
                        j = s[1]
                        h, n = j // 4, S - P * (j % 4)
                        dve.wait_ge(c.r_s.sem, c.r_s.at(l, j + 1))
                        if j >= 2:
                            dve.wait_ge(c.r_pv.sem, c.r_pv.at(l, j - 1))
                        dve.tensor_tensor(g(A_P + S * (j % 2), n), bank[S_B[j % 2]][:, 0:n], tab[:, S * h:S * h + n], ALU.mult).then_inc(c.r_dec.sem, 1)
                for k in range(KT):
                    dve.wait_ge(c.mix_hi.sem, c.mix_hi.at(l, k + 1))
                    dve.tensor_tensor(lo_tiles[k], g(MIX + S * k), hi_tiles[k].bitcast(F32), ALU.subtract).then_inc(c.mix_lo.sem, 1)
                for m in range(KT):
                    lo(c, b, l, b["wo"] + m + LOOK)
                post_norm(c, l, 2, prm[:, P1_POST:P1_POST + KT])
                norm(c, l, 3, 8, x_tiles, prm[:, P1_MLP:P1_MLP + KT], hi_tiles, lo_tiles)
                n0 = b["wo"] + KT
                with dve.Fori(0, T1 // 4) as i:
                    for j in range(4):
                        lo(c, b, l, n0 + j + LOOK, i)
                        dve.wait_ge(c.relu.sem, c.relu.at(l, j + 1 + i * 4))
                        dve.tensor_tensor(f_tile(i * 4 + j), rt[j % 2], rt[j % 2], ALU.mult).then_inc(c.f_done.sem, 1)
                down(c, b, l, n0 + T1, 0, T1)
                post_norm(c, l, 4, prm[:, P1_MPOST:P1_MPOST + KT])
            c.dve_step.check()

            c, b = counts_of(1), b2

            def mlp(l, n0, f0, x0):
                with dve.Fori(0, T2 // 2) as i:
                    for j in range(4):
                        lo(c, b, l, n0 + j + LOOK, i)
                        if j % 2:
                            t = j // 2
                            dve.wait_ge(c.group_done.sem, c.group_done.at(l, b["last_of"][n0] + j + i * 4))
                            dve.wait_ge(c.silu.sem, c.silu.at(l, f0 + t + 1 + i * 2))
                            dve.tensor_tensor(f_tile(i * 2 + t), bank[j][:, :], rt[t], ALU.mult).then_inc(c.f2_done.sem, 1)
                down(c, b, l, n0 + 2 * T2, f0, T2)
                dve.wait_ge(c.group_done.sem, c.group_done.at(l, b["last_of"][n0 + 3 * T2 - 1]))
                for t in range(KT):
                    dve.scalar_tensor_tensor(out=x[:, t, :], in0=bank[t][:, :], scalar=0.5, in1=x[:, t, :], op0=ALU.mult, op1=ALU.add).then_inc(c.x_ready.sem, 1)

            dve.wait_ge(tab_in, 16)
            with dve.Fori(0, LAYERS) as l:
                for n in range(LOOK):
                    lo(c, b, l, n)
                dve.wait_ge(c.prm_in.sem, c.prm_in.at(l, 12))
                norm(c, l, 1, 0, x_tiles, prm[:, P2_F1:P2_F1 + KT], hi_tiles, lo_tiles)
                mlp(l, 0, 0, 0)
                norm(c, l, 2, 8, x_tiles, prm[:, P2_MIX:P2_MIX + KT], hi_tiles, lo_tiles)
                for s in b["steps"]:
                    if s[0] == "g":
                        group(c, b, l, b["groups"][s[1]])
                    elif s[0] == "rn" and s[1] == "cq":
                        norm(c, l, 3, 16, [g(M_V), g(M_V + S)], prm[:, P2_QN:P2_QN + 2], [fshi[:, 0, :], fshi[:, 1, :]], [fslo[:, 0, :], fslo[:, 1, :]])
                    elif s[0] == "rn":
                        norm(c, l, 4, 18, [g(M_V + 2 * S)], prm[:, P2_KVN:P2_KVN + 1], [fshi[:, 2, :]], [fslo[:, 2, :]])
                    elif s[0] == "i":
                        item(c, l, s[1], s[2], s[3], False)
                    elif s[0] == "z":
                        h, jt = s[1:]
                        zi, n, at = 4 * h + 3 - jt, S - P * jt, SB_AT[jt]
                        bk, lb, lr = bank[S_B[zi % 2]][:, 0:n], g(B_LB + at, n), g(B_LR + at, n)
                        dve.wait_ge(c.z.sem, c.z.at(l, zi + 1))
                        if jt == 3:
                            dve.wait_ge(c.pv.sem, c.pv.at(l, 24))
                            if h:
                                dve.wait_ge(c.sb_pv.sem, c.sb_pv.at(l, h))
                        dve.wait_ge(c.z_ln.sem, c.z_ln.at(l, zi + 1))
                        dve.tensor_scalar(lb, bk, HEAD_SCALE, 0.0, ALU.mult, ALU.min).then_inc(c.dve_step.next(), 1)
                        dve.tensor_scalar(lr, bk, -HEAD_SCALE, 0.0, ALU.mult, ALU.min).then_inc(c.dve_step.next(), 1)
                        dve.wait_ge(c.dve_step.sem, c.dve_step.now(l))
                        t_ = g(A_P + S * (zi % 2), n)
                        dve.tensor_tensor(lb, lb, t_, ALU.subtract).then_inc(c.dve_step.next(), 1)
                        dve.tensor_tensor(lr, lr, t_, ALU.subtract).then_inc(c.dve_step.next(), 1)
                        dve.wait_ge(c.dve_step.sem, c.dve_step.now(l))
                        dve.tensor_tensor(lr[:, 0:P], lr[:, 0:P], strict, ALU.mult).then_inc(c.z_lr.sem, 1)
                    elif s[0] == "suf":
                        h, jt = s[1:]
                        zi, n, at = 4 * h + 3 - jt, S - P * jt, SB_AT[jt]
                        lb = g(B_LB + at, n)
                        dve.wait_ge(c.suf.sem, c.suf.at(l, zi + 1))
                        dve.tensor_tensor(lb, lb, bank[T_B[zi % 2]][:, 0:n], ALU.add).then_inc(c.suf_t.sem, 1)
                        dve.wait_ge(c.suf_a.sem, c.suf_a.at(l, zi + 1))
                        dve.tensor_tensor(lb[:, 0:P], lb[:, 0:P], strict, ALU.mult).then_inc(c.suf_m.sem, 1)
                for k in range(KT):
                    dve.wait_ge(c.mix_hi.sem, c.mix_hi.at(l, k + 1))
                    dve.tensor_tensor(lo_tiles[k], g(MIX + S * k), hi_tiles[k].bitcast(F32), ALU.subtract).then_inc(c.mix_lo.sem, 1)
                for m in range(KT):
                    lo(c, b, l, b["wo"] + m + LOOK)
                dve.wait_ge(c.group_done.sem, c.group_done.at(l, b["last_of"][b["wo"] + KT - 1]))
                for t in range(KT):
                    dve.tensor_tensor(x[:, t, :], bank[t][:, :], x[:, t, :], ALU.add).then_inc(c.x_ready.sem, 1)
                norm(c, l, 5, 19, x_tiles, prm[:, P2_F2:P2_F2 + KT], hi_tiles, lo_tiles)
                mlp(l, b["wo"] + KT, T2, 16)
            c.dve_step.check()
            dve.wait_ge(c.rn_rstd.sem, c.rn_rstd.at(2, 1))
            dve.wait_ge(gain_in, 16)
            for t in range(KT):
                dve.scalar_tensor_tensor(out=x_tiles[t], in0=x_tiles[t], scalar=fin_g[:, t:t + 1], in1=rstd, op0=ALU.mult, op1=ALU.mult).then_inc(fin, 1)

        @block.tensor
        def _(pe):
            def mm3(o, wh, wl, ah, al, start, stop):
                pe.matmul(o, wh, ah, start=start, stop=False)
                pe.matmul(o, wh, al, start=False, stop=False)
                return pe.matmul(o, wl, ah, start=False, stop=stop)

            def cols(t, s, k, j=0, n=P, pitch=P):
                return t[:, s, k * pitch + j:k * pitch + j + n]

            def norm(c, l, a, n, bk, d=False):
                for t in range(n):
                    pe.wait_ge(c.rn_sq.sem, c.rn_sq.at(l, a + t + 1))
                    pe.matmul(bk, ones, sq[t % 2], start=t == 0, stop=t == n - 1).then_inc(c.rn_used.sem, 1)

            def need(c, b, l, *names):
                for bk in range(2):
                    late = [b["groups"][n] for n in names if b["groups"][n]["bank"] == bk]
                    if late:
                        pe.wait_ge(c.evac(max(late, key=lambda gr: gr["e"])).sem, c.emptied(l, max(late, key=lambda gr: gr["e"])))

            def item(c, b, l, j, lo_, n, block1):
                its = items[0 if block1 else 1]
                if lo_ <= j < n:
                    it = its[j]
                    h, i, m, br = it["h"], it["i"], it["n"], it["branch"]
                    bk, q = bank[S_B[j % 2]], P * i
                    if br is None:
                        if i == 0:
                            need(c, b, l, f"q{h // 2}", f"k{h // 2}", f"v{h // 2}")
                        r = half(h % 2)
                        lhs, rhs = g(A_Q + S * (h // 2) + q, P, r), g(A_K + S * (h // 2), m, r)
                    elif br == "mla":
                        if j == 0:
                            need(c, b, l, "sm4", "sm5", "mk4", "mk5", "mv2", "mv3")
                        if i == 0:
                            pe.wait_ge(c.kpe.sem, c.kpe.at(l, h + 1))
                        r = (0, MLA_D)
                        lhs, rhs = g(M_Q + S * h + q, P, r), g(M_K + S * h, m, r)
                    else:
                        if j == 24:
                            need(c, b, l, "snq2", "snks", "snkw", "nvs", "nvw", "w20", "w21")
                            pe.wait_ge(c.z_lr.sem, c.z_lr.at(l, 16))
                            pe.wait_ge(c.suf_t.sem, c.suf_t.at(l, 16))
                        r = half(h // 3)
                        lhs = g(N_Q + S * (h % 3) + q, P, r)
                        rhs = g({"sel": N_KS, "win": N_KW, "cmp": M_KC}[br], m, r)
                    if j - lo_ >= 2:
                        free = c.biased if block1 else c.exped
                        pe.wait_ge(free.sem, free.at(l, j - 1))
                    pe.matmul(bk[:, 0:m], lhs, rhs, start=True, stop=False)
                    mask = chunked if block1 else causal
                    if br == "cmp":
                        ins = pe.matmul(bk[:, 0:32], identb, cmpmask[:, 32 * i:32 * i + 32], start=False, stop=True)
                    else:
                        ins = pe.matmul(bk[:, q:q + P], identb, mask, start=False, stop=True)
                    ins.then_inc(c.qk.sem, 1)
                if lo_ <= j - 2 < n:
                    k, it = j - 2, its[j - 2]
                    h, i, br = it["h"], it["i"], it["branch"]
                    o = bank[O_B[h % 2]][HD * (h % 2):HD * (h % 2) + HD, P * i:P * i + P]
                    pe.wait_ge(c.pt.sem, c.pt.at(l, k + 1))
                    oi = h + (10 if br in ("sel", "win", "cmp") else 0)
                    if i == 0 and it["first"] and oi >= 2:
                        pe.wait_ge(c.o_done.sem, c.o_done.at(l, oi - 1))
                    n_k = 1 if br == "cmp" else i + 1
                    for kt in range(n_k):
                        if br == "cmp":
                            v, pt = g(M_VC + HD * (h // 3), HD, (0, 32)), g(A_PT + S * (k % 2), P, (0, 32))
                        else:
                            pt = g(A_PT + S * (k % 2) + P * kt, P)
                            v = {None: lambda: g(A_V + 384 * kt + HD * h, HD), "mla": lambda: g(M_V + 384 * kt + HD * h, HD),
                                 "sel": lambda: g(N_VS + P * kt + HD * (h // 3), HD), "win": lambda: g(N_VW + P * kt + HD * (h // 3), HD)}[br]()
                        ins = pe.matmul(o, v, pt, start=it["first"] and kt == 0, stop=it["last"] and kt == n_k - 1)
                    ins.then_inc(c.pv.sem, 1)
                if lo_ <= j - 1 < n:
                    k, it = j - 1, its[j - 1]
                    pe.wait_ge(c.scaled.sem, c.scaled.at(l, k + 1))
                    if k - lo_ >= 2:
                        pe.wait_ge(c.pt.sem, c.pt.at(l, k - 1))
                    bk = bank[T_B[k % 2]]
                    if it["n"] == 32:
                        ins = pe.transpose(bk[0:32, 0:P], g(A_P + S * (k % 2), 32), ident)
                    else:
                        for kt in range(it["i"] + 1):
                            ins = pe.transpose(bk[:, P * kt:P * kt + P], g(A_P + S * (k % 2) + P * kt, P), ident)
                    ins.then_inc(c.turned.sem, 1)

            def group(c, b, l, gr):
                kind, bk, e = gr["kind"], bank[gr["bank"]], gr["e"]
                unit = gr.get("unit")
                if unit is not None:
                    pe.wait_ge(c.lo_done.sem, c.lo_done.at(l, unit + 1))
                    s = unit % RING
                if e >= 2:
                    pe.wait_ge(c.evacs[gr["bank"]].sem, c.evacs[gr["bank"]].at(l, e // 2))
                if kind == "fm":
                    for k in range(KT):
                        if gr is b["order"][0]:
                            pe.wait_ge(c.rn_lo.sem, c.rn_lo.at(l, (0 if b is b1 else 8) + k + 1))
                        ins = mm3(bk[:, :], cols(whi, s, k), cols(wlo, s, k), hh[:, k, :], hl[:, k, :], k == 0, k == KT - 1)
                elif kind in ("tm", "gates"):
                    n = P if kind == "tm" else 18
                    for t in range(QT):
                        o = bk[:, P * t:P * t + n]
                        for k in range(KT):
                            ah, al = hh[:, k, P * t:P * t + P], hl[:, k, P * t:P * t + P]
                            ins = mm3(o, ah, al, cols(whi, s, k, n=n), cols(wlo, s, k, n=n), k == 0, k == KT - 1)
                elif kind == "swap":
                    r = gr["rows"]
                    need(c, b, l, gr["of"])
                    at = {"r": C_PERM_R, "n": C_PERM_N, "m": C_PERM_M}[gr["perm"]]
                    ins = pe.matmul(bk[0:r[1], :], cs(at, r, r[1]), g(gr["tile"], S, r), start=True, stop=True)
                elif kind == "uq":
                    for k in range(2):
                        if gr["name"] == "mq0":
                            pe.wait_ge(c.rn_lo.sem, c.rn_lo.at(l, 17 + k))
                        ins = mm3(bk[0:MLA_D, :], cols(whi, s, k, MLA_D * gr["j"], MLA_D, 288), cols(wlo, s, k, MLA_D * gr["j"], MLA_D, 288),
                                  fshi[:, k, :], fslo[:, k, :], k == 0, k == 1)
                elif kind == "ukv_k":
                    if gr["name"] == "mk0":
                        pe.wait_ge(c.rn_lo.sem, c.rn_lo.at(l, 19))
                    ins = mm3(bk[:, :], cols(whi, s, gr["j"]), cols(wlo, s, gr["j"]), fshi[:, 2, :], fslo[:, 2, :], True, True)
                elif kind == "ukv_v":
                    v = lambda t_: t_[:, s, 0:768].rearrange("p (h n) -> p h n", h=MLA_H)[:, :, HD:]
                    q = P * gr["j"]
                    ins = mm3(bk[:, 0:384].rearrange("p (h n) -> p h n", h=MLA_H), fshi[:, 2, q:q + P], fslo[:, 2, q:q + P], v(whi), v(wlo), True, True)
                elif kind == "cmp":
                    k = 4 * gr["kv"] + gr["u"]
                    pe.wait_ge(c.px_lo.sem, c.px_lo.at(l, k + 1))
                    for t in range(8):
                        ah, al = fshi[:, k % 2, 64 * t:64 * t + 64], fslo[:, k % 2, 64 * t:64 * t + 64]
                        ins = mm3(bk[:, 0:64], cols(whi, s, t), cols(wlo, s, t), ah, al, gr["u"] == 0 and t == 0, gr["u"] == 3 and t == 7)
                elif kind == "w2":
                    need(c, b, l, f"c{gr['kv']}3")
                    for j in range(2):
                        hid = g(M_HID + 64 * gr["kv"] + 32 * j, 32)
                        if gr["kv"] == 0:
                            ins = pe.matmul(bk[HD * j:HD * j + HD, 0:32], prm[:, P2_WK:P2_WK + HD], hid, start=True, stop=True)
                        else:
                            ins = pe.matmul(bk[0:32, HD * j:HD * j + HD], hid, prm[:, P2_WV:P2_WV + HD], start=True, stop=True)
                elif kind == "cmean":
                    pe.wait_ge(c.taps.sem, c.taps.at(l, 1))
                    for t in range(2):
                        ins = pe.matmul(bk[:, :], ones, g(A_SG + S * t), start=t == 0, stop=t == 1)
                elif kind == "cvar":
                    pe.wait_ge(c.ln_sq.sem, c.ln_sq.at(l, 2))
                    for t in range(2):
                        ins = pe.matmul(bk[:, :], ones, g(A_Y + S * t), start=t == 0, stop=t == 1)
                elif kind == "rmean":
                    pe.wait_ge(c.o_done.sem, c.o_done.at(l, 8 + 2 * gr["t"]))
                    ins = pe.matmul(bk[:, :], blk, g(A_RQ + S * gr["t"]), start=True, stop=True)
                elif kind == "rvar":
                    pe.wait_ge(c.ln_sq.sem, c.ln_sq.at(l, 3 + gr["t"]))
                    ins = pe.matmul(bk[:, :], blk, g(A_RK + S * gr["t"]), start=True, stop=True)
                ins.then_inc(c.group_done.sem, 1)

            def retention(c, b, l, j):
                if j < 24:
                    h, jt = j // 4, j % 4
                    r, n = half(h % 2), S - P * jt
                    if jt == 0:
                        need(c, b, l, f"sq{h // 2}", f"sk{h // 2}", f"rv{h // 2}")
                    if j >= 2:
                        pe.wait_ge(c.r_dec.sem, c.r_dec.at(l, j - 1))
                    pe.matmul(bank[S_B[j % 2]][:, 0:n], g(A_RK + S * (h // 2) + P * jt, P, r), g(A_RQ + S * (h // 2) + P * jt, n, r),
                              start=True, stop=True).then_inc(c.r_s.sem, 1)
                if j % 8 or j >= 24:
                    if j:
                        retention_pv(c, l, j - 1)

            def retention_pv(c, l, k):
                h, jt = k // 4, k % 4
                pe.wait_ge(c.r_dec.sem, c.r_dec.at(l, k + 1))
                if jt == 0:
                    pe.wait_ge(c.o_done.sem, c.o_done.at(l, 6 + h - 1))
                n = S - P * jt
                pe.matmul(bank[O_B[h % 2]][HD * (h % 2):HD * (h % 2) + HD, P * jt:S], g(A_RV + 384 * jt + HD * h, HD), g(A_P + S * (k % 2), n),
                          start=jt == 0, stop=jt == 3).then_inc(c.r_pv.sem, 1)

            def out_product(c, b, l):
                for m in range(KT):
                    pe.wait_ge(c.lo_done.sem, c.lo_done.at(l, b["wo"] + m + 1))
                    s = (b["wo"] + m) % RING
                    for k in range(KT):
                        if m == 0:
                            pe.wait_ge(c.mix_lo.sem, c.mix_lo.at(l, k + 1))
                        ins = mm3(bank[m][:, :], cols(whi, s, k), cols(wlo, s, k), hh[:, k, :], hl[:, k, :], k == 0, k == KT - 1)
                    ins.then_inc(c.group_done.sem, 1)

            def up_unit(c, b, l, n, bk, more):
                pe.wait_ge(c.lo_done.sem, c.lo_done.at(l, n + 1 + more))
                s = n % RING
                for k in range(KT):
                    ins = mm3(bk[:, :], cols(whi, s, k), cols(wlo, s, k), hh[:, k, :], hl[:, k, :], k == 0, k == KT - 1)
                ins.then_inc(c.group_done.sem, 1)

            def down(c, b, l, n0, h0, nt):
                def one(t, i=None, first=False, last=False):
                    more = 0 if i is None else i * 4
                    pe.wait_ge(c.f_lo.sem, c.f_lo.at(l, h0 + t + 1 + more))
                    pe.wait_ge(c.lo_done.sem, c.lo_done.at(l, n0 + t + 1 + more))
                    s, fs = (n0 + t) % RING, t % 2
                    for m in range(KT):
                        ins = mm3(bank[m][:, :], cols(whi, s, m), cols(wlo, s, m), fshi[:, fs, :], fslo[:, fs, :], first, last)
                    ins.then_inc(c.group_done.sem, 1)
                for j in range(4):
                    one(j, first=j == 0)
                whole = nt // 4 * 4 if nt % 4 else nt - 4
                with pe.Fori(1, whole // 4) as i:
                    for j in range(4):
                        one(j, i)
                for j in range(whole, nt):
                    one(j, last=j == nt - 1)

            pe.wait_ge(x_dma, 16)
            pe.wait_ge(const_in, 48)
            pe.wait_ge(masks_ready, 1)
            for k in range(KT):
                if k >= 2:
                    pe.wait_ge(counts_of(0).x_ready.sem, k - 1)
                for t in range(QT):
                    ins = pe.transpose(bank[k % 2][:, P * t:P * t + P], g(D * t + P * k, P), ident)
                ins.then_inc(tin, 1)

            c, b = counts_of(0), b1
            with pe.Fori(0, LAYERS) as l:
                norm(c, l, 0, KT, bank[0][:, :])
                for s in b["steps"]:
                    if s[0] == "g":
                        group(c, b, l, b["groups"][s[1]])
                    elif s[0] == "i":
                        item(c, b, l, s[1], 0, n1, True)
                    elif s[0] == "r":
                        if s[1] == 0:
                            pe.wait_ge(c.biased.sem, c.biased.at(l, n1))
                            pe.wait_ge(c.turned.sem, c.turned.at(l, n1))
                        retention(c, b, l, s[1])
                    elif s[0] == "r_out":
                        retention_pv(c, l, 8 * s[1] + 7)
                pe.wait_ge(c.ret_out.sem, c.ret_out.at(l, 3))
                out_product(c, b, l)
                norm(c, l, 8, KT, bank[0][:, :])
                norm(c, l, 16, KT, bank[0][:, :])
                n0 = b["wo"] + KT
                with pe.Fori(0, T1 // 4) as i:
                    for j in range(4):
                        pe.wait_ge(c.relu.sem, c.relu.at(l, j - 3 + i * 4))
                        if j == 0:
                            pe.wait_ge(c.rn_lo.sem, c.rn_lo.at(l, 16))
                        up_unit(c, b, l, n0 + j, bank[j], i * 4)
                pe.wait_ge(c.f_done.sem, c.f_done.at(l, T1))
                down(c, b, l, n0 + T1, 0, T1)
                norm(c, l, 24, KT, bank[0][:, :])

            c, b = counts_of(1), b2

            def mlp(l, n0, f0, a, b0):
                norm(c, l, a, KT, bank[0][:, :])
                with pe.Fori(0, T2 // 2) as i:
                    for j in range(4):
                        free = c.f2_done if j % 2 else c.silu
                        pe.wait_ge(free.sem, free.at(l, f0 + j // 2 - 1 + i * 2))
                        if j == 0:
                            pe.wait_ge(c.rn_lo.sem, c.rn_lo.at(l, b0 + KT))
                        up_unit(c, b, l, n0 + j, bank[j], i * 4)
                pe.wait_ge(c.f2_done.sem, c.f2_done.at(l, f0 + T2))
                down(c, b, l, n0 + 2 * T2, f0, T2)

            with pe.Fori(0, LAYERS) as l:
                mlp(l, 0, 0, 0, 0)
                norm(c, l, 8, KT, bank[0][:, :])
                for s in b["steps"]:
                    if s[0] == "g":
                        group(c, b, l, b["groups"][s[1]])
                    elif s[0] == "rn":
                        norm(c, l, *((16, 2) if s[1] == "cq" else (18, 1)), bank[2][:, :])
                    elif s[0] == "i":
                        item(c, b, l, s[1], s[2], s[3], False)
                    elif s[0] == "z":
                        h, jt = s[1:]
                        zi, n, r = 4 * h + 3 - jt, S - P * jt, half(h % 2)
                        if zi == 0:
                            need(c, b, l, "bq1", "bk0", "bk1", "bv0", "bv1")
                            pe.wait_ge(c.exped.sem, c.exped.at(l, 24))
                            pe.wait_ge(c.pt.sem, c.pt.at(l, 24))
                        if zi >= 2:
                            pe.wait_ge(c.z_lr.sem, c.z_lr.at(l, zi - 1))
                        pe.matmul(bank[S_B[zi % 2]][:, 0:n], g(B_K + S * (h // 2) + P * jt, P, r), g(B_Q + S * (h // 2) + P * jt, n, r),
                                  start=True, stop=True).then_inc(c.z.sem, 1)
                    elif s[0] == "suf":
                        h, jt = s[1:]
                        zi, n = 4 * h + 3 - jt, S - P * jt
                        pe.wait_ge(c.z_lr.sem, c.z_lr.at(l, zi + 1))
                        if zi >= 2:
                            pe.wait_ge(c.suf_t.sem, c.suf_t.at(l, zi - 1))
                        bk = bank[T_B[zi % 2]]
                        ins = pe.matmul(bk[:, 0:n], tri, g(B_LR + SB_AT[jt], n), start=True, stop=jt == 3)
                        for j2 in range(jt + 1, QT):
                            ins = pe.matmul(bk[:, P * (j2 - jt):n], ones, g(B_LR + SB_AT[j2], S - P * j2), start=False, stop=j2 == 3)
                        ins.then_inc(c.suf.sem, 1)
                    elif s[0] == "sbo":
                        h = s[1]
                        pe.wait_ge(c.suf_m.sem, c.suf_m.at(l, 4 * h + 4))
                        pe.wait_ge(c.o_done.sem, c.o_done.at(l, 6 + h - 1))
                        for jt in range(QT):
                            ins = pe.matmul(bank[O_B[h % 2]][HD * (h % 2):HD * (h % 2) + HD, P * jt:S], g(B_V + 256 * jt + HD * h, HD),
                                            g(B_LB + SB_AT[jt], S - P * jt), start=jt == 0, stop=jt == 3)
                        ins.then_inc(c.sb_pv.sem, 1)
                out_product(c, b, l)
                mlp(l, b["wo"] + KT, T2, 19, 19)

            for t in range(KT):
                pe.wait_ge(c.rn_sq.sem, c.rn_sq.at(2, t + 1))
                pe.matmul(bank[0][:, :], ones, sq[t % 2], start=t == 0, stop=t == KT - 1).then_inc(c.rn_used.sem, 1)
            pe.wait_ge(fin, 1 + KT)
            for n in range(2 * QT):
                if n >= 4:
                    pe.wait_ge(fin_ev, n - 3)
                for k in range(4):
                    ins = pe.transpose(bank[2 + n % 4][:, P * k:P * k + P], x[:, 4 * (n % 2) + k, P * (n // 2):P * (n // 2) + P], ident)
                ins.then_inc(tout, 1)


INPUTS = ["x", "norm_mix_pre", "norm_mix_post", "norm_mlp_pre", "norm_mlp_post", "w_in", "attn_rel_bias", "conv_w", "conv_b",
          "conv_ln_g", "conv_ln_b", "w_out", "w_up", "w_down", "ffn1_norm_2", "ffn1_w_gate_2", "ffn1_w_up_2", "ffn1_w_down_2",
          "mix_norm_2", "w_in_2", "mla_q_norm_2", "mla_w_uq_2", "mla_kv_norm_2", "mla_w_ukv_2", "nsa_gate_bias_2",
          "nsa_cmp_pos_k_2", "nsa_cmp_w1_k_2", "nsa_cmp_w2_k_2", "nsa_cmp_pos_v_2", "nsa_cmp_w1_v_2", "nsa_cmp_w2_v_2",
          "w_out_2", "ffn2_norm_2", "ffn2_w_gate_2", "ffn2_w_up_2", "ffn2_w_down_2", "final_norm_2"]


def kernel(**inputs):
    import concourse.bacc as bacc
    from concourse.bass_utils import run_bass_kernel_spmd

    nc = bacc.Bacc("TRN2", target_bir_lowering=False, num_devices=1)
    arrays, w = {}, {}
    for name in INPUTS:
        a = np.ascontiguousarray(inputs[name])
        arrays[f"in_{name}"] = a
        w[name] = nc.dram_tensor(f"in_{name}", a.shape, mybir.dt.from_np(a.dtype), kind="ExternalInput").ap()
    consts = []
    for name, a in zip(("c_words", "c_masks", "c_tab1", "c_tab2"), constants()):
        arrays[name] = a
        consts.append(nc.dram_tensor(name, a.shape, mybir.dt.from_np(a.dtype), kind="ExternalInput").ap())
    scratch = nc.dram_tensor("bias_rows", [LAYERS * HEADS1, BIAS_ROW], F32).ap()
    out = nc.dram_tensor("out", [1, S, D], F32, kind="ExternalOutput").ap()
    build(nc, w["x"], *consts, scratch, out, w)
    r = run_bass_kernel_spmd(nc, [arrays], core_ids=[0])
    return r.results[0]["out"]
```

```python
from contextlib import ExitStack

import numpy as np

import concourse.bass as bass
from concourse import mybir

F32 = mybir.dt.float32
F32R = mybir.dt.float32r
BF16 = mybir.dt.bfloat16
ALU = mybir.AluOpType
ACT = mybir.ActivationFunctionType
AXX = mybir.AxisListType.X

P = 128
D = 1024
S = 512
KT = D // P
QT = S // P
LAYERS = 2
UNIT = 1024
RING = 4
LOOK = 2
EPS = 1e-6
NEG = -1e30
LN_SET = "natural_log_exp_and_others"
SILU_SET = "silu_and_others"
HD = 64
TURN_LAG, PV_LAG = 2, 3

D_IN, FF1, HEADS1 = 3200, 4096, 6
T1 = FF1 // P
TAPS, CONV = 31, 256
BIAS_ROW = 640
D_IN2, FF2 = 2354, 2816
T2 = FF2 // P
MLA_H, MLA_D, SB_H, NSA_H = 6, 96, 4, 6
CMP_N = 31
MLA_SCALE, HEAD_SCALE = float(96) ** -0.5, 0.125

C_IDENT, C_ONES, C_BLK, C_TRI, C_STRICT, C_PERM_R, C_PERM_N, C_PERM_M, C_VALID = [128 * i for i in range(9)]
C_WORDS = 8 * 128 + 4
SCR_SQ, SCR_RSTD, SCR_TMP, SCR_SQ2 = 0, 1024, 1536, 2560
A_P, A_PT, A_SB, A_H = 0, 1024, 2048, 3072
A_Q, A_K, A_V, A_SG, A_Y, A_RQ, A_RK, A_RV, MIX = 4096, 5632, 7168, 8704, 9728, 10816, 12352, 13888, 15424
A_D = (A_Q, A_K)
F_AT = 3072
YW = 544
M_GATE, M_POSX, M_KC, M_VC, M_HID = 2048, 2128, 2640, 2704, 2832
M_Q, M_K, M_V, M_PE = 3072, 6144, 9216, 10752
B_Q, B_K, B_V = 11264, 12288, 13312
B_LR, B_LB, B_T = (4096, 5376), (6656, 7936), (9216, 9728)
G_WORDS = MIX + 8 * 512
TAB_AT = 20000
N_Q, N_KW, N_VW, N_KS, N_KC, N_VC, N_VS = TAB_AT + 2048, TAB_AT + 3584, M_PE, 14336, MIX + 6 * 512, MIX + 7 * 512, 14848
OUT_AT, MASK_AT, X_AT = 4096, 6144, 8192
SB_AT = [0, 512, 896, 1152]
ACT_STEPS, DVE_STEPS = (2, 32), (119, 226)
A_FIRST = (0, 0)
A1_POST, A1_MLP, A1_MPOST, A1_NEXT = (8, 8, 0), (16, 9), (24, 17, 7), (32, 18)
A2_MIX, A2_Q, A2_KV, A2_MLP, A2_NEXT = (8, 8), (16, 16), (18, 18), (19, 19, 0), (27, 20)
P1_MIX, P1_POST, P1_MLP, P1_MPOST, P1_CW, P1_CB, P1_LG, P1_LB = 0, 8, 16, 240, 32, 94, 96, 98
P2_F1, P2_MIX, P2_F2, P2_QN, P2_KVN, P2_GB, P2_PK, P2_PV, P2_WK, P2_WV = 0, 8, 16, 24, 26, 27, 45, 77, 109, 173
PRM_WORDS = 248


def constants():
    f = np.float32
    p = np.arange(P)
    c = np.zeros((P, C_WORDS), f)
    c[:, C_IDENT:C_IDENT + P] = np.eye(P)
    c[:, C_ONES:C_ONES + P] = 1.0
    c[:, C_BLK:C_BLK + P] = (p[:, None] // HD == p[None, :] // HD) / HD
    c[:, C_TRI:C_TRI + P] = p[:, None] > p[None, :]
    c[:, C_STRICT:C_STRICT + P] = p[:, None] < p[None, :]
    in_head = p % HD
    partner_r = p - in_head + (in_head + 32) % HD
    partner_n = np.where(in_head < 8, p + 8, np.where(in_head < 16, p - 8, p))
    partner_m = np.where((p >= 64) & (p < 80), p + 16, np.where((p >= 80) & (p < 96), p - 16, p))
    for at, partner in ((C_PERM_R, partner_r), (C_PERM_N, partner_n), (C_PERM_M, partner_m)):
        c[partner, at + p] = 1.0
    c[:, C_VALID:C_VALID + QT] = (p[:, None] + P * np.arange(QT)[None, :]) >= 31
    q, k = p[:, None], p[None, :]
    masks = np.zeros((P, 4 * P), f)
    masks[:, 0:P] = np.eye(P)
    masks[:, P:2 * P] = np.where(k > q, NEG, 0)
    masks[:, 2 * P:3 * P] = np.where(k // 64 > q // 64, NEG, 0)
    blk = np.arange(32)[None, None, :]
    tok = (p[:, None] + P * np.arange(QT)[None, :])[:, :, None]
    masks[:, 3 * P:] = np.where(16 * blk + 31 > tok, NEG, 0).reshape(P, P)

    pos = np.arange(S, dtype=f)
    t1 = np.zeros((P, 4096), f)
    log_g = np.log1p(-(2.0 ** (-5.0 - np.arange(HEADS1))))
    diff = (np.arange(S)[None, :] - p[:, None]).astype(np.float64)
    for h in range(HEADS1):
        t1[:, h * S:(h + 1) * S] = np.where(diff >= 0, np.exp(np.maximum(diff, 0) * log_g[h]) * HEAD_SCALE, 0)
    inv = (f(1.0) / (f(10000.0) ** np.linspace(0, 1, 32, dtype=f))).astype(f)
    ang = (inv[in_head % 32][:, None] * pos[None, :]).astype(f)
    t1[:, 3072:3584] = np.cos(ang)
    t1[:, 3584:4096] = np.where(in_head < 32, -1, 1)[:, None] * np.sin(ang)

    t2 = np.zeros((P, 2048), f)

    def partial(at, first, half, rows):
        theta = (f(500000.0) ** (-np.arange(half, dtype=f) / f(half))).astype(f)
        a = (theta[np.where(first >= 0, first, 0) % half][:, None] * pos[None, :]).astype(f)
        on = (first >= 0)[:, None]
        t2[:, at:at + S] = np.where(on, np.cos(a), 1)
        t2[:, at + S:at + 2 * S] = np.where(on, np.where(first < half, -1, 1)[:, None] * np.sin(a), 0)
    partial(0, np.where(in_head < 16, in_head, -1), 8, P)
    partial(1024, np.where((p >= 64) & (p < 96), p - 64, -1), 16, P)
    return c, masks, t1, t2


class Count:

    def __init__(self, sem, per, base=0, step=1):
        self.sem, self.per, self.base, self.step, self.k = sem, per, base, step, 0

    def at(self, layer, k):
        return layer * (self.per * self.step) + (self.base + k) * self.step

    def next(self):
        self.k += 1
        return self.sem

    def now(self, layer):
        return self.at(layer, self.k)

    def check(self):
        if self.k != self.per:
            raise ValueError(f"{self.k} steps, {self.per} stated")


class Counts:

    def evac(self, gr):
        return self.evacs[gr["bank"]]

    def emptied(self, layer, gr):
        return self.evac(gr).at(layer, gr["e"] // 2 + 1)


def softmax_items_block1():
    return [dict(h=h, i=i, n=P * (i + 1), branch=None, first=True, last=True) for h in range(HEADS1) for i in range(QT)]


def softmax_items_block2():
    mla = [dict(h=h, i=i, n=P * (i + 1), branch="mla", first=True, last=True) for h in range(MLA_H) for i in range(QT)]
    nsa = [dict(h=h, i=i, n=32 if b == "cmp" else P * (i + 1), branch=b, first=b == "sel", last=b == "cmp")
           for h in range(NSA_H) for i in range(QT) for b in ("sel", "win", "cmp")]
    return mla, nsa




def copies(groups):
    n = sum(gr.get("evac", True) for gr in groups)
    e = 0
    for gr in groups:
        gr["bank"], gr["e"] = (e + n) % 2, e
        if gr.get("evac", True):
            e += 1
    return groups, e


def weave(*lists):
    keyed = [((i + 0.5) / len(steps), n, i, step) for n, steps in enumerate(lists) for i, step in enumerate(steps)]
    return [k[3] for k in sorted(keyed, key=lambda k: k[:3])]


def plan_block1():
    units, groups = [], {}

    def add(name, kind, col, **more):
        units.append(("w_in", col))
        groups[name] = dict(name=name, kind=kind, unit=len(units) - 1, **more)
        return ("g", name)

    def add_turned(name, col, t, at, **more):
        groups[name] = dict(name=name, kind="turn", of=name + "f", tile=MIX + S * at, off=128 * t, pitch=384, frees="act", **more)
        return add(name + "f", "fm", col, frees="act", dst=MIX + S * at)

    def qkv(t):
        return [add(f"q{t}", "fm", 128 * t, frees="act", dst=A_Q + S * t, scale=HEAD_SCALE),
                add(f"k{t}", "fm", 384 + 128 * t, frees="dve", dst=A_K + S * t),
                add_turned(f"v{t}", 768 + 128 * t, t, 3, dst=A_V)]

    def ret_qkv(t):
        for m, at in (("q", A_RQ), ("k", A_RK)):
            groups[f"s{m}{t}"] = dict(name=f"s{m}{t}", kind="swap", of=f"r{m}{t}", tile=at + S * t, rows=(0, P), perm="r", tab=3072, frees="dve")
        return [add(f"rq{t}", "fm", 1664 + 128 * t, frees="act", dst=A_RQ + S * t),
                add(f"rk{t}", "fm", 2048 + 128 * t, frees="act", dst=A_RK + S * t), ("g", f"sq{t}"),
                add_turned(f"rv{t}", 2432 + 128 * t, t, 4, dst=A_RV), ("g", f"sk{t}")]

    def gate(t):
        return add(f"rg{t}", "fm", 2816 + 128 * t, frees="act", dst=MIX + S * (5 + t), func="Silu", keep=t != 1)

    def heads(t):
        steps = []
        for j in range(8 * t, 8 * t + 8):
            groups[f"rs{j}"] = dict(name=f"rs{j}", kind="rs", j=j, frees="dve")
            steps.append(("g", f"rs{j}"))
            if j % 8:
                steps.append(("r_pv", j - 1))
        return steps + [("r_pv", 8 * t + 7), ("r_out", t)]

    for t in range(3):
        groups[f"lm{t}"] = dict(name=f"lm{t}", kind="rmean", t=t, frees="dve")
        groups[f"lv{t}"] = dict(name=f"lv{t}", kind="rvar", t=t, frees="act", nth=(1, 2, 4)[t], squared=(1, 2, 5)[t])
    groups["cm"] = dict(name="cm", kind="cmean", frees="dve")
    groups["cv"] = dict(name="cv", kind="cvar", frees="act", nth=3, squared=4)

    def items(a, z):
        return [("i", k) for k in range(a, z)]

    def taps(a, z):
        return [("taps", k, k + 1) for k in range(a, z)]
    conv = []
    steps = qkv(0)
    for t in range(2):
        steps.append(add(f"cg{t}", "fm", 1408 + 128 * t, frees="act", dst=A_SG + S * t, func="Sigmoid", keep=t == 0))
        if t == 0:
            steps.append(("g", "v0"))
    for t in range(2):
        conv.append(add(f"ca{t}", "fm", 1152 + 128 * t, frees="dve", glu=t))
    steps += weave(conv, items(0, 1))
    steps += weave(ret_qkv(0) + [("g", "rv0")], items(1, 8), taps(0, 6))
    more = qkv(1)
    r1 = ret_qkv(1)
    steps += weave(more + [r1[0], ("g", "v1")] + r1[1:] + [("g", "rv1")], heads(0), taps(6, 16))
    more, r2 = qkv(2), ret_qkv(2)
    steps += weave(more + [r2[0], ("g", "v2")] + r2[1:] + [("g", "rv2")], heads(1), items(8, 16), taps(16, 26))
    steps += weave([("i", 16)], taps(26, TAPS))
    steps += weave([gate(0), ("g", "lm0"), ("g", "lv0"), gate(1), ("g", "lm1"), ("g", "lv1"), ("g", "cm"), ("g", "cv"), gate(2), ("conv_out",)],
                   heads(2), items(17, HEADS1 * QT + PV_LAG))
    steps += [("mix", 0), ("mix", 1), ("g", "lm2"), ("mix", 2), ("mix", 3), ("mix", 4), ("g", "lv2"), ("mix", 5), ("mix", 6), ("mix", 7)]
    order = [groups[s[1]] for s in steps if s[0] == "g"]
    n_in = len(units)
    units += [("w_out", 128 * m) for m in range(KT)] + [("w_up", t) for t in range(T1)] + [("w_down", t) for t in range(T1)]
    return units, order, groups, steps, n_in


def plan_block2():
    units = []
    for t in range(T2):
        units += [("g1", t), ("u1", t)]
    units += [("d1", t) for t in range(T2)]
    first = len(units)
    groups, steps, units_at = {}, [], {}

    def add(name, kind, src, **more):
        if src is not None:
            units.append(src)
            more["unit"] = len(units) - 1
        groups[name] = dict(name=name, kind=kind, **more)
        return ("g", name)

    for t in range(2):
        steps.append(add(f"cq{t}", "fm", ("w_in", 128 * t), frees="act", dst=M_V + S * t))
    steps.append(("sq", "cq"))
    steps.append(add("ckv", "fm", ("w_in", 256), frees="act", dst=M_V + 2 * S))
    steps += [("rn", "cq"), ("sq", "ckv")]
    steps.append(add("bq0", "fm", ("w_in", 1586), frees="act", dst=B_Q, scale=HEAD_SCALE))
    steps.append(("rn", "ckv"))
    steps.append(add("pe", "fm", ("w_in", 320), frees="act", dst=M_PE, rows=(64, 96)))
    steps.append(add("bq1", "fm", ("w_in", 1586 + 128), frees="act", dst=B_Q + S, scale=HEAD_SCALE))
    steps.append(add("spe", "swap", None, of="pe", tile=M_PE, rows=(64, 96), perm="m", tab=1024, frees="dve"))
    for j in range(2):
        for i in range(3):
            h = 3 * j + i
            if i == 0:
                units.append(("w_uq", 288 * j))
            groups[f"mq{h}"] = dict(name=f"mq{h}", kind="uq", unit=len(units) - 1, j=i, frees="act", dst=M_Q + S * h, rows=(0, MLA_D), scale=MLA_SCALE)
            steps.append(("g", f"mq{h}"))
            if h:
                steps.append(("g", f"sm{h - 1}"))
            groups[f"sm{h}"] = dict(name=f"sm{h}", kind="swap", of=f"mq{h}", tile=M_Q + S * h, rows=(0, MLA_D), perm="m", tab=1024, frees="dve")
    steps.append(("g", "sm5"))
    units.append(("w_ukv", 0))
    for h in range(MLA_H):
        groups[f"mk{h}"] = dict(name=f"mk{h}", kind="ukv_k", unit=len(units) - 1, j=h, frees=("act", "dve")[h % 2], dst=M_K + S * h, rows=(0, HD))
        steps.append(("g", f"mk{h}"))
    for t in range(QT):
        groups[f"mv{t}"] = dict(name=f"mv{t}", kind="ukv_v", unit=len(units) - 1, j=t, frees=("act", "dve")[t % 2], dst=M_V + 384 * t)
        steps.append(("g", f"mv{t}"))
    fill = []
    for t in range(2):
        fill.append(add(f"bk{t}", "fm", ("w_in", 1842 + 128 * t), frees="dve", dst=B_K + S * t))
    def add_turned(name, col, t, **more):
        at = MIX + S * (3 + t)
        groups[name] = dict(name=name, kind="turn", of=name + "f", tile=at, **more)
        return add(name + "f", "fm", ("w_in", col), frees="act", dst=at)
    for t in range(2):
        fill.append(add_turned(f"bv{t}", 2098 + 128 * t, t, frees="act", dst=B_V, off=128 * t, pitch=256))
        if t:
            fill.append(("g", "bv0"))
    for name, col, at in (("kc", 800, N_KC), ("vc", 928, N_VC)):
        fill.append(add(f"n{name}", "fm", ("w_in", col), frees="act", dst=at))
        fill.append(("g", "bv1" if name == "kc" else "snkc"))
    for t in range(3):
        fill.append(add(f"nq{t}", "fm", ("w_in2", t), frees="act", dst=N_Q + S * t, scale=HEAD_SCALE))
        fill.append(("px", t) if t < 2 else ("g", "snq1"))
        if t == 1:
            fill.append(("g", "snq0"))
    for kv in range(2):
        for u in range(2):
            fill.append(add(f"c{kv}{u}", "cmp", ("w1", kv, u), kv=kv, u=u, evac=u == 1, frees="act"))
        groups[f"w2{kv}"] = dict(name=f"w2{kv}", kind="w2", kv=kv, frees="act")
        if kv == 0:
            fill += [("px", 2), ("g", "snq2")]
            fill.append(add("nks", "fm", ("w_in", 1056), frees="act", dst=N_KS))
            fill += [("px", 3), ("g", "w20")]
    fill.append(add("nkw", "fm", ("w_in", 1312), frees="act", dst=N_KW))
    fill.append(("g", "w21"))
    fill.append(("g", "snks"))
    tiles = {"q0": N_Q, "q1": N_Q + S, "q2": N_Q + 2 * S, "kc": N_KC, "ks": N_KS, "kw": N_KW}
    for name, at in tiles.items():
        groups[f"sn{name}"] = dict(name=f"sn{name}", kind="swap", of=f"n{name}", tile=at, rows=(0, P), perm="n", tab=0, frees="dve")
    fill.append(add_turned("nvs", 1184, 0, frees="dve", dst=N_VS, off=0, pitch=128))
    fill.append(("g", "snkw"))
    fill.append(add_turned("nvw", 1440, 1, frees="dve", dst=N_VW, off=0, pitch=128))
    fill.append(("g", "nvs"))
    fill.append(add("gatesf", "fm", ("w_in", 1568), frees="act", dst=M_POSX))
    groups["gates"] = dict(name="gates", kind="turn", of="gatesf", tile=M_POSX, frees="dve")
    fill += [("g", "nvw"), ("g", "gates")]
    at = {}

    def place(j, *step):
        at.setdefault(j, []).append(step)

    def logits(j, h, jt):
        place(j, "z", h, jt)
        place(j + 1, "z_act", h, jt)
        place(j + 2, "z_dve", h, jt)
    n_mla = MLA_H * QT
    j = n_mla + PV_LAG + 1
    for jt in (3, 2, 1, 0):
        logits(j, 0, jt)
        j += 2
    for h in range(SB_H):
        for jt in (3, 2, 1, 0):
            place(j, "suf", h, jt)
            place(j + 1, "suf_add", h, jt)
            place(j + 1, "suf_exp", h, jt)
            place(j + 2, "suf_mask", h, jt)
            if jt == 3 and h:
                place(j, "sbo", h - 1)
                place(j + 1, "sb_out", h - 1)
            j += 2
            if h + 1 < SB_H:
                logits(j, h + 1, jt)
                j += 2
    place(j + 1, "sbo", SB_H - 1)
    place(j + 2, "sb_out", SB_H - 1)
    for k in range(3):
        place(n_mla + 8 + 4 * k, "mix", k)
    for k in range(2):
        place(n_mla + 24 * (k + 1) + PV_LAG, "mix", 3 + k)
    n_items = n_mla + 3 * NSA_H * QT
    n_fill = len(fill)
    for k in range(max(n_items + PV_LAG, max(at) + 1)):
        steps.append(("i", k))
        if k < n_mla:
            while len(fill) > n_fill - (k + 1) * n_fill // n_mla:
                steps.append(fill.pop(0))
        steps += at.get(k, [])
    steps += [("mix", k) for k in (5, 6, 7)]
    order = [groups[s[1]] for s in steps if s[0] == "g"]
    wo = len(units)
    units += [("w_out", 128 * m) for m in range(KT)]
    for t in range(T2):
        units += [("g2", t), ("u2", t)]
    units += [("d2", t) for t in range(T2)]
    return units, order, groups, steps, first, wo


def build(nc, x_in, cst, msk, tab1, tab2, scratch, out, w):
    with ExitStack() as ctx:
        def sb(name, shape, dt=F32):
            return ctx.enter_context(nc.sbuf_tensor(name, shape, dt))

        x = sb("x", [P, KT, S])
        hh, hl = sb("hh", [P, KT, S], F32R), sb("hl", [P, KT, S], F32R)
        raw = sb("raw", [P, RING, UNIT])
        whi, wlo = sb("whi", [P, RING, UNIT], F32R), sb("wlo", [P, RING, UNIT], F32R)
        fshi, fslo = sb("fshi", [P, 3, S], F32R), sb("fslo", [P, 3, S], F32R)
        G = sb("G", [P, G_WORDS])
        tab = sb("tab", [P, 4096])
        c_sb = sb("c_sb", [P, C_WORDS])
        m_sb = sb("m_sb", [P, 4 * P], BF16)
        prm = sb("prm", [P, PRM_WORDS])
        fin_g = sb("fin_g", [P, KT])
        stat = sb("stat", [P, 4, 3])
        eps = sb("eps", [P, 1])
        bank = [ctx.enter_context(nc.psum_tensor(f"bank{i}", [P, S], F32)) for i in range(8)]

        def g(at, n=S, rows=(0, P)):
            if at >= TAB_AT:
                return tab[rows[0]:rows[1], at - TAB_AT:at - TAB_AT + n]
            return G[rows[0]:rows[1], at:at + n]

        def cs(at, rows=(0, P), n=P):
            return c_sb[rows[0]:rows[1], at:at + n]

        def half(k):
            return (HD * k, HD * k + HD)

        ident, ones, blk, tri, strict = cs(C_IDENT), cs(C_ONES), cs(C_BLK), cs(C_TRI), cs(C_STRICT)
        identb, causal, chunked, cmpmask = (m_sb[:, P * i:P * i + P] for i in range(4))
        sq, rstd, tmp = [g(SCR_SQ), g(SCR_SQ + S)], g(SCR_RSTD), [g(SCR_TMP), g(SCR_TMP + S)]
        rt = [g(SCR_SQ), g(SCR_SQ + S)]

        def sq_slot(t):
            return sq[0] if t == 0 else sq[1] if t % 2 else g(SCR_SQ2)
        S_B, T_B, O_B = (2, 3), (4, 5), (6, 7)

        units1, order1, groups1, steps1, wo1 = plan_block1()
        units2, order2, groups2, steps2, in2, wo2 = plan_block2()
        items = (softmax_items_block1(), sum(softmax_items_block2(), []))
        blocks = []
        for units, order, groups, steps, wo in ((units1, order1, groups1, steps1, wo1), (units2, order2, groups2, steps2, wo2)):
            first = 0 if units is units1 else in2
            _, n_evac = copies(order)
            done, last_of = 0, {}
            for i in range(first):
                last_of[i] = i + 1
            done = first
            for gr in order:
                done += 1
                gr["done"] = done
                if gr.get("unit") is not None:
                    gr["starts"] = gr["unit"] not in last_of
                    last_of[gr["unit"]] = done
            for i in range(wo, len(units)):
                done += 1
                last_of[i] = done
            loads = [2 if u[0] == "w_in2" else 1 for u in units]
            size = [576 if u[0] == "w_uq" else 768 if u[0] == "w_ukv" else UNIT for u in units]
            blocks.append(dict(units=units, order=order, groups=groups, steps=steps, wo=wo, first=first, n=len(units),
                               last_of=last_of, groups_n=done, loads=loads, size=size, evacs=[n_evac // 2, (n_evac + 1) // 2]))
        b1, b2 = blocks

        def sem(name):
            return ctx.enter_context(nc.semaphore(name))

        n1, n2 = len(items[0]), len(items[1])
        made = {}

        def counts_of(b):
            c = Counts()

            def signal(name, per1, per2, start=0, step=1):
                if name not in made:
                    made[name] = sem(name)
                if b == 0:
                    return Count(made[name], per1, start, step)
                return Count(made[name], per2, start + LAYERS * per1, step)

            c.landed = [signal(f"landed{s}", sum(b1["loads"][s::RING]), sum(b2["loads"][s::RING]), 0, 16)
                        for s in range(RING)]
            c.hi_done = signal("hi_done", b1["n"], b2["n"])
            c.lo_done = signal("lo_done", b1["n"], b2["n"], RING)
            c.group_done = signal("group_done", b1["groups_n"], b2["groups_n"])
            c.evacs = [signal(f"evac{p}", b1["evacs"][p], b2["evacs"][p]) for p in range(2)]
            c.x_ready = signal("x_ready", 16, 24, KT)
            c.rn_sq = signal("rn_sq", 32, 27)
            c.rn_acc = signal("rn_acc", 14, 7)
            c.rn_used = signal("rn_used", 18, 20)
            c.rn_ln = signal("rn_ln", 4, 5)
            c.rn_rstd = signal("rn_rstd", 4, 5)
            c.rn_tmp = signal("rn_tmp", 8, 11)
            c.rn_hi = signal("rn_hi", 16, 27)
            c.rn_lo = signal("rn_lo", 16, 27, 1)
            c.mix_hi = signal("mix_hi", KT, KT)
            c.mix_lo = signal("mix_lo", KT, KT)
            c.down = signal("down", KT - 1, 2 * (KT - 1))
            c.y0 = signal("y0", 2, 0)
            c.qk = signal("qk", n1, n2)
            c.biased = signal("biased", n1, 0)
            c.maxed = signal("maxed", n1, n2)
            c.exped = signal("exped", n1, n2)
            c.scaled = signal("scaled", n1, n2)
            c.turned = signal("turned", n1, n2)
            c.pt = signal("pt", n1, n2)
            c.pv = signal("pv", n1, n2)
            c.sb_out = signal("sb_out", 0, SB_H)
            c.r_o = signal("r_o", 6, 0)
            c.o_done = signal("o_done", 6, 12)
            c.h_in = [signal(f"h_in{s}", 3, 0, 0, 16) for s in range(2)]
            c.r_pv = signal("r_pv", 24, 0)
            c.ln_sq = signal("ln_sq", 5, 0)
            c.ln_rstd = signal("ln_rstd", 4, 0)
            c.cv_out = signal("cv_out", 2, 0)
            c.ret_out = signal("ret_out", 3, 0)
            c.taps = signal("taps", 1, 0)
            c.z = signal("z", 0, 16)
            c.z_ln = signal("z_ln", 0, 16)
            c.z_lr = signal("z_lr", 0, 16)
            c.suf = signal("suf", 0, 16)
            c.suf_t = signal("suf_t", 0, 16)
            c.suf_a = signal("suf_a", 0, 16)
            c.suf_m = signal("suf_m", 0, 16)
            c.sb_pv = signal("sb_pv", 0, SB_H)
            c.kpe = signal("kpe", 0, MLA_H)
            c.px = signal("px", 0, 4)
            c.px_hi = signal("px_hi", 0, 4)
            c.px_lo = signal("px_lo", 0, 4)
            c.gate = signal("gate", 0, 1)
            c.up_norm = signal("up_norm", T1, 0, 4)
            c.f_done = signal("f_done", T1, 0)
            c.g_norm = signal("g_norm", 0, 2 * T2, 2)
            c.u_norm = signal("u_norm", 0, 2 * T2, 2)
            c.silu = signal("silu", 0, 2 * T2, 2)
            c.f2_done = signal("f2_done", 0, 2 * T2, 2)
            c.f_hi = signal("f_hi", T1, 2 * T2)
            c.f_lo = signal("f_lo", T1, 2 * T2)
            c.act_step = signal("act_step", ACT_STEPS[0], ACT_STEPS[1])
            c.dve_step = signal("dve_step", DVE_STEPS[0], DVE_STEPS[1])
            c.mpost_in = signal("mpost_in", 1, 0, 0, 16)
            c.prm_in = signal("prm_in", 8, 12, 0, 16)
            return c

        const_in, x_dma, tin, out_dma, scr_dma, bias_sem, fin, fin_ev, tout, tab_in = (
            sem(n) for n in ("const_in", "x_dma", "tin", "out_dma", "scr_dma", "bias_sem", "fin", "fin_ev", "tout", "tab_in"))
        rows_zero, gain_in, masks_ready, ident_in, decay_in, rows_in = sem("rows_zero"), sem("gain_in"), sem("masks_ready"), sem("ident_in"), sem("decay_in"), sem("rows_in")

        def slot3(t, s, n=UNIT):
            return t[:, s, 0:n]

        def f_tile(t):
            return G[:, bass.ds(F_AT + t * S, S)]

        block = ctx.enter_context(nc.Block())

        @block.sync
        def _(sp):
            sp.dma_start(ident, cst[:, C_IDENT:C_IDENT + P]).then_inc(ident_in, 16)
            sp.dma_start(G[0:LAYERS * HEADS1, 4096:4096 + 257], w["attn_rel_bias"].rearrange("l h n -> (l h) n")).then_inc(rows_in, 16)
            sp.dma_start(g(X_AT, QT * D).rearrange("p (t d) -> p t d", t=QT), x_in.rearrange("a (t p) d -> p (a t) d", p=P)).then_inc(x_dma, 16)
            sp.dma_start(c_sb[:, C_ONES:C_WORDS], cst[:, C_ONES:C_WORDS]).then_inc(const_in, 16)
            sp.dma_start(g(MASK_AT), msk).then_inc(const_in, 16)

            def load(c, b, l, n, at=None):
                kind, arg = b["units"][n][:2]
                s = n % RING
                more = 0 if at is None else at
                sp.wait_ge(c.lo_done.sem, c.lo_done.at(l, (n - RING + 1 if at is not None else max(n - RING + 1, 0)) + more))
                la = bass.ds(l, 1)
                cols8 = slot3(raw, s).rearrange("p (k n) -> p k n", k=KT)
                done = c.landed[s].sem
                sfx = "" if b is b1 else "_2"
                if kind in ("w_in", "w_out"):
                    src = w[kind + sfx][la, :, arg:arg + P].rearrange("a (k p) n -> p (a k) n", p=P)
                    sp.dma_start(cols8, src).then_inc(done, 16)
                elif kind == "w_in2":
                    for j in range(2):
                        c0 = 416 + 64 * arg + 192 * j
                        src = w["w_in_2"][la, :, c0:c0 + HD].rearrange("a (k p) n -> p (a k) n", p=P)
                        sp.dma_start(cols8[:, :, HD * j:HD * j + HD], src).then_inc(done, 16)
                elif kind == "w_uq":
                    src = w["mla_w_uq_2"][la, :, arg:arg + 288].rearrange("a (k p) n -> p (a k) n", p=P)
                    sp.dma_start(slot3(raw, s, 576).rearrange("p (k n) -> p k n", k=2), src).then_inc(done, 16)
                elif kind == "w_ukv":
                    sp.dma_start(slot3(raw, s, 768), w["mla_w_ukv_2"][la, :, :].rearrange("a p n -> (a p) n")).then_inc(done, 16)
                elif kind == "w1":
                    name = ("nsa_cmp_w1_k_2", "nsa_cmp_w1_v_2")[arg]
                    u = b["units"][n][2]
                    src = w[name][la, 1024 * u:1024 * u + 1024, :].rearrange("a (k p) n -> p (a k) n", p=P)
                    sp.dma_start(cols8, src).then_inc(done, 16)
                else:
                    name = {"w_up": "w_up", "w_down": "w_down", "g1": "ffn1_w_gate_2", "u1": "ffn1_w_up_2", "d1": "ffn1_w_down_2",
                            "g2": "ffn2_w_gate_2", "u2": "ffn2_w_up_2", "d2": "ffn2_w_down_2"}[kind]
                    step = 2 if kind[0] in "gu" else 1
                    tile = arg * P + more * (P // step)
                    if kind in ("w_down", "d1", "d2"):
                        src = w[name][la, bass.ds(tile, P), :].rearrange("a p n -> (a p) n")
                        sp.dma_start(slot3(raw, s), src).then_inc(done, 16)
                    else:
                        src = w[name][la, :, bass.ds(tile, P)].rearrange("a (k p) n -> p (a k) n", p=P)
                        sp.dma_start(cols8, src).then_inc(done, 16)

            def mlp_units(c, b, l, n0, n):
                if n0 == 0:
                    for j in range(RING):
                        load(c, b, l, j)
                with sp.Fori(1 if n0 == 0 else 0, n // 4) as i:
                    for j in range(4):
                        load(c, b, l, n0 + j, i * 4)
                for j in range(n // 4 * 4, n):
                    load(c, b, l, n0 + j)

            c = counts_of(0)
            with sp.Fori(0, LAYERS) as l:
                for n in range(b1["wo"] + KT):
                    load(c, b1, l, n)
                mlp_units(c, b1, l, b1["wo"] + KT, T1)
                mlp_units(c, b1, l, b1["wo"] + KT + T1, T1)
            c = counts_of(1)
            with sp.Fori(0, LAYERS) as l:
                mlp_units(c, b2, l, 0, 2 * T2)
                mlp_units(c, b2, l, 2 * T2, T2)
                for n in range(b2["first"], b2["wo"] + KT):
                    load(c, b2, l, n)
                mlp_units(c, b2, l, b2["wo"] + KT, 2 * T2)
                mlp_units(c, b2, l, b2["wo"] + KT + 2 * T2, T2)
            for t in range(QT):
                sp.wait_ge(fin_ev, 2 * t + 2)
                sp.dma_start(out[0, P * t:P * t + P, :], g(OUT_AT + D * t, D)).then_inc(out_dma, 16)
            sp.wait_ge(out_dma, 16 * QT)

        @block.gpsimd
        def _(pool):
            pool.dma_start(fin_g[:, :], w["final_norm_2"].rearrange("(k p) -> p k", p=P), allow_slow_non_contiguous=True).then_inc(gain_in, 16)
            rows = LAYERS * HEADS1
            pool.wait_ge(bias_sem, 3)
            pool.dma_start(scratch, G[0:rows, 4608:4608 + BIAS_ROW]).then_inc(scr_dma, 16)
            pool.wait_ge(scr_dma, 16)

            def columns(name, l, k):
                return w[name][bass.ds(l, 1), :].rearrange("a (k p) -> p (a k)", p=P)

            c = counts_of(0)
            with pool.Fori(0, LAYERS) as l:
                pool.wait_ge(c.rn_lo.sem, c.rn_lo.at(l, 0))
                done = c.prm_in.sem
                for name, at in (("norm_mix_pre", P1_MIX), ("norm_mix_post", P1_POST), ("norm_mlp_pre", P1_MLP)):
                    pool.dma_start(prm[:, at:at + KT], columns(name, l, KT), allow_slow_non_contiguous=True).then_inc(done, 16)
                for name, at in (("conv_b", P1_CB), ("conv_ln_g", P1_LG), ("conv_ln_b", P1_LB)):
                    pool.dma_start(prm[:, at:at + 2], columns(name, l, 2), allow_slow_non_contiguous=True).then_inc(done, 16)
                for t in range(2):
                    src = w["conv_w"][bass.ds(l, 1), :, P * t:P * t + P].rearrange("a k p -> p (a k)")
                    pool.dma_start(prm[:, P1_CW + TAPS * t:P1_CW + TAPS * t + TAPS], src, allow_slow_non_contiguous=True).then_inc(done, 16)
                pool.wait_ge(c.x_ready.sem, c.x_ready.at(l, 0))
                for h in range(HEADS1):
                    if h >= 2:
                        pool.wait_ge(c.biased.sem, c.biased.at(l, 4 * h - 4))
                    src = bass.AP(tensor=scratch.tensor, offset=l * (HEADS1 * BIAS_ROW) + h * BIAS_ROW, ap=[[1, P], [1, S]])
                    pool.dma_start(g(A_H + S * (h % 2)), src).then_inc(c.h_in[h % 2].sem, 16)
                    if h == 0:
                        pool.dma_start(prm[:, P1_MPOST:P1_MPOST + KT], columns("norm_mlp_post", l, KT), allow_slow_non_contiguous=True).then_inc(c.mpost_in.sem, 16)
            c = counts_of(1)
            pool.wait_ge(c.rn_lo.sem, c.rn_lo.at(0, 0))
            pool.dma_start(tab[:, 0:2048], tab2).then_inc(tab_in, 16)
            with pool.Fori(0, LAYERS) as l:
                pool.wait_ge(c.rn_lo.sem, c.rn_lo.at(l, 0))
                done = c.prm_in.sem
                la = bass.ds(l, 1)
                for name, at, k in (("ffn1_norm_2", P2_F1, KT), ("mix_norm_2", P2_MIX, KT), ("ffn2_norm_2", P2_F2, KT),
                                    ("mla_q_norm_2", P2_QN, 2), ("mla_kv_norm_2", P2_KVN, 1)):
                    pool.dma_start(prm[:, at:at + k], columns(name, l, k), allow_slow_non_contiguous=True).then_inc(done, 16)
                pool.dma_start(prm[:, P2_GB:P2_GB + 18], w["nsa_gate_bias_2"][la, :].to_broadcast([P, 18])).then_inc(done, 16)
                for name, at in (("nsa_cmp_pos_k_2", P2_PK), ("nsa_cmp_pos_v_2", P2_PV)):
                    src = w[name][la, :, :].rearrange("a t d -> d (a t)")
                    for j in range(2):
                        pool.dma_start(prm[HD * j:HD * j + HD, at:at + 32], src, allow_slow_non_contiguous=True).then_inc(done, 16)
                for name, at in (("nsa_cmp_w2_k_2", P2_WK), ("nsa_cmp_w2_v_2", P2_WV)):
                    pool.dma_start(prm[:, at:at + HD], w[name][la, :, :].rearrange("a p n -> (a p) n")).then_inc(done, 16)

        def landed(c, b, eng, l, n, more=0):
            s = n % RING
            eng.wait_ge(c.landed[s].sem, c.landed[s].at(l, sum(b["loads"][s:n + 1:RING]) + more))

        @block.scalar
        def _(act):
            def hi(c, b, l, n, i=None):
                s, m = n % RING, b["size"][n]
                more = 0 if i is None else i * 4
                landed(c, b, act, l, n, 0 if i is None else i)
                if n >= RING or i is not None:
                    act.wait_ge(c.group_done.sem, c.group_done.at(l, b["last_of"][n - RING] + more if n >= RING else n - RING + 1 + more))
                elif b is b2:
                    act.wait_ge(c.group_done.sem, c.group_done.at(l, 0))
                act.activation(slot3(whi, s, m), slot3(raw, s, m), ACT.Copy).then_inc(c.hi_done.sem, 1)

            def square(c, l, at, t, src):
                if t >= 2:
                    act.wait_ge(c.rn_used.sem, c.rn_used.at(l, at[1] + t - 1))
                act.activation(sq[t % 2], src, ACT.Square).then_inc(c.rn_sq.sem, 1)

            def square_added(c, l, at, t, src):
                if t >= 3:
                    act.wait_ge(c.rn_acc.sem, c.rn_acc.at(l, at[2] + t - 2))
                act.activation(sq_slot(t), src, ACT.Square).then_inc(c.rn_sq.sem, 1)

            def rms(c, l, r, at, n, rbank, dim):
                act.wait_ge(c.rn_used.sem, c.rn_used.at(l, at[1] + n))
                act.activation(rstd, rbank, ACT.Ln, scale=1.0 / dim, bias=eps[:, 0:1]).then_inc(c.rn_ln.sem, 1)
                act.wait_ge(c.rn_ln.sem, c.rn_ln.at(l, r))
                act.activation(rstd, rstd, ACT.Exp, scale=-0.5).then_inc(c.rn_rstd.sem, 1)

            def highs(c, l, t0, dst):
                for t in range(len(dst)):
                    act.wait_ge(c.rn_tmp.sem, c.rn_tmp.at(l, t0 + t + 1))
                    act.activation(dst[t], tmp[t % 2], ACT.Copy).then_inc(c.rn_hi.sem, 1)

            def gained_high(c, t, gains):
                act.activation(hh[:, t, :], x[:, t, :], ACT.Copy, scale=gains[:, t:t + 1]).then_inc(c.rn_hi.sem, 1)

            def x_squares(c, l, a, x0):
                for t in range(KT):
                    act.wait_ge(c.x_ready.sem, c.x_ready.at(l, x0 + t + 1))
                    square(c, l, a, t, x[:, t, :])

            def out_product(c, b, l, after):
                for m in range(KT):
                    hi(c, b, l, b["wo"] + m + LOOK)
                    if m:
                        after(m - 1)
                after(KT - 1)

            def post_square(c, l, a, t, y_k):
                if t == 0:
                    act.activation(g(F_AT), bank[0][:, :], ACT.Copy).then_inc(c.y0.sem, 1)
                    act.wait_ge(c.y0.sem, c.y0.at(l, y_k))
                square_added(c, l, a, t, g(F_AT) if t == 0 else bank[t][:, :])

            def item(c, l, j, lo, n, block1):
                its = items[0 if block1 else 1]
                if lo <= j < n:
                    it = its[j]
                    st = stat[:, j % 4, :]
                    act.wait_ge(c.maxed.sem, c.maxed.at(l, j + 1))
                    if j - lo >= 2:
                        act.wait_ge(c.turned.sem, c.turned.at(l, j - 1))
                    m = it["n"]
                    src = g(A_SB + S * (j % 2), m) if block1 else bank[S_B[j % 2]][:, 0:m]
                    act.activation(g(A_P + S * (j % 2), m), src, ACT.Exp, bias=st[:, 0:1], accum_out=st[:, 1:2]).then_inc(c.exped.sem, 1)
                k = j - TURN_LAG
                if lo <= k < n:
                    it = its[k]
                    act.wait_ge(c.turned.sem, c.turned.at(l, k + 1))
                    if k - lo >= 2:
                        act.wait_ge(c.pv.sem, c.pv.at(l, k - 1))
                    if it["n"] == 32:
                        act.activation(g(A_PT + S * (k % 2), P, (0, 32)), bank[T_B[k % 2]][0:32, 0:P], ACT.Copy).then_inc(c.pt.sem, 1)
                    else:
                        act.activation(g(A_PT + S * (k % 2), it["n"]), bank[T_B[k % 2]][:, 0:it["n"]], ACT.Copy).then_inc(c.pt.sem, 1)
                k = j - PV_LAG
                if lo <= k < n:
                    it = its[k]
                    if it["i"] == QT - 1 and it["last"]:
                        act.wait_ge(c.pv.sem, c.pv.at(l, k + 1))
                        head_out(c, l, it["h"], it["h"] // 2 + (3 if it["branch"] == "cmp" else 0))

            def head_out(c, l, h, tile):
                act.activation(g(MIX + S * tile, S, half(h % 2)), bank[O_B[h % 2]][HD * (h % 2):HD * (h % 2) + HD, :],
                               ACT.Copy).then_inc(c.o_done.sem, 1)

            def group(c, b, l, gr):
                if gr.get("starts") and gr["unit"] + LOOK < b["n"]:
                    hi(c, b, l, gr["unit"] + LOOK)
                kind, bk = gr["kind"], bank[gr["bank"]]
                evac = c.evac(gr).sem
                if kind == "cvar" or kind == "rvar":
                    tiles = [A_SG, A_SG + S] if kind == "cvar" else [A_RQ + S * gr["t"]]
                    to = [A_Y, A_Y + S] if kind == "cvar" else [A_RK + S * gr["t"]]
                    act.wait_ge(c.evac(b["groups"]["cm" if kind == "cvar" else f"lm{gr['t']}"]).sem, c.emptied(l, b["groups"]["cm" if kind == "cvar" else f"lm{gr['t']}"]))
                    for s_, d_ in zip(tiles, to):
                        act.activation(g(d_), g(s_), ACT.Square).then_inc(c.ln_sq.sem, 1)
                    act.wait_ge(c.group_done.sem, c.group_done.at(l, gr["done"]))
                    act.activation(g(to[0]), bk[:, :], ACT.Ln, scale=1.0 / CONV if kind == "cvar" else 1.0, bias=eps[:, 0:1]).then_inc(evac, 1)
                    act.wait_ge(c.evac(gr).sem, c.emptied(l, gr))
                    act.activation(g(to[0]), g(to[0]), ACT.Exp, scale=-0.5).then_inc(c.ln_rstd.sem, 1)
                    return
                if gr["frees"] != "act" or not gr.get("evac", True):
                    if gr["name"] == "gates":
                        act.wait_ge(c.evac(gr).sem, c.emptied(l, gr))
                        act.activation(g(M_GATE, 72), g(M_GATE, 72), ACT.Sigmoid).then_inc(c.gate.sem, 1)
                        act.preload_act_table_set(LN_SET)
                    return
                act.wait_ge(c.group_done.sem, c.group_done.at(l, gr["done"]))
                if kind in ("fm", "uq", "ukv_k"):
                    r = gr.get("rows", (0, P))
                    act.activation(g(gr["dst"], S, r), bk[r[0]:r[1], :], act_func(gr.get("func")), scale=gr.get("scale", 1.0)).then_inc(evac, 1)
                    if gr.get("func") and not gr.get("keep"):
                        act.preload_act_table_set(LN_SET)
                elif kind == "turn":
                    act.activation(tokens(gr), bk[:, :].rearrange("p (t n) -> p t n", t=QT), ACT.Copy).then_inc(evac, 1)
                elif kind == "ukv_v":
                    act.activation(g(gr["dst"], 384), bk[:, 0:384], ACT.Copy).then_inc(evac, 1)
                elif kind == "cmp":
                    act.activation(g(M_HID + 64 * gr["kv"], 64), bk[:, 0:64], ACT.Gelu_apprx_tanh).then_inc(evac, 1)
                    act.preload_act_table_set(LN_SET)
                elif kind == "w2":
                    if gr["kv"] == 0:
                        act.activation(g(M_KC, 32), bk[:, 0:32], ACT.Copy).then_inc(evac, 1)
                    else:
                        act.activation(g(M_VC, P, (0, 32)), bk[0:32, 0:P], ACT.Copy).then_inc(evac, 1)

            def act_func(name):
                return {None: ACT.Copy, "Sigmoid": ACT.Sigmoid, "Silu": ACT.Silu}[name]

            def tokens(gr):
                return g(gr["dst"], QT * gr["pitch"]).rearrange("p (t n) -> p t n", t=QT)[:, :, gr["off"]:gr["off"] + P]

            def down(c, b, l, n0, f0, nt, fsem):
                def one(j, i=None):
                    t, more = j, 0 if i is None else i * 4
                    f_hi(t + 1, more, i)
                    if n0 + t + LOOK < b["n"]:
                        hi(c, b, l, n0 + t + LOOK, i)

                def f_hi(t, more, i):
                    if t >= nt and i is None:
                        return
                    act.wait_ge(fsem.sem, fsem.at(l, f0 + t + 1 + more))
                    if t >= 2 or i is not None:
                        act.wait_ge(c.group_done.sem, c.group_done.at(l, b["last_of"][n0] + t - 2 + more))
                    else:
                        act.wait_ge(c.group_done.sem, c.group_done.at(l, b["last_of"][n0 - 1]))
                    act.activation(fshi[:, t % 2, :], f_tile(t + more), ACT.Copy).then_inc(c.f_hi.sem, 1)
                f_hi(0, 0, None)
                for j in range(4):
                    one(j)
                with act.Fori(1, (nt - 4) // 4 if nt % 4 == 0 else nt // 4) as i:
                    for j in range(4):
                        one(j, i)
                for j in range((nt - 4) if nt % 4 == 0 else nt // 4 * 4, nt):
                    one(j)

            act.preload_act_table_set(LN_SET)
            c = counts_of(0)
            for k in range(KT + 1):
                if k < KT:
                    act.wait_ge(tin, k + 1)
                    act.activation(x[:, k, :], bank[1 + k % 2][:, :], ACT.Copy).then_inc(c.x_ready.sem, 1)
                if k:
                    act.wait_ge(c.x_ready.sem, k)
                    square(c, 0, A_FIRST, k - 1, x[:, k - 1, :])
            act.dma_start(tab[:, :], tab1).then_inc(decay_in, 16)
            act.sem_inc(counts_of(1).silu.sem, 2)

            c, b = counts_of(0), b1
            x_tiles = [x[:, t, :] for t in range(KT)]
            h_tiles = [hh[:, t, :] for t in range(KT)]
            with act.Fori(0, LAYERS) as l:
                act.preload_act_table_set(LN_SET)
                rms(c, l, 1, A_FIRST, KT, bank[0][:, :], D)
                hi(c, b, l, 0)
                highs(c, l, 0, h_tiles)
                for n in range(1, LOOK):
                    hi(c, b, l, n)
                act.wait_ge(c.prm_in.sem, c.prm_in.at(l, 8))
                for s in b["steps"]:
                    if s[0] == "g":
                        group(c, b, l, b["groups"][s[1]])
                    elif s[0] == "i":
                        item(c, l, s[1], 0, n1, True)
                    elif s[0] == "r_out":
                        for h in (2 * s[1], 2 * s[1] + 1):
                            r = half(h % 2)
                            act.wait_ge(c.r_pv.sem, c.r_pv.at(l, 4 * h + 4))
                            act.activation(g(A_RQ + S * s[1], S, r), bank[O_B[1 - h % 2]][r[0]:r[1], :], ACT.Copy).then_inc(c.r_o.sem, 1)
                    elif s[0] == "conv_out":
                        for t in range(2):
                            act.wait_ge(c.cv_out.sem, c.cv_out.at(l, t + 1))
                            act.activation(g(MIX + S * (3 + t)), g(A_SG + S * t), ACT.Silu, scale=prm[:, P1_LG + t:P1_LG + t + 1],
                                           bias=prm[:, P1_LB + t:P1_LB + t + 1]).then_inc(c.act_step.next(), 1)
                        act.preload_act_table_set(LN_SET)
                    elif s[0] == "mix":
                        k = s[1]
                        if k < 3:
                            act.wait_ge(c.o_done.sem, c.o_done.at(l, 2 * k + 2))
                        elif k < 5:
                            act.wait_ge(c.act_step.sem, c.act_step.now(l))
                        else:
                            act.wait_ge(c.ret_out.sem, c.ret_out.at(l, k - 4))
                        act.activation(hh[:, k, :], g(MIX + S * k), ACT.Copy).then_inc(c.mix_hi.sem, 1)

                def after(m):
                    act.wait_ge(c.group_done.sem, c.group_done.at(l, b["last_of"][b["wo"] + m]))
                    post_square(c, l, A1_POST, m, 1)
                out_product(c, b, l, after)
                rms(c, l, 2, A1_POST, 1, bank[0][:, :], D)
                for t in range(KT):
                    act.wait_ge(c.x_ready.sem, c.x_ready.at(l, t + 1))
                    gained_high(c, t, prm[:, P1_MLP:P1_MLP + KT])
                    square(c, l, A1_MLP, t, x[:, t, :])
                rms(c, l, 3, A1_MLP, KT, bank[0][:, :], D)
                n0 = b["wo"] + KT
                with act.Fori(0, T1 // 4) as i:
                    for j in range(4):
                        hi(c, b, l, n0 + j + LOOK, i)
                n0 += T1
                down(c, b, l, n0, 0, T1, c.f_done)
                for t in range(KT):
                    if t < KT - 1:
                        act.wait_ge(c.down.sem, c.down.at(l, t + 1))
                    else:
                        act.wait_ge(c.group_done.sem, c.group_done.at(l, b["last_of"][b["n"] - 1]))
                    post_square(c, l, A1_MPOST, t, 2)
                rms(c, l, 4, A1_MPOST, 1, bank[0][:, :], D)
                x_squares(c, l, A1_NEXT, KT)
            c.act_step.check()

            c, b = counts_of(1), b2

            def mlp(l, n0, f0, h0):
                with act.Fori(0, T2 // 2) as i:
                    act.preload_act_table_set(SILU_SET)
                    for j in range(4):
                        hi(c, b, l, n0 + j + LOOK, i)
                        if j % 2 == 0:
                            t = j // 2
                            act.wait_ge(c.g_norm.sem, c.g_norm.at(l, f0 + t + 1 + i * 2))
                            act.wait_ge(c.f2_done.sem, c.f2_done.at(l, f0 + t - 1 + i * 2))
                            act.activation(rt[t], tmp[t], ACT.Silu).then_inc(c.silu.sem, 1)
                act.preload_act_table_set(LN_SET)
                down(c, b, l, n0 + 2 * T2, f0, T2, c.f2_done)

            with act.Fori(0, LAYERS) as l:
                act.preload_act_table_set(LN_SET)
                hi(c, b, l, 0)
                act.wait_ge(c.prm_in.sem, c.prm_in.at(l, 12))
                for t in range(KT):
                    gained_high(c, t, prm[:, P2_F1:P2_F1 + KT])
                rms(c, l, 1, A_FIRST, KT, bank[0][:, :], D)
                for n in range(1, LOOK):
                    hi(c, b, l, n)
                mlp(l, 0, 0, 0)
                x_squares(c, l, A2_MIX, 0)
                rms(c, l, 2, A2_MIX, KT, bank[0][:, :], D)
                highs(c, l, 0, h_tiles)
                for s in b["steps"]:
                    if s[0] == "g":
                        group(c, b, l, b["groups"][s[1]])
                    elif s[0] == "px":
                        k = s[1]
                        act.wait_ge(c.px.sem, c.px.at(l, k + 1))
                        before = b["groups"][f"c0{k - 2}" if k >= 2 else "mv3"]
                        act.wait_ge(c.group_done.sem, c.group_done.at(l, before["done"]))
                        act.activation(fshi[:, k % 2, :], g(M_POSX), ACT.Copy).then_inc(c.px_hi.sem, 1)
                    elif s[0] == "sq" and s[1] == "cq":
                        for t in range(2):
                            act.wait_ge(c.evac(b["groups"][f"cq{t}"]).sem, c.emptied(l, b["groups"][f"cq{t}"]))
                            square(c, l, A2_Q, t, g(M_V + S * t))
                    elif s[0] == "sq":
                        act.wait_ge(c.evac(b["groups"]["ckv"]).sem, c.emptied(l, b["groups"]["ckv"]))
                        square(c, l, A2_KV, 0, g(M_V + 2 * S))
                    elif s[0] == "rn" and s[1] == "cq":
                        rms(c, l, 3, A2_Q, 2, bank[2][:, :], 256)
                        highs(c, l, 8, [fshi[:, 0, :], fshi[:, 1, :]])
                    elif s[0] == "rn":
                        rms(c, l, 4, A2_KV, 1, bank[2][:, :], 128)
                        highs(c, l, 10, [fshi[:, 2, :]])
                    elif s[0] == "i":
                        item(c, l, s[1], 0, n2, False)
                    elif s[0] == "z_act":
                        h, jt = s[1:]
                        zi, n = 4 * h + 3 - jt, S - P * jt
                        t_ = g(B_T[zi % 2], n)
                        act.wait_ge(c.z.sem, c.z.at(l, zi + 1))
                        act.activation(t_, bank[0][:, 0:n], ACT.Abs).then_inc(c.act_step.next(), 1)
                        act.wait_ge(c.act_step.sem, c.act_step.now(l))
                        act.activation(t_, t_, ACT.Exp, scale=-1.0).then_inc(c.act_step.next(), 1)
                        act.wait_ge(c.act_step.sem, c.act_step.now(l))
                        act.activation(t_, t_, ACT.Ln, bias=1.0).then_inc(c.z_ln.sem, 1)
                    elif s[0] == "suf_exp":
                        h, jt = s[1:]
                        zi, n, at = 4 * h + 3 - jt, S - P * jt, B_LB[h % 2] + SB_AT[jt]
                        act.wait_ge(c.suf_t.sem, c.suf_t.at(l, zi + 1))
                        act.activation(g(at, n), g(at, n), ACT.Exp).then_inc(c.suf_a.sem, 1)
                    elif s[0] == "mix":
                        k = s[1]
                        if k < 6:
                            act.wait_ge(c.o_done.sem, c.o_done.at(l, 2 * k + 2))
                        else:
                            act.wait_ge(c.sb_out.sem, c.sb_out.at(l, 2 * k - 10))
                        act.activation(hh[:, k, :], g(MIX + S * k), ACT.Copy).then_inc(c.mix_hi.sem, 1)
                    elif s[0] == "sb_out":
                        h, r = s[1], half(s[1] % 2)
                        act.wait_ge(c.sb_pv.sem, c.sb_pv.at(l, h + 1))
                        act.activation(g(MIX + S * (6 + h // 2), S, r), bank[O_B[1 - h % 2]][r[0]:r[1], :], ACT.Copy).then_inc(c.sb_out.sem, 1)

                def after(m):
                    act.wait_ge(c.x_ready.sem, c.x_ready.at(l, KT + m + 1))
                    square_added(c, l, A2_MLP, m, x_tiles[m])
                out_product(c, b, l, after)
                act.wait_ge(c.group_done.sem, c.group_done.at(l, b["last_of"][b["wo"] + KT - 1]))
                for t in range(KT):
                    gained_high(c, t, prm[:, P2_F2:P2_F2 + KT])
                rms(c, l, 5, A2_MLP, 1, bank[0][:, :], D)
                mlp(l, b["wo"] + KT, T2, 0)
                x_squares(c, l, A2_NEXT, 2 * KT)
            c.act_step.check()

            rms(c, LAYERS, 1, A_FIRST, KT, bank[0][:, :], D)
            for n in range(2 * QT):
                act.wait_ge(tout, n + 1)
                if n == 0:
                    act.wait_ge(fin, KT)
                act.activation(g(OUT_AT + S * n), bank[2 + n % 4][:, :], ACT.Copy).then_inc(fin_ev, 1)

        @block.vector
        def _(dve):
            def lo(c, b, l, n, i=None):
                s, m = n % RING, b["size"][n]
                dve.wait_ge(c.hi_done.sem, c.hi_done.at(l, n + 1 + (0 if i is None else i * 4)))
                dve.tensor_tensor(slot3(wlo, s, m), slot3(raw, s, m), slot3(whi, s, m).bitcast(F32), ALU.subtract).then_inc(c.lo_done.sem, 1)

            def norm(c, l, r, b0, src, gains, hi_tiles, lo_tiles):
                dve.wait_ge(c.rn_rstd.sem, c.rn_rstd.at(l, r))
                if b0:
                    dve.wait_ge(c.rn_lo.sem, c.rn_lo.at(l, b0))
                n = len(src)
                for t in range(n + 1):
                    if t < n:
                        if t >= 2:
                            dve.wait_ge(c.rn_lo.sem, c.rn_lo.at(l, b0 + t - 1))
                        dve.scalar_tensor_tensor(out=tmp[t % 2], in0=src[t], scalar=gains[:, t:t + 1], in1=rstd, op0=ALU.mult,
                                                 op1=ALU.mult).then_inc(c.rn_tmp.sem, 1)
                    if t >= 1:
                        dve.wait_ge(c.rn_hi.sem, c.rn_hi.at(l, b0 + t))
                        dve.tensor_tensor(lo_tiles[t - 1], tmp[(t - 1) % 2], hi_tiles[t - 1].bitcast(F32), ALU.subtract).then_inc(c.rn_lo.sem, 1)

            def add_squares(c, l, at, t):
                dve.wait_ge(c.rn_sq.sem, c.rn_sq.at(l, at[0] + t + 1))
                if t >= 2:
                    dve.wait_ge(c.rn_acc.sem, c.rn_acc.at(l, at[2] + t - 1))
                dve.tensor_tensor(sq[0], sq[0], sq_slot(t), ALU.add).then_inc(c.rn_acc.sem, 1)

            def gained_low(c, l, b0, t, gains):
                dve.wait_ge(c.rn_hi.sem, c.rn_hi.at(l, b0 + t + 1))
                dve.scalar_tensor_tensor(out=hl[:, t, :], in0=x[:, t, :], scalar=gains[:, t:t + 1], in1=hh[:, t, :].bitcast(F32),
                                         op0=ALU.mult, op1=ALU.subtract).then_inc(c.rn_lo.sem, 1)

            def post_norm(c, l, r, x0, gains, behind=None):
                def add(t, ahead):
                    dve.wait_ge(c.dve_step.sem, c.dve_step.at(l, c.dve_step.k - ahead))
                    dve.tensor_tensor(x[:, t, :], x[:, t, :], tmp[t % 2], ALU.add).then_inc(c.x_ready.sem, 1)
                dve.wait_ge(c.rn_rstd.sem, c.rn_rstd.at(l, r))
                for t in range(KT):
                    y = g(F_AT) if t == 0 else bank[t][:, :]
                    if t >= 2:
                        dve.wait_ge(c.x_ready.sem, c.x_ready.at(l, x0 + t - 1))
                    dve.scalar_tensor_tensor(out=tmp[t % 2], in0=y, scalar=gains[:, t:t + 1], in1=rstd, op0=ALU.mult, op1=ALU.mult).then_inc(c.dve_step.next(), 1)
                    if t:
                        add(t - 1, 1)
                    if behind and t > 1:
                        behind(t - 2)
                add(KT - 1, 0)
                if behind:
                    behind(KT - 2)
                    behind(KT - 1)

            def item(c, l, j, lo_, n, block1):
                its = items[0 if block1 else 1]
                if lo_ <= j < n:
                    it, m, st = its[j], its[j]["n"], stat[:, j % 4, :]
                    bk = bank[S_B[j % 2]]
                    dve.wait_ge(c.qk.sem, c.qk.at(l, j + 1))
                    if block1:
                        if it["i"] == 0:
                            dve.wait_ge(c.h_in[it["h"] % 2].sem, c.h_in[it["h"] % 2].at(l, it["h"] // 2 + 1))
                        if j >= 2:
                            dve.wait_ge(c.exped.sem, c.exped.at(l, j - 1))
                        s_ = g(A_SB + S * (j % 2), m)
                        h_ = A_H + S * (it["h"] % 2)
                        table = G[:, h_ + m - 1:(h_ - 1 if h_ else None):-1]
                        dve.tensor_tensor(s_, bk[:, 0:m], table, ALU.add).then_inc(c.biased.sem, 1)
                        dve.wait_ge(c.biased.sem, c.biased.at(l, j + 1))
                        dve.tensor_reduce(st[:, 0:1], s_, AXX, ALU.max, negate=True).then_inc(c.maxed.sem, 1)
                    else:
                        dve.tensor_reduce(st[:, 0:1], bk[:, 0:m], AXX, ALU.max, negate=True).then_inc(c.maxed.sem, 1)
                if lo_ <= j - 1 < n:
                    k = j - 1
                    it, st, p_ = its[k], stat[:, k % 4, :], g(A_P + S * (k % 2), its[k]["n"])
                    dve.wait_ge(c.exped.sem, c.exped.at(l, k + 1))
                    dve.reciprocal(st[:, 2:3], st[:, 1:2]).then_inc(c.dve_step.next(), 1)
                    dve.wait_ge(c.dve_step.sem, c.dve_step.now(l))
                    if it["branch"] in ("cmp", "sel", "win"):
                        gate = ("cmp", "sel", "win").index(it["branch"]) + 3 * it["h"] + 18 * it["i"]
                        if k == 24:
                            dve.wait_ge(c.gate.sem, c.gate.at(l, 1))
                        if it["branch"] == "cmp":
                            dve.tensor_tensor(st[:, 2:3], st[:, 2:3], cs(C_VALID + it["i"], n=1), ALU.mult).then_inc(c.dve_step.next(), 1)
                            dve.wait_ge(c.dve_step.sem, c.dve_step.now(l))
                        dve.tensor_scalar(p_, p_, st[:, 2:3], g(M_GATE + gate, 1), ALU.mult, ALU.mult).then_inc(c.scaled.sem, 1)
                    else:
                        dve.tensor_scalar(p_, p_, st[:, 2:3], None, ALU.mult).then_inc(c.scaled.sem, 1)

            def taps(c, l, a, z):
                for k in range(a, z):
                    for t in range(2):
                        y_, acc, wk = g(A_Y + YW * t + k), g(A_SG + S * t), prm[:, P1_CW + TAPS * t + k:P1_CW + TAPS * t + k + 1]
                        if k == 0:
                            if t == 0:
                                dve.wait_ge(c.dve_step.sem, c.dve_step.now(l))
                                for u in range(2):
                                    dve.wait_ge(c.evac(b1["groups"][f"ca{u}"]).sem, c.emptied(l, b1["groups"][f"ca{u}"]))
                            dve.tensor_scalar(acc, y_, wk, prm[:, P1_CB + t:P1_CB + t + 1], ALU.mult, ALU.add).then_inc(c.dve_step.next(), 1)
                            continue
                        dve.wait_ge(c.dve_step.sem, c.dve_step.at(l, tap_at[t]))
                        ins = dve.scalar_tensor_tensor(out=acc, in0=y_, scalar=wk, in1=acc, op0=ALU.mult, op1=ALU.add)
                        if k == TAPS - 1 and t == 1:
                            ins.then_inc(c.taps.sem, 1)
                        else:
                            ins.then_inc(c.dve_step.next(), 1)
                            tap_at[t] = c.dve_step.k
                    if k == 0:
                        tap_at[0], tap_at[1] = c.dve_step.k - 1, c.dve_step.k
            tap_at = [0, 0]

            def swap(c, l, gr, bk, evac):
                if gr["name"] == "sq0":
                    dve.wait_ge(decay_in, 16)
                r = gr["rows"]
                tile, t0 = g(gr["tile"], S, r), gr["tab"]
                swapped = bk[r[0]:r[1], :]
                dve.tensor_tensor(swapped, swapped, tab[r[0]:r[1], (t0 + S):(t0 + 2 * S)], ALU.mult).then_inc(c.dve_step.next(), 1)
                dve.tensor_tensor(tile, tile, tab[r[0]:r[1], t0:t0 + S], ALU.mult).then_inc(c.dve_step.next(), 1)
                dve.wait_ge(c.dve_step.sem, c.dve_step.now(l))
                dve.tensor_tensor(tile, swapped, tile, ALU.add).then_inc(evac, 1)

            def blocks(c, b, l, k):
                kv, u = k // 2, k % 2
                if k == 0:
                    dve.wait_ge(c.prm_in.sem, c.prm_in.at(l, 12))
                    dve.memset(g(M_POSX), 0.0).then_inc(c.dve_step.next(), 1)
                    dve.wait_ge(c.dve_step.sem, c.dve_step.now(l))
                dve.wait_ge(c.evac(b["groups"]["nvc" if kv else "snkc"]).sem, c.emptied(l, b["groups"]["nvc" if kv else "snkc"]))
                if k:
                    dve.wait_ge(c.px_lo.sem, c.px_lo.at(l, k))
                src, pos = (N_VC, P2_PV) if kv else (N_KC, P2_PK)
                for odd in range(2):
                    for j in range(2):
                        r = half(j)
                        dst = g(M_POSX, S, half(odd)).rearrange("p (t n) -> p t n", t=8)[:, :, 32 * j:32 * j + CMP_N]
                        tok = G[r[0]:r[1], src + 16 * u:src + 16 * u + 16 * CMP_N].rearrange("p (n t) -> p t n", t=16)[:, odd::2, :]
                        pe_ = prm[r[0]:r[1], pos + 16 * u + odd:pos + 16 * u + 16:2].unsqueeze(2).to_broadcast([HD, 8, CMP_N])
                        if (odd, j) == (1, 1):
                            dve.wait_ge(c.dve_step.sem, c.dve_step.now(l))
                            dve.tensor_tensor(dst, tok, pe_, ALU.add).then_inc(c.px.sem, 1)
                        else:
                            dve.tensor_tensor(dst, tok, pe_, ALU.add).then_inc(c.dve_step.next(), 1)
                dve.wait_ge(c.px_hi.sem, c.px_hi.at(l, k + 1))
                dve.tensor_tensor(fslo[:, k % 2, :], g(M_POSX), fshi[:, k % 2, :].bitcast(F32), ALU.subtract).then_inc(c.px_lo.sem, 1)

            def group(c, b, l, gr):
                if gr.get("starts") and gr["unit"] + LOOK < b["n"]:
                    lo(c, b, l, gr["unit"] + LOOK)
                kind, bk = gr["kind"], bank[gr["bank"]]
                evac = c.evac(gr).sem
                if kind == "ukv_k":
                    if gr["name"] == "mk0":
                        dve.wait_ge(c.evac(b["groups"]["spe"]).sem, c.emptied(l, b["groups"]["spe"]))
                    dve.tensor_copy(g(M_K + S * gr["j"], S, (64, 96)), g(M_PE, S, (64, 96))).then_inc(c.kpe.sem, 1)
                if kind == "cvar":
                    dve.wait_ge(c.ln_rstd.sem, c.ln_rstd.at(l, gr["nth"]))
                    for t in range(2):
                        dve.tensor_tensor(g(A_SG + S * t), g(A_SG + S * t), g(A_Y), ALU.mult).then_inc(c.cv_out.sem, 1)
                if kind == "rvar":
                    t = gr["t"]
                    dve.wait_ge(c.ln_rstd.sem, c.ln_rstd.at(l, gr["nth"]))
                    dve.tensor_tensor(g(A_RQ + S * t), g(A_RQ + S * t), g(A_RK + S * t), ALU.mult).then_inc(c.dve_step.next(), 1)
                    dve.wait_ge(c.dve_step.sem, c.dve_step.now(l))
                    dve.wait_ge(c.evac(b["groups"][f"rg{t}"]).sem, c.emptied(l, b["groups"][f"rg{t}"]))
                    dve.tensor_tensor(g(MIX + S * (5 + t)), g(MIX + S * (5 + t)), g(A_RQ + S * t), ALU.mult).then_inc(c.ret_out.sem, 1)
                if gr["frees"] != "dve" or not gr.get("evac", True):
                    return
                dve.wait_ge(c.group_done.sem, c.group_done.at(l, gr["done"]))
                if kind == "swap":
                    swap(c, l, gr, bk, evac)
                elif gr["name"] == "gates":
                    for t in range(QT):
                        ins = dve.tensor_tensor(g(M_GATE + 18 * t, 18), bk[:, P * t:P * t + 18], prm[:, P2_GB:P2_GB + 18], ALU.add)
                        if t < QT - 1:
                            ins.then_inc(c.dve_step.next(), 1)
                    ins.then_inc(evac, 1)
                elif kind == "rs":
                    j = gr["j"]
                    h, n = j // 4, S - P * (j % 4)
                    if j == 0:
                        dve.wait_ge(c.qk.sem, c.qk.at(l, 8))
                    if j >= 2:
                        dve.wait_ge(c.r_pv.sem, c.r_pv.at(l, j - 1))
                    dve.tensor_tensor(g(A_D[j % 2], n), bk[:, 0:n], tab[:, S * h:S * h + n], ALU.mult).then_inc(evac, 1)
                elif kind == "cmean":
                    for t in range(2):
                        ins = dve.scalar_tensor_tensor(out=g(A_SG + S * t), in0=bk[:, :], scalar=-1.0 / CONV, in1=g(A_SG + S * t), op0=ALU.mult, op1=ALU.add)
                        if t == 0:
                            ins.then_inc(c.dve_step.next(), 1)
                    ins.then_inc(evac, 1)
                elif kind == "rmean":
                    tile = g(A_RQ + S * gr["t"])
                    dve.tensor_tensor(tile, tile, bk[:, :], ALU.subtract).then_inc(evac, 1)
                elif "glu" in gr:
                    t = gr["glu"]
                    dve.wait_ge(c.evac(b["groups"][f"cg{t}"]).sem, c.emptied(l, b["groups"][f"cg{t}"]))
                    dve.memset(g(A_Y + YW * t, TAPS - 1), 0.0).then_inc(c.dve_step.next(), 1)
                    dve.tensor_tensor(g(A_Y + YW * t + TAPS - 1), bk[:, :], g(A_SG + S * t), ALU.mult).then_inc(evac, 1)
                elif kind == "turn":
                    dve.tensor_copy(tokens(gr), bk[:, :].rearrange("p (t n) -> p t n", t=QT)).then_inc(evac, 1)
                elif kind == "ukv_v":
                    dve.tensor_copy(g(gr["dst"], 384), bk[:, 0:384]).then_inc(evac, 1)
                else:
                    r = gr.get("rows", (0, P))
                    dve.tensor_copy(g(gr["dst"], S, r), bk[r[0]:r[1], :]).then_inc(evac, 1)

            def tokens(gr):
                return g(gr["dst"], QT * gr["pitch"]).rearrange("p (t n) -> p t n", t=QT)[:, :, gr["off"]:gr["off"] + P]

            def down(c, b, l, n0, h0, nt):
                def f_lo(t, more, i):
                    if t >= nt and i is None:
                        return
                    dve.wait_ge(c.f_hi.sem, c.f_hi.at(l, h0 + t + 1 + more))
                    dve.tensor_tensor(fslo[:, t % 2, :], f_tile(t + more), fshi[:, t % 2, :].bitcast(F32), ALU.subtract).then_inc(c.f_lo.sem, 1)

                def one(t, i=None):
                    f_lo(t + 1, 0 if i is None else i * 4, i)
                    if n0 + t + LOOK < b["n"]:
                        lo(c, b, l, n0 + t + LOOK, i)
                f_lo(0, 0, None)
                for j in range(4):
                    one(j)
                whole = nt // 4 * 4 if nt % 4 else nt - 4
                with dve.Fori(1, whole // 4) as i:
                    for j in range(4):
                        one(j, i)
                for j in range(whole, nt):
                    one(j)

            dve.memset(eps[:, :], EPS).then_inc(bias_sem, 1)
            rows, ext = LAYERS * HEADS1, 4608
            dve.memset(G[0:rows, ext:ext + BIAS_ROW], 0.0).then_inc(rows_zero, 1)
            dve.wait_ge(rows_zero, 1)
            dve.wait_ge(rows_in, 16)
            dve.tensor_copy(G[0:rows, ext:ext + 256], G[0:rows, 4097:4097 + 256]).then_inc(bias_sem, 1)
            dve.tensor_scalar(G[0:rows, ext + 256:ext + BIAS_ROW], G[0:rows, ext + 256:ext + BIAS_ROW], G[0:rows, 4096 + 256:4096 + 257], None,
                              ALU.add).then_inc(bias_sem, 1)
            dve.wait_ge(const_in, 32)
            dve.tensor_copy(m_sb[:, :], g(MASK_AT)).then_inc(masks_ready, 1)
            dve.sem_inc(counts_of(0).lo_done.sem, RING)
            dve.sem_inc(counts_of(0).up_norm.sem, 4)
            dve.sem_inc(counts_of(1).g_norm.sem, 2)
            dve.sem_inc(counts_of(1).u_norm.sem, 2)
            dve.sem_inc(counts_of(0).rn_lo.sem, 1)
            dve.sem_inc(counts_of(1).f2_done.sem, 2)

            x_tiles = [x[:, t, :] for t in range(KT)]
            hi_tiles, lo_tiles = [hh[:, t, :] for t in range(KT)], [hl[:, t, :] for t in range(KT)]
            c, b = counts_of(0), b1
            with dve.Fori(0, LAYERS) as l:
                lo(c, b, l, 0)
                dve.wait_ge(c.prm_in.sem, c.prm_in.at(l, 8))
                norm(c, l, 1, 0, x_tiles, prm[:, P1_MIX:P1_MIX + KT], hi_tiles, lo_tiles)
                for n in range(1, LOOK):
                    lo(c, b, l, n)
                for s in b["steps"]:
                    if s[0] == "g":
                        group(c, b, l, b["groups"][s[1]])
                    elif s[0] == "i":
                        item(c, l, s[1], 0, n1, True)
                    elif s[0] == "taps":
                        taps(c, l, s[1], s[2])
                    elif s[0] == "mix":
                        k = s[1]
                        dve.wait_ge(c.mix_hi.sem, c.mix_hi.at(l, k + 1))
                        dve.tensor_tensor(lo_tiles[k], g(MIX + S * k), hi_tiles[k].bitcast(F32), ALU.subtract).then_inc(c.mix_lo.sem, 1)
                for m in range(KT):
                    lo(c, b, l, b["wo"] + m + LOOK)
                    if m >= 2:
                        add_squares(c, l, A1_POST, m - 1)
                add_squares(c, l, A1_POST, KT - 1)
                post_norm(c, l, 2, 0, prm[:, P1_POST:P1_POST + KT], lambda t: gained_low(c, l, 8, t, prm[:, P1_MLP:P1_MLP + KT]))
                n0 = b["wo"] + KT
                with dve.Fori(0, T1 // 4) as i:
                    for j in range(4):
                        lo(c, b, l, n0 + j + LOOK, i)
                        dve.wait_ge(c.group_done.sem, c.group_done.at(l, b["last_of"][n0] + j + i * 4))
                        if j == 0:
                            dve.wait_ge(c.rn_rstd.sem, c.rn_rstd.at(l, 3))
                        dve.tensor_tensor(tmp[j % 2], bank[1 + j][:, :], rstd, ALU.mult).then_inc(c.up_norm.sem, 1)
                        dve.wait_ge(c.up_norm.sem, c.up_norm.at(l, j + 1 + i * 4))
                        dve.scalar_tensor_tensor(out=f_tile(i * 4 + j), in0=tmp[j % 2], scalar=0.0, in1=tmp[j % 2], op0=ALU.max,
                                                 op1=ALU.mult).then_inc(c.f_done.sem, 1)
                down(c, b, l, n0 + T1, 0, T1)
                for t in range(1, KT):
                    add_squares(c, l, A1_MPOST, t)
                dve.wait_ge(c.mpost_in.sem, c.mpost_in.at(l, 1))
                post_norm(c, l, 4, KT, prm[:, P1_MPOST:P1_MPOST + KT])
            c.dve_step.check()

            c, b = counts_of(1), b2

            def mlp(l, n0, f0, d0, r):
                with dve.Fori(0, T2 // 2) as i:
                    for j in range(4):
                        lo(c, b, l, n0 + j + LOOK, i)
                        t = j // 2
                        dve.wait_ge(c.group_done.sem, c.group_done.at(l, b["last_of"][n0] + j + i * 4))
                        if j % 2 == 0:
                            if j == 0:
                                dve.wait_ge(c.rn_rstd.sem, c.rn_rstd.at(l, r))
                            dve.wait_ge(c.silu.sem, c.silu.at(l, f0 + t - 1 + i * 2))
                            dve.tensor_tensor(tmp[t], bank[4 + j][:, :], rstd, ALU.mult).then_inc(c.g_norm.sem, 1)
                        else:
                            f = f_tile(i * 2 + t)
                            dve.tensor_tensor(f, bank[4 + j][:, :], rstd, ALU.mult).then_inc(c.u_norm.sem, 1)
                            dve.wait_ge(c.u_norm.sem, c.u_norm.at(l, f0 + t + 1 + i * 2))
                            dve.wait_ge(c.silu.sem, c.silu.at(l, f0 + t + 1 + i * 2))
                            dve.tensor_tensor(f, f, rt[t], ALU.mult).then_inc(c.f2_done.sem, 1)
                down(c, b, l, n0 + 2 * T2, f0, T2)
                for t in range(KT):
                    if t < KT - 1:
                        dve.wait_ge(c.down.sem, c.down.at(l, d0 + t + 1))
                    else:
                        dve.wait_ge(c.group_done.sem, c.group_done.at(l, b["last_of"][n0 + 3 * T2 - 1]))
                    dve.scalar_tensor_tensor(out=x[:, t, :], in0=bank[t][:, :], scalar=0.5, in1=x[:, t, :], op0=ALU.mult, op1=ALU.add).then_inc(c.x_ready.sem, 1)

            dve.wait_ge(tab_in, 16)
            with dve.Fori(0, LAYERS) as l:
                lo(c, b, l, 0)
                dve.wait_ge(c.prm_in.sem, c.prm_in.at(l, 12))
                for t in range(KT):
                    gained_low(c, l, 0, t, prm[:, P2_F1:P2_F1 + KT])
                for n in range(1, LOOK):
                    lo(c, b, l, n)
                mlp(l, 0, 0, 0, 1)
                norm(c, l, 2, 8, x_tiles, prm[:, P2_MIX:P2_MIX + KT], hi_tiles, lo_tiles)
                for s in b["steps"]:
                    if s[0] == "g":
                        group(c, b, l, b["groups"][s[1]])
                    elif s[0] == "px":
                        blocks(c, b, l, s[1])
                    elif s[0] == "rn" and s[1] == "cq":
                        norm(c, l, 3, 16, [g(M_V), g(M_V + S)], prm[:, P2_QN:P2_QN + 2], [fshi[:, 0, :], fshi[:, 1, :]], [fslo[:, 0, :], fslo[:, 1, :]])
                    elif s[0] == "rn":
                        norm(c, l, 4, 18, [g(M_V + 2 * S)], prm[:, P2_KVN:P2_KVN + 1], [fshi[:, 2, :]], [fslo[:, 2, :]])
                    elif s[0] == "i":
                        item(c, l, s[1], 0, n2, False)
                    elif s[0] == "z_dve":
                        h, jt = s[1:]
                        zi, n, at = 4 * h + 3 - jt, S - P * jt, SB_AT[jt]
                        bk, lb, lr, t_ = bank[0][:, 0:n], g(B_LB[h % 2] + at, n), g(B_LR[h % 2] + at, n), g(B_T[zi % 2], n)
                        if jt == 3 and h >= 2:
                            dve.wait_ge(c.sb_pv.sem, c.sb_pv.at(l, h - 1))
                        dve.wait_ge(c.z_ln.sem, c.z_ln.at(l, zi + 1))
                        dve.tensor_scalar(lb, bk, 0.0, None, ALU.min).then_inc(c.dve_step.next(), 1)
                        dve.tensor_scalar(lr, bk, -1.0, 0.0, ALU.mult, ALU.min).then_inc(c.dve_step.next(), 1)
                        dve.wait_ge(c.dve_step.sem, c.dve_step.now(l))
                        dve.tensor_tensor(lb, lb, t_, ALU.subtract).then_inc(c.dve_step.next(), 1)
                        dve.tensor_tensor(lr, lr, t_, ALU.subtract).then_inc(c.dve_step.next(), 1)
                        dve.wait_ge(c.dve_step.sem, c.dve_step.now(l))
                        dve.tensor_tensor(lr[:, 0:P], lr[:, 0:P], strict, ALU.mult).then_inc(c.z_lr.sem, 1)
                    elif s[0] == "suf_add":
                        h, jt = s[1:]
                        zi, n = 4 * h + 3 - jt, S - P * jt
                        lb = g(B_LB[h % 2] + SB_AT[jt], n)
                        dve.wait_ge(c.suf.sem, c.suf.at(l, zi + 1))
                        dve.tensor_tensor(lb, lb, bank[1][:, 0:n], ALU.add).then_inc(c.suf_t.sem, 1)
                    elif s[0] == "suf_mask":
                        h, jt = s[1:]
                        d = g(B_LB[h % 2] + SB_AT[jt], P)
                        dve.wait_ge(c.suf_a.sem, c.suf_a.at(l, 4 * h + 4 - jt))
                        dve.tensor_tensor(d, d, strict, ALU.mult).then_inc(c.suf_m.sem, 1)
                    elif s[0] == "mix":
                        k = s[1]
                        dve.wait_ge(c.mix_hi.sem, c.mix_hi.at(l, k + 1))
                        dve.tensor_tensor(lo_tiles[k], g(MIX + S * k), hi_tiles[k].bitcast(F32), ALU.subtract).then_inc(c.mix_lo.sem, 1)

                def update(t):
                    dve.wait_ge(c.group_done.sem, c.group_done.at(l, b["last_of"][b["wo"] + t]))
                    dve.tensor_tensor(x[:, t, :], bank[t][:, :], x[:, t, :], ALU.add).then_inc(c.x_ready.sem, 1)
                for m in range(KT):
                    lo(c, b, l, b["wo"] + m + LOOK)
                    if m:
                        update(m - 1)
                    if m >= 3:
                        add_squares(c, l, A2_MLP, m - 2)
                update(KT - 1)
                add_squares(c, l, A2_MLP, KT - 2)
                add_squares(c, l, A2_MLP, KT - 1)
                for t in range(KT):
                    gained_low(c, l, 19, t, prm[:, P2_F2:P2_F2 + KT])
                mlp(l, b["wo"] + KT, T2, KT - 1, 5)
            c.dve_step.check()
            dve.wait_ge(c.rn_rstd.sem, c.rn_rstd.at(2, 1))
            dve.wait_ge(gain_in, 16)
            for t in range(KT):
                dve.scalar_tensor_tensor(out=x_tiles[t], in0=x_tiles[t], scalar=fin_g[:, t:t + 1], in1=rstd, op0=ALU.mult, op1=ALU.mult).then_inc(fin, 1)

        @block.tensor
        def _(pe):
            def mm3(o, wh, wl, ah, al, start, stop):
                pe.matmul(o, wh, ah, start=start, stop=False)
                pe.matmul(o, wh, al, start=False, stop=False)
                return pe.matmul(o, wl, ah, start=False, stop=stop)

            def cols(t, s, k, j=0, n=P, pitch=P):
                return t[:, s, k * pitch + j:k * pitch + j + n]

            def norm_tile(c, l, a, n, bk, t):
                pe.wait_ge(c.rn_sq.sem, c.rn_sq.at(l, a[0] + t + 1))
                pe.matmul(bk, ones, sq[t % 2], start=t == 0, stop=t == n - 1).then_inc(c.rn_used.sem, 1)

            def norm_added(c, l, a):
                pe.wait_ge(c.rn_acc.sem, c.rn_acc.at(l, a[2] + KT - 1))
                pe.matmul(bank[0][:, :], ones, sq[0], start=True, stop=True).then_inc(c.rn_used.sem, 1)

            def norm(c, l, a, n, bk):
                for t in range(n):
                    norm_tile(c, l, a, n, bk, t)

            def need(c, b, l, *names):
                for bk in range(2):
                    late = [b["groups"][n] for n in names if b["groups"][n]["bank"] == bk]
                    if late:
                        pe.wait_ge(c.evac(max(late, key=lambda gr: gr["e"])).sem, c.emptied(l, max(late, key=lambda gr: gr["e"])))

            def item(c, b, l, j, lo_, n, block1):
                its = items[0 if block1 else 1]
                if lo_ <= j < n:
                    it = its[j]
                    h, i, m, br = it["h"], it["i"], it["n"], it["branch"]
                    bk, q = bank[S_B[j % 2]], P * i
                    if br is None:
                        if i == 0:
                            need(c, b, l, f"q{h // 2}", f"k{h // 2}", f"v{h // 2}")
                        r = half(h % 2)
                        lhs, rhs = g(A_Q + S * (h // 2) + q, P, r), g(A_K + S * (h // 2), m, r)
                    elif br == "mla":
                        if j == 0:
                            need(c, b, l, "sm4", "sm5", "mk4", "mk5", "mv2", "mv3")
                        if i == 0:
                            pe.wait_ge(c.kpe.sem, c.kpe.at(l, h + 1))
                        r = (0, MLA_D)
                        lhs, rhs = g(M_Q + S * h + q, P, r), g(M_K + S * h, m, r)
                    else:
                        if j == 24:
                            need(c, b, l, *(gr["name"] for gr in b["order"]))
                        r = half(h // 3)
                        lhs = g(N_Q + S * (h % 3) + q, P, r)
                        rhs = g({"sel": N_KS, "win": N_KW, "cmp": M_KC}[br], m, r)
                    if j - lo_ >= 2:
                        free = c.biased if block1 else c.exped
                        pe.wait_ge(free.sem, free.at(l, j - 1))
                    pe.matmul(bk[:, 0:m], lhs, rhs, start=True, stop=False)
                    mask = chunked if block1 else causal
                    if br == "cmp":
                        ins = pe.matmul(bk[:, 0:32], identb, cmpmask[:, 32 * i:32 * i + 32], start=False, stop=True)
                    else:
                        ins = pe.matmul(bk[:, q:q + P], identb, mask, start=False, stop=True)
                    ins.then_inc(c.qk.sem, 1)
                k = j - PV_LAG
                if lo_ <= k < n:
                    it = its[k]
                    h, i, br = it["h"], it["i"], it["branch"]
                    o = bank[O_B[h % 2]][HD * (h % 2):HD * (h % 2) + HD, P * i:P * i + P]
                    pe.wait_ge(c.pt.sem, c.pt.at(l, k + 1))
                    oi = h + (6 if br in ("sel", "win", "cmp") else 0)
                    if i == 0 and it["first"] and oi >= 2:
                        pe.wait_ge(c.o_done.sem, c.o_done.at(l, oi - 1))
                    n_k = 1 if br == "cmp" else i + 1
                    for kt in range(n_k):
                        if br == "cmp":
                            v, pt = g(M_VC + HD * (h // 3), HD, (0, 32)), g(A_PT + S * (k % 2), P, (0, 32))
                        else:
                            pt = g(A_PT + S * (k % 2) + P * kt, P)
                            v = {None: lambda: g(A_V + 384 * kt + HD * h, HD), "mla": lambda: g(M_V + 384 * kt + HD * h, HD),
                                 "sel": lambda: g(N_VS + P * kt + HD * (h // 3), HD), "win": lambda: g(N_VW + P * kt + HD * (h // 3), HD)}[br]()
                        ins = pe.matmul(o, v, pt, start=it["first"] and kt == 0, stop=it["last"] and kt == n_k - 1)
                    ins.then_inc(c.pv.sem, 1)
                k = j - TURN_LAG
                if lo_ <= k < n:
                    it = its[k]
                    pe.wait_ge(c.scaled.sem, c.scaled.at(l, k + 1))
                    if k - lo_ >= 2:
                        pe.wait_ge(c.pt.sem, c.pt.at(l, k - 1))
                    bk = bank[T_B[k % 2]]
                    if it["n"] == 32:
                        ins = pe.transpose(bk[0:32, 0:P], g(A_P + S * (k % 2), 32), ident)
                    else:
                        for kt in range(it["i"] + 1):
                            ins = pe.transpose(bk[:, P * kt:P * kt + P], g(A_P + S * (k % 2) + P * kt, P), ident)
                    ins.then_inc(c.turned.sem, 1)

            def group(c, b, l, gr):
                kind, bk, e = gr["kind"], bank[gr["bank"]], gr["e"]
                unit = gr.get("unit")
                if unit is not None:
                    pe.wait_ge(c.lo_done.sem, c.lo_done.at(l, unit + 1))
                    s = unit % RING
                if e >= 2:
                    pe.wait_ge(c.evacs[gr["bank"]].sem, c.evacs[gr["bank"]].at(l, e // 2))
                if kind == "fm":
                    for k in range(KT):
                        if gr is b["order"][0]:
                            pe.wait_ge(c.rn_lo.sem, c.rn_lo.at(l, (0 if b is b1 else 8) + k + 1))
                        ins = mm3(bk[:, :], cols(whi, s, k), cols(wlo, s, k), hh[:, k, :], hl[:, k, :], k == 0, k == KT - 1)
                elif kind == "turn":
                    need(c, b, l, gr["of"])
                    for t in range(QT):
                        ins = pe.transpose(bk[:, P * t:P * t + P], g(gr["tile"] + P * t, P), ident)
                elif kind == "swap":
                    r = gr["rows"]
                    need(c, b, l, gr["of"])
                    at = {"r": C_PERM_R, "n": C_PERM_N, "m": C_PERM_M}[gr["perm"]]
                    ins = pe.matmul(bk[0:r[1], :], cs(at, r, r[1]), g(gr["tile"], S, r), start=True, stop=True)
                elif kind == "uq":
                    for k in range(2):
                        if gr["name"] == "mq0":
                            pe.wait_ge(c.rn_lo.sem, c.rn_lo.at(l, 17 + k))
                        ins = mm3(bk[0:MLA_D, :], cols(whi, s, k, MLA_D * gr["j"], MLA_D, 288), cols(wlo, s, k, MLA_D * gr["j"], MLA_D, 288),
                                  fshi[:, k, :], fslo[:, k, :], k == 0, k == 1)
                elif kind == "ukv_k":
                    if gr["name"] == "mk0":
                        pe.wait_ge(c.rn_lo.sem, c.rn_lo.at(l, 19))
                    ins = mm3(bk[:, :], cols(whi, s, gr["j"]), cols(wlo, s, gr["j"]), fshi[:, 2, :], fslo[:, 2, :], True, True)
                elif kind == "ukv_v":
                    v = lambda t_: t_[:, s, 0:768].rearrange("p (h n) -> p h n", h=MLA_H)[:, :, HD:]
                    q = P * gr["j"]
                    ins = mm3(bk[:, 0:384].rearrange("p (h n) -> p h n", h=MLA_H), fshi[:, 2, q:q + P], fslo[:, 2, q:q + P], v(whi), v(wlo), True, True)
                elif kind == "cmp":
                    k = 2 * gr["kv"] + gr["u"]
                    pe.wait_ge(c.px_lo.sem, c.px_lo.at(l, k + 1))
                    for t in range(8):
                        ah, al = fshi[:, k % 2, 64 * t:64 * t + 64], fslo[:, k % 2, 64 * t:64 * t + 64]
                        ins = mm3(bk[:, 0:64], cols(whi, s, t), cols(wlo, s, t), ah, al, gr["u"] == 0 and t == 0, gr["u"] == 1 and t == 7)
                elif kind == "w2":
                    need(c, b, l, f"c{gr['kv']}1")
                    for j in range(2):
                        hid = g(M_HID + 64 * gr["kv"] + 32 * j, 32)
                        if gr["kv"] == 0:
                            ins = pe.matmul(bk[HD * j:HD * j + HD, 0:32], prm[:, P2_WK:P2_WK + HD], hid, start=True, stop=True)
                        else:
                            ins = pe.matmul(bk[0:32, HD * j:HD * j + HD], hid, prm[:, P2_WV:P2_WV + HD], start=True, stop=True)
                elif kind == "rs":
                    h, jt = gr["j"] // 4, gr["j"] % 4
                    r, n = half(h % 2), S - P * jt
                    if jt == 0:
                        need(c, b, l, f"sq{h // 2}", f"sk{h // 2}", f"rv{h // 2}")
                    ins = pe.matmul(bk[:, 0:n], g(A_RK + S * (h // 2) + P * jt, P, r), g(A_RQ + S * (h // 2) + P * jt, n, r), start=True, stop=True)
                elif kind == "cmean":
                    pe.wait_ge(c.taps.sem, c.taps.at(l, 1))
                    for t in range(2):
                        ins = pe.matmul(bk[:, :], ones, g(A_SG + S * t), start=t == 0, stop=t == 1)
                elif kind == "cvar":
                    pe.wait_ge(c.ln_sq.sem, c.ln_sq.at(l, gr["squared"]))
                    for t in range(2):
                        ins = pe.matmul(bk[:, :], ones, g(A_Y + S * t), start=t == 0, stop=t == 1)
                elif kind == "rmean":
                    pe.wait_ge(c.r_o.sem, c.r_o.at(l, 2 + 2 * gr["t"]))
                    ins = pe.matmul(bk[:, :], blk, g(A_RQ + S * gr["t"]), start=True, stop=True)
                elif kind == "rvar":
                    pe.wait_ge(c.ln_sq.sem, c.ln_sq.at(l, gr["squared"]))
                    ins = pe.matmul(bk[:, :], blk, g(A_RK + S * gr["t"]), start=True, stop=True)
                ins.then_inc(c.group_done.sem, 1)

            def retention_pv(c, b, l, k):
                h, jt, r = k // 4, k % 4, half(k // 4 % 2)
                gr = b["groups"][f"rs{k}"]
                pe.wait_ge(c.evac(gr).sem, c.emptied(l, gr))
                if jt == 0 and h >= 2:
                    pe.wait_ge(c.r_o.sem, c.r_o.at(l, h - 1))
                n = S - P * jt
                pe.matmul(bank[O_B[1 - h % 2]][r[0]:r[1], P * jt:S], g(A_RV + 384 * jt + HD * h, HD), g(A_D[k % 2], n),
                          start=jt == 0, stop=jt == 3).then_inc(c.r_pv.sem, 1)

            def out_product(c, b, l):
                for m in range(KT):
                    pe.wait_ge(c.lo_done.sem, c.lo_done.at(l, b["wo"] + m + 1))
                    s = (b["wo"] + m) % RING
                    for k in range(KT):
                        if m == 0:
                            pe.wait_ge(c.mix_lo.sem, c.mix_lo.at(l, k + 1))
                            if k == 0 and b is b1:
                                pe.wait_ge(c.evacs[0].sem, c.evacs[0].at(l, b["evacs"][0]))
                            elif k == 0:
                                pe.wait_ge(c.z_lr.sem, c.z_lr.at(l, 4 * SB_H))
                        ins = mm3(bank[m][:, :], cols(whi, s, k), cols(wlo, s, k), hh[:, k, :], hl[:, k, :], k == 0, k == KT - 1)
                    ins.then_inc(c.group_done.sem, 1)

            def up_unit(c, b, l, n, bk, more, rn, sums=False):
                pe.wait_ge(c.lo_done.sem, c.lo_done.at(l, n + 1 + more))
                s = n % RING
                for k in range(KT):
                    if sums:
                        norm_tile(c, l, A1_MLP, KT, bank[0][:, :], k)
                    if rn is not None:
                        pe.wait_ge(c.rn_lo.sem, c.rn_lo.at(l, rn + k + 1))
                    ins = mm3(bk[:, :], cols(whi, s, k), cols(wlo, s, k), hh[:, k, :], hl[:, k, :], k == 0, k == KT - 1)
                ins.then_inc(c.group_done.sem, 1)

            def down(c, b, l, n0, h0, nt, a):
                def one(t, i=None, first=False, last=False):
                    more = 0 if i is None else i * 4
                    pe.wait_ge(c.f_lo.sem, c.f_lo.at(l, h0 + t + 1 + more))
                    pe.wait_ge(c.lo_done.sem, c.lo_done.at(l, n0 + t + 1 + more))
                    s, fs = (n0 + t) % RING, t % 2
                    for m in range(KT):
                        ins = mm3(bank[m][:, :], cols(whi, s, m), cols(wlo, s, m), fshi[:, fs, :], fslo[:, fs, :], first, last)
                        if last and m < KT - 1:
                            ins.then_inc(c.down.sem, 1)
                        elif m == KT - 1:
                            ins.then_inc(c.group_done.sem, 1)
                        if last and m >= 2 and len(a) == 2:
                            norm_tile(c, l, a, KT, bank[0][:, :], m - 2)
                for j in range(4):
                    one(j, first=j == 0)
                whole = nt // 4 * 4 if nt % 4 else nt - 4
                with pe.Fori(1, whole // 4) as i:
                    for j in range(4):
                        one(j, i)
                for j in range(whole, nt):
                    one(j, last=j == nt - 1)
                if len(a) == 2:
                    for t in range(KT - 2, KT):
                        norm_tile(c, l, a, KT, bank[0][:, :], t)
                else:
                    norm_added(c, l, a)

            pe.wait_ge(x_dma, 16)
            pe.wait_ge(ident_in, 16)
            c, b = counts_of(0), b1
            for k in range(KT):
                if k >= 2:
                    pe.wait_ge(c.x_ready.sem, k - 1)
                for t in range(QT):
                    ins = pe.transpose(bank[1 + k % 2][:, P * t:P * t + P], g(X_AT + D * t + P * k, P), ident)
                ins.then_inc(tin, 1)
                if k == 0:
                    pe.wait_ge(const_in, 32)
                    pe.wait_ge(masks_ready, 1)
                if k >= 2:
                    norm_tile(c, 0, A_FIRST, KT, bank[0][:, :], k - 2)
            for k in range(KT - 2, KT):
                norm_tile(c, 0, A_FIRST, KT, bank[0][:, :], k)
            with pe.Fori(0, LAYERS) as l:
                for s in b["steps"]:
                    if s[0] == "g":
                        group(c, b, l, b["groups"][s[1]])
                    elif s[0] == "i":
                        item(c, b, l, s[1], 0, n1, True)
                    elif s[0] == "r_pv":
                        retention_pv(c, b, l, s[1])
                out_product(c, b, l)
                norm_added(c, l, A1_POST)
                n0 = b["wo"] + KT

                def ups(more, first):
                    for j in range(4):
                        pe.wait_ge(c.up_norm.sem, c.up_norm.at(l, j - 3 + more))
                        up_unit(c, b, l, n0 + j, bank[1 + j], more, KT if j == 0 and first else None, first and j == 0)
                ups(0, True)
                with pe.Fori(1, T1 // 4) as i:
                    ups(i * 4, False)
                pe.wait_ge(c.f_done.sem, c.f_done.at(l, T1))
                down(c, b, l, n0 + T1, 0, T1, A1_MPOST)
                norm(c, l, A1_NEXT, KT, bank[0][:, :])

            c, b = counts_of(1), b2

            def mlp(l, n0, f0, a, b0, sums):
                def ups(more, half_more, first):
                    for j in range(4):
                        free = c.u_norm if j % 2 else c.g_norm
                        pe.wait_ge(free.sem, free.at(l, f0 + j // 2 - 1 + half_more))
                        up_unit(c, b, l, n0 + j, bank[4 + j], more, b0 if j == 0 and first else None)
                        if first and j == 0 and sums:
                            norm_added(c, l, sums)
                ups(0, 0, True)
                with pe.Fori(1, T2 // 2) as i:
                    ups(i * 4, i * 2, False)
                pe.wait_ge(c.f2_done.sem, c.f2_done.at(l, f0 + T2))
                down(c, b, l, n0 + 2 * T2, f0, T2, a)

            with pe.Fori(0, LAYERS) as l:
                mlp(l, 0, 0, A2_MIX, 0, None)
                for s in b["steps"]:
                    if s[0] == "g":
                        group(c, b, l, b["groups"][s[1]])
                    elif s[0] == "rn":
                        norm(c, l, *((A2_Q, 2) if s[1] == "cq" else (A2_KV, 1)), bank[2][:, :])
                    elif s[0] == "i":
                        item(c, b, l, s[1], 0, n2, False)
                    elif s[0] == "z":
                        h, jt = s[1:]
                        zi, n, r = 4 * h + 3 - jt, S - P * jt, half(h % 2)
                        if zi:
                            pe.wait_ge(c.z_lr.sem, c.z_lr.at(l, zi))
                        pe.matmul(bank[0][:, 0:n], g(B_K + S * (h // 2) + P * jt, P, r), g(B_Q + S * (h // 2) + P * jt, n, r),
                                  start=True, stop=True).then_inc(c.z.sem, 1)
                    elif s[0] == "suf":
                        h, jt = s[1:]
                        zi, n, lr = 4 * h + 3 - jt, S - P * jt, B_LR[h % 2]
                        pe.wait_ge(c.z_lr.sem, c.z_lr.at(l, zi + 1))
                        if zi:
                            pe.wait_ge(c.suf_t.sem, c.suf_t.at(l, zi))
                        ins = pe.matmul(bank[1][:, 0:n], tri, g(lr + SB_AT[jt], n), start=True, stop=jt == 3)
                        for j2 in range(jt + 1, QT):
                            ins = pe.matmul(bank[1][:, P * (j2 - jt):n], ones, g(lr + SB_AT[j2], S - P * j2), start=False, stop=j2 == 3)
                        ins.then_inc(c.suf.sem, 1)
                    elif s[0] == "sbo":
                        h = s[1]
                        pe.wait_ge(c.suf_m.sem, c.suf_m.at(l, 4 * h + 4))
                        if h >= 2:
                            pe.wait_ge(c.sb_out.sem, c.sb_out.at(l, h - 1))
                        for jt in range(QT):
                            ins = pe.matmul(bank[O_B[1 - h % 2]][HD * (h % 2):HD * (h % 2) + HD, P * jt:S], g(B_V + 256 * jt + HD * h, HD),
                                            g(B_LB[h % 2] + SB_AT[jt], S - P * jt), start=jt == 0, stop=jt == 3)
                        ins.then_inc(c.sb_pv.sem, 1)
                out_product(c, b, l)
                mlp(l, b["wo"] + KT, T2, A2_NEXT, 19, A2_MLP)

            pe.wait_ge(fin, KT)
            for n in range(2 * QT):
                if n >= 4:
                    pe.wait_ge(fin_ev, n - 3)
                for k in range(4):
                    ins = pe.transpose(bank[2 + n % 4][:, P * k:P * k + P], x[:, 4 * (n % 2) + k, P * (n // 2):P * (n // 2) + P], ident)
                ins.then_inc(tout, 1)


INPUTS = ["x", "norm_mix_pre", "norm_mix_post", "norm_mlp_pre", "norm_mlp_post", "w_in", "attn_rel_bias", "conv_w", "conv_b",
          "conv_ln_g", "conv_ln_b", "w_out", "w_up", "w_down", "ffn1_norm_2", "ffn1_w_gate_2", "ffn1_w_up_2", "ffn1_w_down_2",
          "mix_norm_2", "w_in_2", "mla_q_norm_2", "mla_w_uq_2", "mla_kv_norm_2", "mla_w_ukv_2", "nsa_gate_bias_2",
          "nsa_cmp_pos_k_2", "nsa_cmp_w1_k_2", "nsa_cmp_w2_k_2", "nsa_cmp_pos_v_2", "nsa_cmp_w1_v_2", "nsa_cmp_w2_v_2",
          "w_out_2", "ffn2_norm_2", "ffn2_w_gate_2", "ffn2_w_up_2", "ffn2_w_down_2", "final_norm_2"]


def kernel(**inputs):
    import concourse.bacc as bacc
    from concourse.bass_utils import run_bass_kernel_spmd

    nc = bacc.Bacc("TRN2", target_bir_lowering=False, num_devices=1)
    arrays, w = {}, {}
    for name in INPUTS:
        a = np.ascontiguousarray(inputs[name])
        arrays[f"in_{name}"] = a
        w[name] = nc.dram_tensor(f"in_{name}", a.shape, mybir.dt.from_np(a.dtype), kind="ExternalInput").ap()
    consts = []
    for name, a in zip(("c_words", "c_masks", "c_tab1", "c_tab2"), constants()):
        arrays[name] = a
        consts.append(nc.dram_tensor(name, a.shape, mybir.dt.from_np(a.dtype), kind="ExternalInput").ap())
    scratch = nc.dram_tensor("bias_rows", [LAYERS * HEADS1, BIAS_ROW], F32).ap()
    out = nc.dram_tensor("out", [1, S, D], F32, kind="ExternalOutput").ap()
    build(nc, w["x"], *consts, scratch, out, w)
    r = run_bass_kernel_spmd(nc, [arrays], core_ids=[0])
    return r.results[0]["out"]
```
